# Optimizing a Trainium2 kernel written in Bass

```python
import math
import jax, jax.numpy as jnp
from jax import lax
import numpy as np

D_MODEL = 1024
BATCH = 1
SEQ = 512
DEPTH = 2
DEC_BATCH = 8
DEC_SEQ = 1
PAST_LEN = 2048
PAGE_SIZE = 128

N_MIXERS = 2
NSA_HEADS = 16
NSA_KV_HEADS = 4
HEAD_DIM = 64
NSA_GROUP = NSA_HEADS // NSA_KV_HEADS
NSA_Q = NSA_HEADS * HEAD_DIM
NSA_KV = NSA_KV_HEADS * HEAD_DIM
NSA_IN = NSA_Q + 6 * NSA_KV + 3 * NSA_HEADS
BLOCK = 64
TOP_BLOCKS = 16
N_LOCAL_BLOCKS = 2
WINDOW = 512
QUERY_BLOCK = 16
FORCE_SCORE = 1e4
HGRN_HEADS = 8
HGRN_DK = D_MODEL // HGRN_HEADS
HGRN_DV = D_MODEL // HGRN_HEADS
HGRN_CHUNK = 64
N_BUCKETS = 32
MAX_DISTANCE = 1024
D_FF = ((8 * D_MODEL + 3 * 256 - 1) // (3 * 256)) * 256
N_NSA = (DEPTH + 1) // 2
N_HGRN = DEPTH // 2

kernel_name = "nsa_hgrn2_hybrid_step"

def rms_norm(x, w, eps=1e-6):
    xf = x.astype(jnp.float32)
    y = xf * lax.rsqrt(jnp.mean(xf * xf, axis=-1, keepdims=True) + eps)
    return (y * w.astype(jnp.float32)).astype(x.dtype)

def t5_bucket(dist):
    n = jnp.maximum(dist, 0)
    max_exact = N_BUCKETS // 2
    nf = jnp.maximum(n, 1).astype(jnp.float32)
    large = max_exact + (jnp.log(nf / max_exact) / math.log(MAX_DISTANCE / max_exact)
                         * (N_BUCKETS - max_exact)).astype(jnp.int32)
    large = jnp.minimum(large, N_BUCKETS - 1)
    return jnp.where(n < max_exact, n, large)

def masked_softmax(s, mask):
    s = jnp.where(mask, s.astype(jnp.float32), -jnp.inf)
    m = jnp.max(s, axis=-1, keepdims=True)
    m = jnp.where(jnp.isfinite(m), m, 0.0)
    e = jnp.exp(s - m)
    d = jnp.sum(e, axis=-1, keepdims=True)
    return e / jnp.where(d > 0, d, 1.0)

def compress_blocks(rows, pe, w1, w2):
    b, l, g, d = rows.shape
    z = rows.reshape(b, l // BLOCK, BLOCK, g, d) + pe[None, None, :, None, :]
    z = jnp.transpose(z, (0, 1, 3, 2, 4)).reshape(b, l // BLOCK, g, BLOCK * d)
    return jax.nn.silu(z @ w1) @ w2

def to_key_blocks(rows):
    b, l, g, d = rows.shape
    return jnp.transpose(rows.reshape(b, l // BLOCK, BLOCK, g, d), (0, 3, 1, 2, 4))

def nsa_split(h):
    b, t, _ = h.shape
    q = h[..., :NSA_Q].reshape(b, t, NSA_HEADS, HEAD_DIM)
    kv = h[..., NSA_Q:NSA_Q + 6 * NSA_KV].reshape(b, t, 3, 2, NSA_KV_HEADS, HEAD_DIM)
    gates = h[..., NSA_Q + 6 * NSA_KV:].reshape(b, t, 3, NSA_HEADS)
    return q, kv, gates

def nsa_attend(q, qpos, kc, vc, ks_blk, vs_blk, kw, vw, kwpos, gate_logits, rel_bias):
    b, t = q.shape[0], q.shape[1]
    G, R = NSA_KV_HEADS, NSA_GROUP
    scale = HEAD_DIM ** -0.5
    qg = q.reshape(b, t, G, R, HEAD_DIM)
    tab = rel_bias.reshape(N_BUCKETS, G, R)
    nb = kc.shape[1]
    blk = jnp.arange(nb)
    dist_c = qpos[:, None] - ((blk + 1) * BLOCK - 1)[None, :]
    bias_c = jnp.transpose(tab[t5_bucket(dist_c)], (2, 3, 0, 1))
    s_c = jnp.einsum('btgrd,bngd->bgrtn', qg, kc) * scale + bias_c
    p_c = masked_softmax(s_c, dist_c >= 0)
    o_c = jnp.einsum('bgrtn,bngd->btgrd', p_c, vc)
    imp = jnp.sum(p_c, axis=2)
    started = (blk * BLOCK)[None, :] <= qpos[:, None]
    cur = (qpos // BLOCK)[:, None]
    forced = started & ((blk[None, :] == 0) | (blk[None, :] > cur - N_LOCAL_BLOCKS))
    score = jnp.where(forced, FORCE_SCORE, jnp.where(dist_c >= 0, imp, -jnp.inf))
    top_val, top_idx = lax.top_k(score, min(TOP_BLOCKS, nb))
    gather = jax.vmap(jax.vmap(lambda kb, ib: kb[ib]))
    k_sel = gather(ks_blk, top_idx)
    v_sel = gather(vs_blk, top_idx)
    tok = top_idx[..., None] * BLOCK + jnp.arange(BLOCK)
    dist_s = qpos[None, None, :, None, None] - tok
    n_sel = top_idx.shape[-1] * BLOCK
    mask_s = ((top_val > -jnp.inf)[..., None] & (dist_s >= 0)).reshape(b, G, 1, t, n_sel)
    bias_s = tab[t5_bucket(dist_s), jnp.arange(G)[None, :, None, None, None]]
    bias_s = jnp.moveaxis(bias_s.reshape(b, G, t, n_sel, R), -1, 2)
    s_s = jnp.einsum('btgrd,bgtjd->bgrtj', qg, k_sel.reshape(b, G, t, n_sel, HEAD_DIM)) * scale + bias_s
    p_s = masked_softmax(s_s, mask_s)
    o_s = jnp.einsum('bgrtj,bgtjd->btgrd', p_s, v_sel.reshape(b, G, t, n_sel, HEAD_DIM))
    dist_w = qpos[:, None] - kwpos[None, :]
    mask_w = (dist_w >= 0) & (dist_w < WINDOW) & (kwpos[None, :] >= 0)
    bias_w = jnp.transpose(tab[t5_bucket(dist_w)], (2, 3, 0, 1))
    s_w = jnp.einsum('btgrd,bsgd->bgrts', qg, kw) * scale + bias_w
    p_w = masked_softmax(s_w, mask_w)
    o_w = jnp.einsum('bgrts,bsgd->btgrd', p_w, vw)
    gts = jax.nn.sigmoid(gate_logits.astype(jnp.float32)).reshape(b, t, 3, G, R, 1)
    o = gts[:, :, 0] * o_c + gts[:, :, 1] * o_s + gts[:, :, 2] * o_w
    return o.reshape(b, t, NSA_Q).astype(q.dtype)

def nsa_prompt(x, w_in, w_out, cmp_pe, cmp_w1, cmp_w2, rel_bias):
    b, s, _ = x.shape
    q, kv, gl = nsa_split(x @ w_in)
    kv_c, kv_s, kv_w = kv[:, :, 0], kv[:, :, 1], kv[:, :, 2]
    kc = compress_blocks(kv_c[:, :, 0], cmp_pe[0], cmp_w1[0], cmp_w2[0])
    vc = compress_blocks(kv_c[:, :, 1], cmp_pe[1], cmp_w1[1], cmp_w2[1])
    ks_blk = to_key_blocks(kv_s[:, :, 0])
    vs_blk = to_key_blocks(kv_s[:, :, 1])
    kw_pad = jnp.pad(kv_w, ((0, 0), (WINDOW, 0), (0, 0), (0, 0), (0, 0)))

    def query_block(i):
        q0 = i * QUERY_BLOCK
        qb = lax.dynamic_slice_in_dim(q, q0, QUERY_BLOCK, axis=1)
        gb = lax.dynamic_slice_in_dim(gl, q0, QUERY_BLOCK, axis=1)
        kwb = lax.dynamic_slice_in_dim(kw_pad, q0, WINDOW + QUERY_BLOCK, axis=1)
        qpos = q0 + jnp.arange(QUERY_BLOCK)
        kwpos = q0 - WINDOW + jnp.arange(WINDOW + QUERY_BLOCK)
        return nsa_attend(qb, qpos, kc, vc, ks_blk, vs_blk, kwb[:, :, 0], kwb[:, :, 1], kwpos, gb, rel_bias)

    o = lax.map(query_block, jnp.arange(s // QUERY_BLOCK))
    o = jnp.moveaxis(o, 0, 1).reshape(b, s, NSA_Q)
    win_buf = min(WINDOW, PAST_LEN)
    tail = kv_w[:, max(s - win_buf, 0):]
    if s < win_buf:
        tail = jnp.pad(tail, ((0, 0), (win_buf - s, 0), (0, 0), (0, 0), (0, 0)))
    return o @ w_out, kv_c, kv_s, tail

def nsa_sample(x, cache_cmp, cache_slc, win_state, page_table, w_in, w_out, cmp_pe, cmp_w1, cmp_w2, rel_bias):
    b, t, _ = x.shape
    q, kv, gl = nsa_split(x @ w_in)
    kv_c, kv_s, kv_w = kv[:, :, 0], kv[:, :, 1], kv[:, :, 2]
    pad = (-(PAST_LEN + t)) % BLOCK

    def full_rows(cache, new):
        past = cache[page_table].reshape(b, -1, *cache.shape[2:])
        rows = jnp.concatenate([past, new], axis=1)
        return jnp.pad(rows, ((0, 0), (0, pad), (0, 0), (0, 0), (0, 0)))

    fc = full_rows(cache_cmp, kv_c)
    fs = full_rows(cache_slc, kv_s)
    kc = compress_blocks(fc[:, :, 0], cmp_pe[0], cmp_w1[0], cmp_w2[0])
    vc = compress_blocks(fc[:, :, 1], cmp_pe[1], cmp_w1[1], cmp_w2[1])
    ks_blk = to_key_blocks(fs[:, :, 0])
    vs_blk = to_key_blocks(fs[:, :, 1])
    kw_all = jnp.concatenate([win_state, kv_w], axis=1)
    win_buf = win_state.shape[1]
    qpos = PAST_LEN + jnp.arange(t)
    kwpos = PAST_LEN - win_buf + jnp.arange(win_buf + t)
    o = nsa_attend(q, qpos, kc, vc, ks_blk, vs_blk, kw_all[:, :, 0], kw_all[:, :, 1], kwpos, gl, rel_bias)
    return o @ w_out, kv_c, kv_s, kw_all[:, t:]

def hgrn_chunk(S0, q, k, v, log_f):
    G = jnp.cumsum(log_f, axis=2)
    c = q.shape[2]
    causal = jnp.tril(jnp.ones((c, c), dtype=bool))
    diff = G[:, :, :, None, :] - G[:, :, None, :, :]
    decay = jnp.exp(jnp.where(causal[:, :, None], diff, -jnp.inf))
    attn = jnp.sum(q[:, :, :, None, :] * k[:, :, None, :, :] * decay, axis=-1)
    o = jnp.einsum('bhtk,bhkv->bhtv', q * jnp.exp(G), S0) + jnp.einsum('bhts,bhsv->bhtv', attn, v)
    G_last = G[:, :, -1, :]
    S = jnp.exp(G_last)[..., None] * S0 + jnp.einsum('bhsk,bhsv->bhkv', k * jnp.exp(G_last[:, :, None, :] - G), v)
    return o, S

def hgrn_recurrence(q, k, v, log_f, S0):
    b, h, t, _ = q.shape
    c = HGRN_CHUNK if t % HGRN_CHUNK == 0 else t
    n = t // c

    def split(a):
        return jnp.moveaxis(a.reshape(b, h, n, c, a.shape[-1]), 2, 0)

    def step(S, inp):
        o, S = hgrn_chunk(S, *inp)
        return S, o

    S_final, o = lax.scan(step, S0, (split(q), split(k), split(v), split(log_f)))
    return jnp.moveaxis(o, 0, 2).reshape(b, h, t, -1), S_final

def hgrn_mixer(x, S0, w_in, w_out, norm_w, lb):
    b, t, _ = x.shape
    hq, hf, hi, hg = jnp.split((x @ w_in).astype(jnp.float32), 4, axis=-1)

    def heads(a):
        return jnp.transpose(a.reshape(b, t, HGRN_HEADS, -1), (0, 2, 1, 3))

    f = lb + (1.0 - lb) * jax.nn.sigmoid(hf)
    o, S = hgrn_recurrence(heads(jax.nn.silu(hq)), heads(1.0 - f), heads(hi), heads(jnp.log(f)),
                           S0.astype(jnp.float32))
    o = rms_norm(jnp.transpose(o, (0, 2, 1, 3)), norm_w).reshape(b, t, D_MODEL)
    o = o * jax.nn.sigmoid(hg)
    return o.astype(x.dtype) @ w_out, S

def swiglu(x, w_gu, w_down):
    a, g = jnp.split(x @ w_gu, 2, axis=-1)
    return (jax.nn.silu(a) * g) @ w_down

def setup_inputs(seed: int = 0) -> dict:
    key = jax.random.key(seed)
    ks = jax.random.split(key, 24)
    n_pages = PAST_LEN // PAGE_SIZE
    n_used = DEC_BATCH * n_pages
    pool = n_used + (n_used + 3) // 4
    win_buf = min(WINDOW, PAST_LEN)
    nrm = jax.random.normal
    f32 = jnp.float32
    page_table = jax.random.permutation(ks[0], pool)[:n_used].reshape(DEC_BATCH, n_pages).astype(jnp.int32)
    return {
        "x_prompt": nrm(ks[1], (BATCH, SEQ, D_MODEL), f32),
        "x_sample": nrm(ks[2], (DEC_BATCH, DEC_SEQ, D_MODEL), f32),
        "cache_cmp_kv": nrm(ks[3], (N_NSA, pool, PAGE_SIZE, 2, NSA_KV_HEADS, HEAD_DIM), f32),
        "cache_slc_kv": nrm(ks[4], (N_NSA, pool, PAGE_SIZE, 2, NSA_KV_HEADS, HEAD_DIM), f32),
        "state_win_kv": nrm(ks[5], (N_NSA, DEC_BATCH, win_buf, 2, NSA_KV_HEADS, HEAD_DIM), f32),
        "state_hgrn": 0.5 * nrm(ks[6], (N_HGRN, DEC_BATCH, HGRN_HEADS, HGRN_DK, HGRN_DV), f32),
        "page_table": page_table,
        "norm_w": 1.0 + 0.05 * nrm(ks[7], (DEPTH, 4, D_MODEL), f32),
        "nsa_w_in": nrm(ks[8], (N_NSA, D_MODEL, NSA_IN), f32) * D_MODEL ** -0.5,
        "nsa_w_out": nrm(ks[9], (N_NSA, NSA_Q, D_MODEL), f32) * NSA_Q ** -0.5,
        "nsa_cmp_pe": 0.1 * nrm(ks[10], (N_NSA, 2, BLOCK, HEAD_DIM), f32),
        "nsa_cmp_w1": nrm(ks[11], (N_NSA, 2, BLOCK * HEAD_DIM, HEAD_DIM), f32) * (BLOCK * HEAD_DIM) ** -0.5,
        "nsa_cmp_w2": nrm(ks[12], (N_NSA, 2, HEAD_DIM, HEAD_DIM), f32) * HEAD_DIM ** -0.5,
        "rel_bias": 0.5 * nrm(ks[13], (N_BUCKETS, NSA_HEADS), f32),
        "hgrn_w_in": nrm(ks[14], (N_HGRN, D_MODEL, 4 * D_MODEL), f32) * D_MODEL ** -0.5,
        "hgrn_w_out": nrm(ks[15], (N_HGRN, D_MODEL, D_MODEL), f32) * D_MODEL ** -0.5,
        "hgrn_norm_w": 1.0 + 0.05 * nrm(ks[16], (N_HGRN, HGRN_DV), f32),
        "hgrn_lb_logits": nrm(ks[17], (DEPTH, HGRN_HEADS * HGRN_DK), f32),
        "ffn_w_gu": nrm(ks[18], (DEPTH, D_MODEL, 2 * D_FF), f32) * D_MODEL ** -0.5,
        "ffn_w_down": nrm(ks[19], (DEPTH, D_FF, D_MODEL), f32) * D_FF ** -0.5,
    }

def reference(x_prompt, x_sample, cache_cmp_kv, cache_slc_kv, state_win_kv, state_hgrn, page_table,
              norm_w, nsa_w_in, nsa_w_out, nsa_cmp_pe, nsa_cmp_w1, nsa_cmp_w2, rel_bias,
              hgrn_w_in, hgrn_w_out, hgrn_norm_w, hgrn_lb_logits, ffn_w_gu, ffn_w_down):
    lb_all = jnp.cumsum(jax.nn.softmax(hgrn_lb_logits.astype(jnp.float32), axis=0), axis=0)
    lb_all = lb_all - lb_all[0]
    hp, hs = x_prompt, x_sample
    p_cmp, p_slc, p_win, p_hgrn = [], [], [], []
    s_cmp, s_slc, s_win, s_hgrn = [], [], [], []
    for layer in range(DEPTH):
        j = layer // N_MIXERS
        nw = norm_w[layer]
        xp, xs = rms_norm(hp, nw[0]), rms_norm(hs, nw[0])
        if layer % N_MIXERS == 0:
            mp, c_p, sl_p, w_p = nsa_prompt(xp, nsa_w_in[j], nsa_w_out[j], nsa_cmp_pe[j], nsa_cmp_w1[j],
                                            nsa_cmp_w2[j], rel_bias)
            ms, c_s, sl_s, w_s = nsa_sample(xs, cache_cmp_kv[j], cache_slc_kv[j], state_win_kv[j], page_table,
                                            nsa_w_in[j], nsa_w_out[j], nsa_cmp_pe[j], nsa_cmp_w1[j],
                                            nsa_cmp_w2[j], rel_bias)
            p_cmp.append(c_p); p_slc.append(sl_p); p_win.append(w_p)
            s_cmp.append(c_s); s_slc.append(sl_s); s_win.append(w_s)
        else:
            S0 = jnp.zeros((hp.shape[0], HGRN_HEADS, HGRN_DK, HGRN_DV), jnp.float32)
            mp, S_p = hgrn_mixer(xp, S0, hgrn_w_in[j], hgrn_w_out[j], hgrn_norm_w[j], lb_all[layer])
            ms, S_s = hgrn_mixer(xs, state_hgrn[j], hgrn_w_in[j], hgrn_w_out[j], hgrn_norm_w[j], lb_all[layer])
            p_hgrn.append(S_p); s_hgrn.append(S_s)
        hp = hp + rms_norm(mp, nw[1])
        hs = hs + rms_norm(ms, nw[1])
        hp = hp + rms_norm(swiglu(rms_norm(hp, nw[2]), ffn_w_gu[layer], ffn_w_down[layer]), nw[3])
        hs = hs + rms_norm(swiglu(rms_norm(hs, nw[2]), ffn_w_gu[layer], ffn_w_down[layer]), nw[3])
    return (hp, hs, jnp.stack(p_cmp), jnp.stack(p_slc), jnp.stack(p_win), jnp.stack(p_hgrn),
            jnp.stack(s_cmp), jnp.stack(s_slc), jnp.stack(s_win), jnp.stack(s_hgrn))


_drawn_inputs = setup_inputs


def setup_inputs(seed=0):
    import zlib

    import numpy as np

    out = dict(_drawn_inputs(seed))
    spreads = {}
    factors = {}
    for name, (base, spread) in spreads.items():
        noise = np.random.default_rng([zlib.crc32(name.encode()), seed]).standard_normal(out[name].shape)
        drawn = base * np.exp(spread * noise) if base else spread * noise
        out[name] = __import__('jax').numpy.asarray(drawn.astype(out[name].dtype))
    for name, factor in factors.items():
        out[name] = (out[name] * factor).astype(out[name].dtype)
    return out
```

```python
from contextlib import ExitStack

import numpy as np

import concourse.bass as bass
from concourse import mybir

F32 = mybir.dt.float32
I32 = mybir.dt.int32
ALU = mybir.AluOpType
ACT = mybir.ActivationFunctionType
AX = mybir.AxisListType.X

P = 128
D_MODEL = 1024
KC = D_MODEL // P
SEQ = 512
NB = 8
T = SEQ + NB
TH = T // 2
TILES = SEQ // P
PAST = 2048
PAGES = PAST // P
POOL = 160
HEADS, KVH, HD = 16, 4, 64
GP = KVH // 2
REP = HEADS // KVH
BLOCK = 64
NBLK = PAST // BLOCK
PBLK = SEQ // BLOCK
WIN = 512
N_BUCKETS = 32
MAX_DISTANCE = 1024
D_FF = 2816
FF = D_FF // P
HH = 8
NSA_UNITS = 21
HGRN_UNITS = 32
EPS = 1e-6
NEG = -1e30
FLOOR = -1e20
Q_U, CK_U, CV_U, SK_U, SV_U, WK_U, WV_U, GATE_U = 0, 8, 10, 12, 14, 16, 18, 20
RING = 4
SUBK = 11
SKEW = SEQ + P
LEVELS = [64, 32, 16, 8, 4, 2]


class Seq:

    def __init__(self, eng, sem, base=0):
        self.eng, self.sem, self.base, self.n = eng, sem, base, 0

    def __call__(self, ins):
        ins.then_inc(self.sem, 1)
        self.n += 1
        return self.n

    def wait(self, n=None):
        self.eng.wait_ge(self.sem, self.base + (self.n if n is None else n))

    def link(self, ins):
        self(ins)
        self.wait()


class Core:

    def __init__(self, nc, ctx):
        self.nc = nc
        sb = lambda n, s, d=F32: ctx.enter_context(nc.sbuf_tensor(n, s, d))
        sem = lambda n: ctx.enter_context(nc.semaphore(n))
        self.X = sb("X", [P, KC, T])
        self.XW = sb("XW", [P, KC, T])
        self.rstd = sb("rstd", [P, T])
        self.ring = sb("ring", [P, RING, SUBK * P])
        self.nw = sb("nw", [P, 2, 4, KC])
        self.ident = sb("ident", [P, P])
        self.ones = sb("ones", [P, P])
        self.loaded = [sem(f"weights_loaded{s}") for s in range(RING)]
        self.tile_done = [sem(f"weights_used{s}") for s in range(RING)]
        self.psum_free = [sem(f"unit_evacuated{s}") for s in range(RING)]
        self.loads = [0] * RING
        self.done = [0] * RING
        self.freed = [1] * RING


def pairs(ap):
    return ap.rearrange("p (h t) -> p h t", h=2)


def load_tile(eng, c, w, s, index, kcs):
    dst = c.ring[:, s, 0:kcs * P]
    src = w[bass.ds(index, 1)] if not isinstance(index, int) else w[index:index + 1]
    eng.dma_start(dst, src.rearrange("o p n -> p (o n)")).then_inc(c.loaded[s], 16)


def linear(c, name, w, n_units, subs, kcs, src, evac, nxt, width=P):
    nc = c.nc
    tiles = n_units * subs
    loops, rest = tiles // RING, tiles % RING
    per = RING // subs
    base_load, base_done, base_free = list(c.loads), list(c.done), list(c.freed)
    with ExitStack() as ctx:
        ps = [ctx.enter_context(nc.psum_tensor(f"{name}_ps{j}", [P, 2, 512], F32)) for j in range(per)]
        block = ctx.enter_context(nc.Block())

        @block.sync
        def _(sp):
            if loops > 1:
                with sp.Fori(0, loops - 1) as i:
                    for s in range(RING):
                        sp.wait_ge(c.tile_done[s], i + (base_done[s] + 1))
                        load_tile(sp, c, w, s, i * RING + (RING + s), kcs)
            for s in range(RING):
                sp.wait_ge(c.tile_done[s], base_done[s] + loops)
                if s < rest:
                    load_tile(sp, c, w, s, loops * RING + s, kcs)
                    sp.wait_ge(c.tile_done[s], base_done[s] + loops + 1)
                if nxt is not None:
                    load_tile(sp, c, nxt[0], s, s, nxt[1])

        @block.tensor
        def _(pe):
            def one(s, i_load, i_free, cols=P):
                j, sub = s // subs, s % subs
                pe.wait_ge(c.loaded[s], i_load)
                if sub == 0:
                    pe.wait_ge(c.psum_free[j], i_free)
                for k in range(kcs):
                    for h in range(2):
                        last = pe.matmul(ps[j][0:cols, h, 0:TH], c.ring[:, s, k * P:k * P + cols],
                                         src[:, sub * kcs + k, h * TH:(h + 1) * TH],
                                         start=(sub == 0 and k == 0), stop=(sub == subs - 1 and k == kcs - 1))
                last.then_inc(c.tile_done[s], 1)

            with pe.Fori(0, loops) as i:
                for s in range(RING):
                    one(s, i * 16 + 16 * base_load[s], i + base_free[s // subs])
            for s in range(rest):
                one(s, 16 * (base_load[s] + loops), base_free[s // subs] + loops, width)

        def ready(eng, j, i):
            s = j * subs + subs - 1
            eng.wait_ge(c.tile_done[s], i + (base_done[s] + 1))

        evac(block, ps, per, loops, rest // subs, ready, base_free)
    for s in range(RING):
        c.done[s] += loops + (s < rest)
        c.loads[s] += loops - 1 + (s < rest) + (nxt is not None)
        if s < per:
            c.freed[s] += loops + (s < rest)


def evac_scaled(c, dst, width=P):
    def evac(block, ps, per, loops, rest, ready, base_free):
        @block.vector
        def _(dve):
            with dve.Fori(0, loops) as i:
                for j in range(per):
                    ready(dve, j, i)
                    dve.tensor_tensor(dst[:, bass.ds(i * per + j, 1), :].rearrange("p o (h t) -> p (o h) t", h=2),
                                      ps[j][:, :, 0:TH], pairs(c.rstd[:, :]), ALU.mult).then_inc(c.psum_free[j], 1)
            for j in range(rest):
                ready(dve, j, loops)
                dve.tensor_tensor(pairs(dst[0:width, loops * per + j, :]), ps[j][0:width, :, 0:TH],
                                  pairs(c.rstd[0:width, :]), ALU.mult).then_inc(c.psum_free[j], 1)
    return evac


def evac_swiglu(c, dst, a_t, g_t, sems):
    a_in, a_act, g_in, prod = sems

    def evac(block, ps, per, loops, rest, ready, base_free):
        @block.vector
        def _(dve):
            with dve.Fori(0, loops) as i:
                for m in range(2):
                    ready(dve, 2 * m, i)
                    dve.wait_ge(prod[m], i + 1)
                    dve.tensor_tensor(pairs(a_t[:, m, :]), ps[2 * m][:, :, 0:TH], pairs(c.rstd[:, :]),
                                      ALU.mult).then_inc(c.psum_free[2 * m], 1)
                    ready(dve, 2 * m + 1, i)
                    dve.tensor_tensor(pairs(g_t[:, m, :]), ps[2 * m + 1][:, :, 0:TH], pairs(c.rstd[:, :]),
                                      ALU.mult).then_inc(c.psum_free[2 * m + 1], 1)

        @block.scalar
        def _(act):
            with act.Fori(0, loops) as i:
                for m in range(2):
                    act.wait_ge(c.psum_free[2 * m], i + (base_free[2 * m] + 1))
                    act.activation(a_t[:, m, :], a_t[:, m, :], ACT.Silu).then_inc(a_act[m], 1)

        @block.gpsimd
        def _(pool):
            for m in range(2):
                pool.sem_inc(prod[m], 1)
            with pool.Fori(0, loops) as i:
                for m in range(2):
                    pool.wait_ge(a_act[m], i + 1)
                    pool.wait_ge(c.psum_free[2 * m + 1], i + (base_free[2 * m + 1] + 1))
                    pool.tensor_tensor(dst[:, bass.ds(i * 2 + m, 1), :].rearrange("p o t -> p (o t)"),
                                       a_t[:, m, :], g_t[:, m, :], ALU.mult).then_inc(prod[m], 1)
    return evac


def evac_squares(c, dst, sq, ssq, sems):
    squared, added = sems

    def evac(block, ps, per, loops, rest, ready, base_free):
        @block.scalar
        def _(act):
            with act.Fori(0, loops) as i:
                for j in range(per):
                    ready(act, j, i)
                    act.activation(dst[:, bass.ds(i * per + j, 1), :].rearrange("p o (h t) -> p (o h) t", h=2),
                                   ps[j][:, :, 0:TH], ACT.Copy).then_inc(c.psum_free[j], 1)

        @block.vector
        def _(dve):
            dve.memset(ssq[:, :], 0.0).then_inc(added, 1)
            with dve.Fori(0, loops) as i:
                for j in range(per):
                    dve.wait_ge(c.psum_free[j], i + (base_free[j] + 1))
                    v = dst[:, bass.ds(i * per + j, 1), :].rearrange("p o t -> p (o t)")
                    dve.wait_ge(added, i * per + (j + 1))
                    dve.tensor_tensor(sq[:, :], v, v, ALU.mult).then_inc(squared, 1)
                    dve.wait_ge(squared, i * per + (j + 1))
                    dve.tensor_tensor(ssq[:, :], ssq[:, :], sq[:, :], ALU.add).then_inc(added, 1)
    return evac


def norm_step(c, name, ssq, sq, post=None, pre=None):
    nc = c.nc
    with ExitStack() as ctx:
        sem = lambda n: nc.alloc_semaphore(f"{name}_{n}")
        summed, mean_in, rooted, own_done, x_new, squared, added = [sem(n) for n in
            ("token_sums", "mean_squares", "roots", "dve_chain", "x_new", "squares", "squares_added")]
        ps = ctx.enter_context(nc.psum_tensor(f"{name}_ps", [P, 2, 512], F32))
        tmp = ctx.enter_context(nc.sbuf_tensor(f"{name}_tmp", [P, 2, T], F32))
        block = ctx.enter_context(nc.Block())
        rounds = (post is not None) + (pre is not None)

        @block.tensor
        def _(pe):
            for r in range(rounds):
                if post is None or r:
                    pe.wait_ge(added, KC)
                for h in range(2):
                    mm = pe.matmul(ps[:, h, 0:TH], c.ones[:, :], ssq[:, h * TH:(h + 1) * TH], start=True, stop=True)
                mm.then_inc(summed, 1)

        @block.scalar
        def _(act):
            for r in range(rounds):
                if post is None or r:
                    for k in range(KC):
                        if post is not None:
                            act.wait_ge(x_new, k + 1)
                        if k >= 2:
                            act.wait_ge(added, k - 1)
                        act.activation(tmp[:, k % 2, :], c.X[:, k, :], ACT.Square).then_inc(squared, 1)
                act.wait_ge(mean_in, r + 1)
                act.activation(c.rstd[:, :], c.rstd[:, :], ACT.Sqrt).then_inc(rooted, 1)

        @block.vector
        def _(dve):
            own = Seq(dve, own_done)

            def rstd(r):
                dve.wait_ge(summed, r + 1)
                dve.tensor_scalar(pairs(c.rstd[:, :]), ps[:, :, 0:TH], 1.0 / D_MODEL, EPS, ALU.mult, ALU.add)\
                   .then_inc(mean_in, 1)
                dve.wait_ge(rooted, r + 1)
                own.link(dve.reciprocal(c.rstd[:, :], c.rstd[:, :]))

            if post is not None:
                rstd(0)
            for k in range(KC):
                if post is not None:
                    own.link(dve.scalar_tensor_tensor(sq[:, :], post[0][:, k, :], post[1][:, k:k + 1], c.rstd[:, :],
                                                      ALU.mult, ALU.mult))
                    dve.tensor_tensor(c.X[:, k, :], c.X[:, k, :], sq[:, :], ALU.add).then_inc(x_new, 1)
                    dve.wait_ge(x_new, k + 1)
                if pre is not None:
                    own(dve.tensor_scalar(c.XW[:, k, :], c.X[:, k, :], pre[:, k:k + 1], None, ALU.mult))
            if pre is not None:
                for k in range(KC):
                    dve.wait_ge(squared, k + 1)
                    if k == 0:
                        dve.tensor_copy(ssq[:, :], tmp[:, 0, :]).then_inc(added, 1)
                    else:
                        dve.wait_ge(added, k)
                        dve.tensor_tensor(ssq[:, :], ssq[:, :], tmp[:, k % 2, :], ALU.add).then_inc(added, 1)
                rstd(rounds - 1)


def compress(c, HT, d, kcT, kcBD, vcS, BDv):
    nc = c.nc
    CH = 32
    NCH = NB * PAGES // CH
    with ExitStack() as ctx:
        sem = lambda n: nc.alloc_semaphore(f"cmp_{n}")
        sb = lambda n, s: ctx.enter_context(nc.sbuf_tensor(f"cmp_{n}", s, F32))
        w1 = sb("w1", [P, 2, BLOCK // 2, P])
        rows = sb("rows", [P, 2, CH, 256])
        free = c.XW[:, :, :].rearrange("p k t -> p (k t)")
        HN = NB * PAGES * 4 + 2 * PBLK
        hid = free[:, 0:2 * HN].rearrange("p (a n) -> p a n", a=2)
        hid_rep = free[:, 2 * HN:2 * HN + P].rearrange("p (a b n) -> p a b n", a=GP, b=8)
        v_rep = free[:, 2 * HN + P:2 * HN + 2 * P]
        pe_in = free[:, 1400:1528].rearrange("p (a n) -> p a n", a=2)
        w2 = free[:, 1528:1784].rearrange("p (a n) -> p a n", a=2)
        pe_w = free[:, 1784:1786]
        mask = free[:, 1786:1802]
        ps_c = [ctx.enter_context(nc.psum_tensor(f"cmp_ps{j}", [P, 512], F32)) for j in range(2)]
        ps_p = ctx.enter_context(nc.psum_tensor("cmp_psp", [P, 512], F32))
        ps_k = ctx.enter_context(nc.psum_tensor("cmp_psk", [P, 512], F32))
        ps_q = ctx.enter_context(nc.psum_tensor("cmp_psq", [P, 512], F32))
        ps_v = ctx.enter_context(nc.psum_tensor("cmp_psv", [P, 512], F32))
        small, w1_in = sem("small_loaded"), [sem(f"w1_half{h}_loaded") for h in range(2)]
        rows_in = [sem(f"rows{s}_loaded") for s in range(2)]
        w1_used = sem("w1_half0_used")
        prompt_done, pe_done, pe_out = sem("prompt_products"), sem("pe_products"), sem("pe_copied")
        chunk_done = [sem(f"chunk{s}_products") for s in range(2)]
        chunk_out = [sem(f"chunk{s}_silu") for s in range(2)]
        prompt_out, second, moved, own_done = sem("prompt_silu"), sem("second_products"), sem("rep_ready"), sem("chain")
        block = ctx.enter_context(nc.Block())

        @block.sync
        def _(sp):
            sp.dma_start(pe_in[:, :, :], d["cmp_pe"]).then_inc(small, 16)
            sp.dma_start(w2[:, :, :], d["cmp_w2"]).then_inc(small, 16)
            sp.dma_start(mask[:, :], d["head_mask"]).then_inc(small, 16)
            for kv in range(2):
                for h in range(2):
                    if kv:
                        sp.wait_ge(*((w1_used, 1) if h == 0 else (chunk_done[1], NCH // 2)))
                    sp.dma_start(w1[:, h].rearrange("p t n -> p (t n)"), d["cmp_w1"][kv, h]).then_inc(w1_in[h], 16)
                for ch in range(NCH):
                    s = ch % 2
                    if kv or ch >= 2:
                        sp.wait_ge(chunk_done[s], kv * (NCH // 2) + ch // 2)
                    with sp.Fori(0, CH) as i:
                        page = sp.value_load(c.pages[0:1, bass.ds(i + ch * CH, 1)], min_val=0, max_val=POOL - 1)
                        sp.dma_start(rows[:, s, bass.ds(i, 1), :].rearrange("p o n -> p (o n)"),
                                     d["cache_cmp"][kv, bass.ds(page, 1)].rearrange("o p n -> p (o n)"))\
                          .then_inc(rows_in[s], 16)

        @block.tensor
        def _(pe):
            pe.wait_ge(small, 48)
            for kv in range(2):
                for h in range(2):
                    pe.wait_ge(w1_in[h], 16 * (kv + 1))
                if kv:
                    pe.wait_ge(prompt_out, 1)
                for t in range(BLOCK):
                    mm = pe.matmul(ps_p[:, 0:16], w1[:, t // 32, t % 32, :],
                                   HT[:, CK_U + 2 * kv:CK_U + 2 * kv + 2, t:SEQ:BLOCK], start=t == 0, stop=t == BLOCK - 1)
                mm.then_inc(prompt_done, 1)
                for t in range(BLOCK):
                    mm = pe.matmul(ps_p[:, 16:17], w1[:, t // 32, t % 32, :], pe_in[:, kv, t:t + 1],
                                   start=t == 0, stop=t == BLOCK - 1)
                mm.then_inc(pe_done, 1)
                for ch in range(NCH):
                    s = ch % 2
                    n = kv * (NCH // 2) + ch // 2
                    pe.wait_ge(rows_in[s], 16 * CH * (n + 1))
                    if n:
                        pe.wait_ge(chunk_out[s], n)
                    v = rows[:, s].rearrange("p g (c t) -> p g c t", t=BLOCK)
                    for t in range(BLOCK):
                        mm = pe.matmul(ps_c[s][:, 0:P], w1[:, t // 32, t % 32, :], v[:, :, :, t],
                                       start=t == 0, stop=t == BLOCK - 1)
                        if ch == NCH - 1 and t == 31 and kv == 0:
                            mm.then_inc(w1_used, 1)
                    mm.then_inc(chunk_done[s], 1)
            pe.wait_ge(chunk_out[0], NCH)
            pe.wait_ge(chunk_out[1], NCH)
            pe.wait_ge(prompt_out, 2)
            pe.matmul(ps_k[:, :], w2[:, 0, :], hid[:, 0, 0:512], start=True, stop=True).then_inc(second, 1)
            pe.matmul(ps_q[:, 0:16], w2[:, 0, :], hid[:, 0, 512:528], start=True, stop=True).then_inc(second, 1)
            for j in range(4):
                mm = pe.matmul(ps_v[:, j * P:(j + 1) * P], hid[:, 1, j:512:4], w2[:, 1, :], start=True, stop=True)
            mm.then_inc(second, 1)
            pe.wait_ge(moved, 1)
            pe.matmul(ps_c[0][:, 0:P], hid_rep[:, :, :, :].rearrange("p a b n -> p (a b n)"), w2[:, 1, :],
                      start=True, stop=True).then_inc(second, 1)

        @block.scalar
        def _(act):
            for kv in range(2):
                act.wait_ge(pe_done, kv + 1)
                act.activation(pe_w[:, kv:kv + 1], ps_p[:, 16:17], ACT.Copy).then_inc(pe_out, 1)
                act.wait_ge(pe_out, kv + 1)
                act.activation(hid[:, kv, 512:528], ps_p[:, 0:16], ACT.Silu, bias=pe_w[:, kv:kv + 1])\
                   .then_inc(prompt_out, 1)
                for ch in range(NCH):
                    s = ch % 2
                    act.wait_ge(chunk_done[s], kv * (NCH // 2) + ch // 2 + 1)
                    act.activation(hid[:, kv, ch * P:(ch + 1) * P], ps_c[s][:, 0:P], ACT.Silu,
                                   bias=pe_w[:, kv:kv + 1]).then_inc(chunk_out[s], 1)

        @block.vector
        def _(dve):
            own = Seq(dve, own_done)
            own.link(dve.memset(kcBD[:, :, :, :], 0.0))
            dve.wait_ge(prompt_out, 2)
            dve.tensor_copy(hid_rep[:, :, :, :], hid[:, 1, 512:528].rearrange("p (g n) -> p g n", g=GP)
                            .unsqueeze(2).broadcast_to([P, GP, 8, PBLK])).then_inc(moved, 1)
            dve.wait_ge(second, 1)
            own(dve.tensor_copy(kcT[:, :], ps_k[:, :]))
            dve.wait_ge(second, 2)
            for g2 in range(2):
                rows_g = slice(g2 * HD, (g2 + 1) * HD)
                own(dve.tensor_copy(kcBD[rows_g, :, g2, :], ps_q[rows_g, 0:16].rearrange("p (g n) -> p g n", g=GP)))
            dve.wait_ge(second, 3)
            own(dve.tensor_copy(vcS[:, :], ps_v[:, :]))
            dve.wait_ge(second, 4)
            own.link(dve.tensor_copy(v_rep[:, :], ps_c[0][:, 0:P]))
            dve.wait_ge(small, 48)
            for g2 in range(2):
                own(dve.tensor_tensor(BDv[:, :, g2, :],
                                      v_rep[:, g2 * HD:(g2 + 1) * HD].unsqueeze(1).broadcast_to([P, 8, HD]),
                                      mask[:, :].rearrange("p (c g) -> p c g", g=2)[:, :, g2].unsqueeze(2)
                                      .broadcast_to([P, 8, HD]), ALU.mult))


def attention_setup(c, HT, d, tabs, T_bias, biasC, Vtok, gT, Vnew):
    nc = c.nc
    with ExitStack() as ctx:
        sem = lambda n: nc.alloc_semaphore(f"set_{n}")
        sb = lambda n, s: ctx.enter_context(nc.sbuf_tensor(f"set_{n}", s, F32))
        oh = sb("onehot", [N_BUCKETS + 1, 2, 1024])
        R = sb("bias_row", [16, 1024])
        sg = sb("gates", [48, T])
        ps = [ctx.enter_context(nc.psum_tensor(f"set_ps{j}", [P, 512], F32)) for j in range(6)]
        loaded, scaled, gated, row_ready, row_out, t_in = [sem(n) for n in
            ("loaded", "q_scaled", "gates", "bias_row", "bias_row_out", "bias_tiles_in")]
        made, moved, gate_out = sem("psum_ready"), sem("psum_moved"), sem("gates_out")
        block = ctx.enter_context(nc.Block())

        @block.sync
        def _(sp):
            sp.dma_start(oh[:, :, :], d["onehot_rows"]).then_inc(loaded, 16)
            sp.dma_start(tabs[:, :], d["tabs"]).then_inc(loaded, 16)
            sp.dma_start(d["kv_out"], HT[:, CK_U:GATE_U, :]).then_inc(gate_out, 16)
            sp.wait_ge(gated, 1)
            sp.dma_start(d["gate_scratch"], sg[:, SEQ:T]).then_inc(gate_out, 16)
            sp.wait_ge(moved, 2)
            sp.dma_start(d["bias_scratch"], R[:, :]).then_inc(row_out, 16)
            sp.wait_ge(row_out, 16)
            sp.dma_start(d["bias_skew"], bass.AP(d["bias_scratch"].tensor, 0, [[0, P], [1024, HEADS], [1, SKEW]]))\
              .then_inc(t_in, 16)
            sp.wait_ge(t_in, 16)
            sp.dma_start(T_bias[:, :, :], bass.AP(d["bias_skew"].tensor, P - 1, [[HEADS * SKEW - 1, P], [SKEW, HEADS], [1, SEQ]]))\
              .then_inc(t_in, 16)
            sp.wait_ge(t_in, 32)
            sp.wait_ge(gate_out, 32)

        @block.tensor
        def _(pe):
            pe.wait_ge(loaded, 32)
            for j in range(2):
                pe.matmul(ps[j][0:16, :], tabs[:, 0:16], oh[:, 0, j * 512:(j + 1) * 512], start=True, stop=True)\
                  .then_inc(made, 1)
            for i in range(TILES):
                for n in range(PBLK):
                    at = P * i - BLOCK * n - (BLOCK - 1) + 511
                    mm = pe.matmul(ps[2][:, (i * PBLK + n) * 16:(i * PBLK + n + 1) * 16], oh[:, 1, at:at + P],
                                   tabs[:, 0:16], start=True, stop=True)
            mm.then_inc(made, 1)
            pe.wait_ge(gated, 1)
            for i in range(TILES):
                mm = pe.transpose(ps[3][:, i * 48:(i + 1) * 48], sg[:, i * P:(i + 1) * P], c.ident[0:48, 0:48])
            mm.then_inc(made, 1)
            for j, u in enumerate((SV_U, SV_U + 1, WV_U, WV_U + 1)):
                mm = pe.transpose(ps[4][0:NB, j * P:(j + 1) * P], HT[:, u, SEQ:T], c.ident[:, :])
            mm.then_inc(made, 1)
            for i in range(TILES):
                b = ps[5] if i % 2 == 0 else ps[0]
                if i == 1:
                    pe.wait_ge(moved, 2)
                if i >= 2:
                    pe.wait_ge(moved, 4 + i)
                for j, u in enumerate((SV_U, SV_U + 1, WV_U, WV_U + 1)):
                    mm = pe.transpose(b[:, j * P:(j + 1) * P], HT[:, u, i * P:(i + 1) * P], c.ident[:, :])
                mm.then_inc(made, 1)

        @block.scalar
        def _(act):
            act.activation(sg[:, :], HT[0:48, GATE_U, :], ACT.Sigmoid).then_inc(gated, 1)

        @block.vector
        def _(dve):
            dve.tensor_scalar(HT[:, 0:8, :], HT[:, 0:8, :], HD ** -0.5, None, ALU.mult).then_inc(scaled, 1)
            for j in range(2):
                dve.wait_ge(made, j + 1)
                dve.tensor_copy(R[:, j * 512:(j + 1) * 512], ps[j][0:16, :]).then_inc(moved, 1)
            dve.wait_ge(made, 3)
            dve.tensor_copy(biasC[:, :, :, :], ps[2][:, :].rearrange("p (i n h) -> p i h n", i=TILES, n=PBLK))\
               .then_inc(moved, 1)
            dve.wait_ge(made, 4)
            dve.tensor_copy(gT[:, :, :], ps[3][:, 0:192].rearrange("p (i n) -> p i n", i=TILES)).then_inc(moved, 1)
            dve.wait_ge(made, 5)
            dve.tensor_copy(Vnew[:, :], ps[4][0:NB, :]).then_inc(moved, 1)
            for i in range(TILES):
                dve.wait_ge(made, 6 + i)
                dve.tensor_copy(Vtok[:, i, :], (ps[5] if i % 2 == 0 else ps[0])[:, :]).then_inc(moved, 1)


def prompt_compressed(c, HT, kcBD, BDv, biasC, gT, Otok):
    nc = c.nc
    with ExitStack() as ctx:
        sem = lambda n: nc.alloc_semaphore(f"pc_{n}")
        sb = lambda n, s: ctx.enter_context(nc.sbuf_tensor(f"pc_{n}", s, F32))
        S = sb("scores", [P, TILES * HEADS, PBLK])
        mx = sb("max", [P, TILES * HEADS])
        sm = sb("sum", [P, TILES * HEADS])
        PT = sb("probsT", [P, SEQ])
        ps_s = ctx.enter_context(nc.psum_tensor("pc_ps", [P, 512], F32))
        ps_t = ctx.enter_context(nc.psum_tensor("pc_pt", [P, 512], F32))
        ps_o = [ctx.enter_context(nc.psum_tensor(f"pc_po{j}", [P, 2, 512], F32)) for j in range(2)]
        scores, shifted, expd, probs, turned, turned_out, outs, outs_moved, own_done = [sem(n) for n in
            ("scores", "shifted", "exp", "probs", "turned", "turned_out", "outs", "outs_moved", "chain")]
        block = ctx.enter_context(nc.Block())
        wide = lambda a: a.unsqueeze(2).broadcast_to([P, TILES * HEADS, PBLK])

        @block.tensor
        def _(pe):
            for i in range(TILES):
                for u in range(8):
                    at = (i * 8 + u) * 16
                    mm = pe.matmul(ps_s[:, at:at + 16], HT[:, u, i * P:(i + 1) * P],
                                   kcBD[:, u // REP].rearrange("p g n -> p (g n)"), start=True, stop=True)
            mm.then_inc(scores, 1)
            pe.wait_ge(probs, 1)
            for i in range(TILES):
                mm = pe.transpose(ps_t[:, i * P:(i + 1) * P],
                                  S[:, i * HEADS:(i + 1) * HEADS, :].rearrange("p h n -> p (h n)"), c.ident[:, :])
            mm.then_inc(turned, 1)
            pe.wait_ge(turned_out, 1)
            for i in range(TILES):
                if i >= 2:
                    pe.wait_ge(outs_moved, i - 1)
                for j in range(2):
                    mm = pe.matmul(ps_o[i % 2][:, j, :], PT[:, i * P:(i + 1) * P],
                                   BDv[:, 4 * j:4 * j + 4].rearrange("p c g n -> p (c g n)"), start=True, stop=True)
                mm.then_inc(outs, 1)

        @block.scalar
        def _(act):
            act.wait_ge(shifted, 1)
            act.activation(S[:, :, :], S[:, :, :], ACT.Exp).then_inc(expd, 1)

        @block.vector
        def _(dve):
            own = Seq(dve, own_done)
            dve.wait_ge(scores, 1)
            own.link(dve.tensor_tensor(S[:, :, :], ps_s[:, :].rearrange("p (m n) -> p m n", n=PBLK),
                                       biasC[:, :, :, :].rearrange("p i h n -> p (i h) n"), ALU.add))
            own.link(dve.tensor_reduce(mx[:, :], S[:, :, :], AX, ALU.max))
            own.link(dve.tensor_scalar(mx[:, :], mx[:, :], FLOOR, None, ALU.max))
            dve.tensor_tensor(S[:, :, :], S[:, :, :], wide(mx[:, :]), ALU.subtract).then_inc(shifted, 1)
            dve.wait_ge(expd, 1)
            own.link(dve.tensor_reduce(sm[:, :], S[:, :, :], AX, ALU.add))
            own.link(dve.tensor_scalar(sm[:, :], sm[:, :], 1e-30, None, ALU.max))
            own.link(dve.reciprocal(sm[:, :], sm[:, :]))
            own.link(dve.tensor_tensor(sm[:, :].rearrange("p (i h) -> p i h", i=TILES),
                                       sm[:, :].rearrange("p (i h) -> p i h", i=TILES), gT[:, :, 0:16], ALU.mult))
            dve.tensor_tensor(S[:, :, :], S[:, :, :], wide(sm[:, :]), ALU.mult).then_inc(probs, 1)
            dve.wait_ge(turned, 1)
            dve.tensor_copy(PT[:, :], ps_t[:, :]).then_inc(turned_out, 1)
            for i in range(TILES):
                dve.wait_ge(outs, i + 1)
                dve.tensor_copy(Otok[:, i, :], ps_o[i % 2][:, :, :].rearrange("p a b -> p (a b)")).then_inc(outs_moved, 1)


def prompt_attention(c, HT, T_bias, Vtok, gT, Otok):
    nc = c.nc
    items = [(s, g2, br, i) for s in range(2) for g2 in range(2) for br in range(2) for i in range(TILES)]
    N = len(items)
    with ExitStack() as ctx:
        sem = lambda n: nc.alloc_semaphore(f"pa_{n}")
        sb = lambda n, s: ctx.enter_context(nc.sbuf_tensor(f"pa_{n}", s, F32))
        Qs = [sb(f"q{s}", [P, 2, SEQ]) for s in range(2)]
        Tb = [sb(f"bias{s}", [P, 2, SEQ]) for s in range(2)]
        Sb = [sb(f"scores{j}", [P, SEQ]) for j in range(3)]
        E = [sb(f"exp{j}", [P, SEQ]) for j in range(3)]
        ET = [sb(f"expT{j}", [P, SEQ]) for j in range(2)]
        nm = sb("neg_max", [P, 2 * 16])
        rs = sb("row_sum", [P, 2 * 16])
        sc = sb("scale", [P, 2, 16])
        tmp = sb("tmp", [P, 16, HD])
        ps_s = [ctx.enter_context(nc.psum_tensor(f"pa_s{j}", [P, 512], F32)) for j in range(2)]
        ps_t = [ctx.enter_context(nc.psum_tensor(f"pa_t{j}", [P, 512], F32)) for j in range(2)]
        ps_o = [ctx.enter_context(nc.psum_tensor(f"pa_o{j}", [P, 2, 512], F32)) for j in range(2)]
        staged, cleared = [sem(f"chunk{s}_staged") for s in range(2)], sem("cleared")
        scored, biased, expd, turned, turned_out, mixed, merged, own_done = [sem(n) for n in
            ("scores", "biased", "exp", "turned", "turned_out", "mixed", "merged", "chain")]
        block = ctx.enter_context(nc.Block())
        waited = sem("waited")
        n_merge = 6

        @block.gpsimd
        def _(pool):
            for s in range(2):
                pool.memset(Qs[s][:, :, :], 0.0).then_inc(cleared, 1)
            pool.wait_ge(cleared, 2)
            with pool.Fori(0, GP) as gp:
                with pool.Fori(0, 2) as rr:
                    for s in range(2):
                        pool.wait_ge(merged, (gp * 4 + rr * 2) + (s + 1))
                        u = gp * REP + rr * 2 + s
                        own = Seq(pool, staged[s], (gp * 2 + rr) * 4)
                        for g2 in range(2):
                            rows = slice(g2 * HD, (g2 + 1) * HD)
                            own.link(pool.tensor_copy(Qs[s][rows, g2, :], HT[rows, bass.ds(u, 1), 0:SEQ]
                                                      .rearrange("p o t -> p (o t)")))
                            own.link(pool.tensor_copy(Tb[s][:, g2, :], T_bias[:, bass.ds(u * 2 + g2, 1), :]
                                                      .rearrange("p o t -> p (o t)")))

        @block.tensor
        def _(pe):
            with pe.Fori(0, GP) as gp:
                with pe.Fori(0, 2) as rr:
                    it = gp * 2 + rr
                    for n in range(N + 2):
                        if n < N:
                            s, g2, br, i = items[n]
                            if n % 16 == 0:
                                pe.wait_ge(staged[s], it * 4 + 4)
                            if n >= 2:
                                pe.wait_ge(biased, it * N + (n - 1))
                            pe.matmul(ps_s[n % 2][:, 0:(i + 1) * P], Qs[s][:, g2, i * P:(i + 1) * P],
                                      HT[:, bass.ds(gp + (SK_U + 4 * br), 1), 0:(i + 1) * P]
                                      .rearrange("p o t -> p (o t)"), start=True, stop=True).then_inc(scored, 1)
                        if 1 <= n <= N:
                            m = n - 1
                            s, g2, br, i = items[m]
                            pe.wait_ge(expd, it * N + (m + 1))
                            if m >= 2:
                                pe.wait_ge(turned_out, it * N + (m - 1))
                            for j in range(i + 1):
                                mm = pe.transpose(ps_t[m % 2][:, j * P:(j + 1) * P], E[m % 3][:, j * P:(j + 1) * P],
                                                  c.ident[:, :])
                            mm.then_inc(turned, 1)
                        if n >= 2:
                            m = n - 2
                            s, g2, br, i = items[m]
                            pe.wait_ge(turned_out, it * N + (m + 1))
                            if m % 16 == 0:
                                pe.wait_ge(merged, it * 2 + (s + 1))
                            at = (br * 2 + g2) * TILES + i
                            out = ps_o[s][:, at // 8, (at % 8) * HD:(at % 8 + 1) * HD]
                            for j in range(i + 1):
                                v = Vtok[:, j, :].rearrange("p (b n) -> p b n", b=2)[:, br, :]
                                mm = pe.matmul(out, ET[m % 2][:, j * P:(j + 1) * P],
                                               v[:, bass.ds(gp * P + g2 * HD, HD)], start=j == 0, stop=j == i)
                            mm.then_inc(mixed, 1)

        @block.scalar
        def _(act):
            with act.Fori(0, GP) as gp:
                with act.Fori(0, 2) as rr:
                    it = gp * 2 + rr
                    for n, (s, g2, br, i) in enumerate(items):
                        act.wait_ge(biased, it * N + (n + 1))
                        if n >= 3:
                            act.wait_ge(turned, it * N + (n - 2))
                        w = (i + 1) * P
                        k = s * 16 + (br * 2 + g2) * TILES + i
                        act.activation(E[n % 3][:, 0:w], Sb[n % 3][:, 0:w], ACT.Exp, bias=nm[:, k:k + 1], scale=-1.0,
                                       accum_out=rs[:, k:k + 1]).then_inc(expd, 1)

        @block.vector
        def _(dve):
            dve.sem_inc(merged, 1)
            dve.sem_inc(merged, 1)
            with dve.Fori(0, GP) as gp:
                with dve.Fori(0, 2) as rr:
                    it = gp * 2 + rr
                    own = Seq(dve, own_done, it * (2 * n_merge))

                    def merge(s):
                        dve.wait_ge(mixed, it * N + 16 * (s + 1))
                        k = slice(s * 16, (s + 1) * 16)
                        own.link(dve.reciprocal(sc[:, s, :], rs[:, k]))
                        for br in range(2):
                            g = gT[:, :, 16 * (br + 1):16 * (br + 2)].rearrange("p i (c g) -> p c g i", g=2)
                            o = sc[:, s, 8 * br:8 * br + 8].rearrange("p (g i) -> p g i", g=2)
                            own(dve.tensor_tensor(o, o, g[:, bass.ds(gp * REP + rr * 2 + s, 1)]
                                                  .rearrange("p o g i -> p (o g) i"), ALU.mult))
                        own.wait()
                        own.link(dve.tensor_tensor(tmp[:, :, :], ps_o[s][:, :, :].rearrange("p a (b n) -> p (a b) n", n=HD),
                                                   sc[:, s, :].unsqueeze(2).broadcast_to([P, 16, HD]), ALU.mult))
                        own.link(dve.tensor_tensor(tmp[:, 0:8, :], tmp[:, 0:8, :], tmp[:, 8:16, :], ALU.add))
                        o = Otok[:, :, :].rearrange("p i (c n) -> p c i n", n=P)[:, bass.ds(gp * REP + rr * 2 + s, 1)]\
                            .rearrange("p o i n -> p (o i) n")
                        for g2 in range(2):
                            og = o[:, :, g2 * HD:(g2 + 1) * HD]
                            ins = dve.tensor_tensor(og, og, tmp[:, 4 * g2:4 * g2 + 4, :], ALU.add)
                            if g2 == 0:
                                own.link(ins)
                            else:
                                ins.then_inc(merged, 1)

                    for n in range(N + 1):
                        if n < N:
                            s, g2, br, i = items[n]
                            w = (i + 1) * P
                            k = s * 16 + (br * 2 + g2) * TILES + i
                            dve.wait_ge(cleared, 2)
                            dve.wait_ge(scored, it * N + (n + 1))
                            if n >= 3:
                                dve.wait_ge(expd, it * N + (n - 2))
                            dve.sem_inc(waited, 1)
                            dve.tensor_tensor_reduce(Sb[n % 3][:, 0:w], ps_s[n % 2][:, 0:w],
                                                     Tb[s][:, g2, SEQ - w:SEQ], -1.0, 3e38, ALU.add, ALU.min,
                                                     nm[:, k:k + 1]).then_inc(biased, 1)
                        if n >= 1:
                            m = n - 1
                            s, g2, br, i = items[m]
                            dve.wait_ge(turned, it * N + (m + 1))
                            if m >= 2:
                                dve.wait_ge(mixed, it * N + (m - 1))
                            dve.tensor_copy(ET[m % 2][:, 0:(i + 1) * P], ps_t[m % 2][:, 0:(i + 1) * P])\
                               .then_inc(turned_out, 1)
                        if n == 20:
                            merge(0)
                    merge(1)
                    assert own.n == 2 * (n_merge)


def turn_outputs(c, Otok):
    nc = c.nc
    with ExitStack() as ctx:
        ps = [ctx.enter_context(nc.psum_tensor(f"to_ps{j}", [P, 512], F32)) for j in range(2)]
        turned = nc.alloc_semaphore("to_turned")
        moved = nc.alloc_semaphore("to_moved")
        block = ctx.enter_context(nc.Block())

        @block.tensor
        def _(pe):
            for u in range(KC):
                if u >= 2:
                    pe.wait_ge(moved, u - 1)
                for i in range(TILES):
                    mm = pe.transpose(ps[u % 2][:, i * P:(i + 1) * P], Otok[:, i, u * P:(u + 1) * P], c.ident[:, :])
                mm.then_inc(turned, 1)

        @block.vector
        def _(dve):
            for u in range(KC):
                dve.wait_ge(turned, u + 1)
                dve.tensor_copy(c.XW[:, u, 0:SEQ], ps[u % 2][:, :]).then_inc(moved, 1)


def sample_scores(c, HT, d, tabs, kcT, psS, psW, psM):
    nc = c.nc
    PG = 8
    with ExitStack() as ctx:
        sem = lambda n: nc.alloc_semaphore(f"ss_{n}")
        sb = lambda n, s: ctx.enter_context(nc.sbuf_tensor(f"ss_{n}", s, F32))
        oh = sb("onehot", [N_BUCKETS + 1, PAST + WIN + NBLK + 1])
        wk = sb("win_k", [P, NB, GP, WIN])
        kb = sb("k_pages", [P, 2, PG, GP * P])
        qz = sb("q_padded", [P, NB * 272])
        loaded, wk_in, patched, out_done, cleared, q_in = [sem(n) for n in
            ("loaded", "win_in", "win_patched", "win_out", "cleared", "q_in")]
        k_in = [sem(f"pages{s}_in") for s in range(2)]
        k_used = [sem(f"pages{s}_used") for s in range(2)]
        block = ctx.enter_context(nc.Block())
        q_of = lambda b, g: qz[:, (b * GP + g) * P:(b * GP + g + 1) * P]

        @block.sync
        def _(sp):
            sp.dma_start(oh[:, :], d["onehot_sample"]).then_inc(loaded, 16)
            sp.dma_start(wk[:, :, :, :], d["win_k"]).then_inc(wk_in, 16)
            for n in range(NB * PAGES // PG):
                s = n % 2
                if n >= 2:
                    sp.wait_ge(k_used[s], n // 2)
                with sp.Fori(0, PG) as i:
                    page = sp.value_load(c.pages[0:1, bass.ds(i + n * PG, 1)], min_val=0, max_val=POOL - 1)
                    sp.dma_start(kb[:, s, bass.ds(i, 1), :].rearrange("p o n -> p (o n)"),
                                 d["slc_k"][bass.ds(page, 1)].rearrange("o p n -> p (o n)")).then_inc(k_in[s], 16)
            sp.wait_ge(patched, 1)
            sp.dma_start(d["win_k_out"], wk[:, :, :, :]).then_inc(out_done, 16)
            sp.wait_ge(out_done, 16)

        @block.gpsimd
        def _(pool):
            pool.memset(qz[:, :], 0.0).then_inc(cleared, 1)

        @block.vector
        def _(dve):
            dve.wait_ge(wk_in, 16)
            dve.tensor_copy(wk[:, :, :, WIN - 1], HT[:, WK_U:WK_U + 2, SEQ:T].rearrange("p g b -> p b g"))\
               .then_inc(patched, 1)
            dve.wait_ge(cleared, 1)
            v = qz[:, :].rearrange("p (b x) -> p b x", x=272)
            for g2 in range(2):
                rows = slice(g2 * HD, (g2 + 1) * HD)
                for g in range(GP):
                    at = g * 136 + g2
                    dve.tensor_copy(v[rows, :, at:at + 7:2], HT[rows, g * REP:(g + 1) * REP, SEQ:T]
                                    .rearrange("p r b -> p b r")).then_inc(q_in, 1)

        @block.tensor
        def _(pe):
            pe.wait_ge(loaded, 16)
            tab = tabs[:, 16:16 + P]
            for j in range(4):
                pe.matmul(psS[:, j, :], tab, oh[:, j * 512:(j + 1) * 512], start=True, stop=False, skip_group_check=True)
            pe.matmul(psW[:, :], tab, oh[:, PAST:PAST + WIN], start=True, stop=False, skip_group_check=True)
            pe.matmul(psM[:, 0:NBLK + 1], tab, oh[:, PAST + WIN:], start=True, stop=False, skip_group_check=True)
            pe.wait_ge(q_in, 4)
            pe.wait_ge(patched, 1)
            for b in range(NB):
                for g in range(GP):
                    last = b == NB - 1 and g == GP - 1
                    pe.matmul(psW[:, :], q_of(b, g), wk[:, b, g, :], start=False, stop=last, skip_group_check=True)
                    pe.matmul(psM[:, 0:NBLK], q_of(b, g),
                              kcT[:, b * PAGES * 4:(b + 1) * PAGES * 4].rearrange("p (n x) -> p n x", x=4)[:, :, 2 * g:2 * g + 2],
                              start=False, stop=last, skip_group_check=True)
                    pe.matmul(psM[:, NBLK:NBLK + 1], q_of(b, g), HT[:, SK_U + g, SEQ + b:SEQ + b + 1],
                              start=False, stop=last, skip_group_check=True)
            for n in range(NB * PAGES // PG):
                s, b = n % 2, n * PG // PAGES
                pe.wait_ge(k_in[s], 16 * PG * (n // 2 + 1))
                for j in range(PG // 4):
                    bank = (n * PG % PAGES) // 4 + j
                    for g in range(GP):
                        mm = pe.matmul(psS[:, bank, :], q_of(b, g), kb[:, s, 4 * j:4 * j + 4, g * P:(g + 1) * P],
                                       start=False, stop=(b == NB - 1 and g == GP - 1), skip_group_check=True)
                mm.then_inc(k_used[s], 1)


def sample_softmax(c, d, Ps, psS, psW, psM, consts):
    nc = c.nc
    Pslc, Pwin, Pcmp, Pnew = Ps
    bmask, gsum = consts
    with ExitStack() as ctx:
        sem = lambda n: nc.alloc_semaphore(f"sx_{n}")
        sb = lambda n, s: ctx.enter_context(nc.sbuf_tensor(f"sx_{n}", s, F32))
        ps_i = ctx.enter_context(nc.psum_tensor("sx_ps", [P, 512], F32))
        g = sb("gates", [P, 3])
        nm = sb("neg_max", [P, 4])
        sm = sb("sums", [P, 4])
        new_e = sb("new_e", [P, 2])
        pc = sb("cmp", [P, NBLK])
        pcg = sb("cmp_gated", [P, NBLK])
        score = sb("score", [P, NBLK + 1])
        top = sb("top", [P, 8])
        drop = sb("drop", [P, NBLK + 1])
        g_in, own_done, shifted, expd, cmp_ready, summed = [sem(n) for n in
            ("gates_in", "chain", "max_ready", "exp", "cmp_ready", "group_sums")]
        block = ctx.enter_context(nc.Block())

        @block.sync
        def _(sp):
            with nc.allow_non_contiguous_dma(reason="384 numbers"):
                for b in range(NB):
                    sp.dma_start(g[b * HEADS:(b + 1) * HEADS, :],
                                 d["gate_scratch"].rearrange("(r h) b -> b h r", r=3)[b]).then_inc(g_in, 16)

        @block.tensor
        def _(pe):
            pe.wait_ge(cmp_ready, 1)
            pe.matmul(ps_i[:, 0:NBLK], gsum[:, :], pc[:, :], start=True, stop=True).then_inc(summed, 1)

        @block.scalar
        def _(act):
            act.wait_ge(shifted, 1)
            act.activation(pc[:, :], psM[:, 0:NBLK], ACT.Exp, bias=nm[:, 0:1], accum_out=sm[:, 0:1]).then_inc(expd, 1)
            act.wait_ge(shifted, 2)
            act.activation(Pwin[:, :], psW[:, :], ACT.Exp, bias=nm[:, 1:2], accum_out=sm[:, 1:2]).then_inc(expd, 1)
            act.wait_ge(shifted, 3)
            act.activation(Pslc[:, :], Pslc[:, :], ACT.Exp, bias=nm[:, 2:3], accum_out=sm[:, 2:3]).then_inc(expd, 1)

        @block.vector
        def _(dve):
            own = Seq(dve, own_done)
            own.link(dve.tensor_reduce(nm[:, 0:1], psM[:, 0:NBLK], AX, ALU.max))
            dve.tensor_scalar(nm[:, 0:1], nm[:, 0:1], -1.0, None, ALU.mult).then_inc(shifted, 1)
            own.link(dve.tensor_reduce(nm[:, 1:2], psW[:, :], AX, ALU.max))
            dve.tensor_scalar(nm[:, 1:2], nm[:, 1:2], -1.0, None, ALU.mult).then_inc(shifted, 1)
            dve.wait_ge(expd, 1)
            own.link(dve.reciprocal(sm[:, 3:4], sm[:, 0:1]))
            dve.tensor_scalar(pc[:, :], pc[:, :], sm[:, 3:4], None, ALU.mult).then_inc(cmp_ready, 1)
            dve.wait_ge(g_in, 16 * NB)
            dve.wait_ge(cmp_ready, 1)
            own.link(dve.tensor_scalar(pcg[:, :], pc[:, :], g[:, 0:1], None, ALU.mult))
            for par in range(2):
                own(dve.tensor_tensor(Pcmp[:, par].rearrange("p (b n) -> p b n", b=NB),
                                      pcg[:, par:NBLK:2].unsqueeze(1).broadcast_to([P, NB, PAGES]),
                                      bmask[:, :].unsqueeze(2).broadcast_to([P, NB, PAGES]), ALU.mult))
            dve.wait_ge(summed, 1)
            own.link(dve.tensor_copy(score[:, 0:NBLK], ps_i[:, 0:NBLK]))
            own(dve.memset(score[:, 0:1], 1e4))
            own.link(dve.memset(score[:, NBLK - 1:NBLK + 1], 1e4))
            for r in range(2):
                own.link(dve.max(top[:, :], score[:, :]))
                own.link(dve.match_replace(score[:, :], top[:, :], score[:, :], NEG))
            own.link(dve.tensor_scalar(drop[:, :], score[:, :], FLOOR, NEG, ALU.is_gt, ALU.mult))
            own(dve.tensor_tensor(Pslc[:, 0:PAST].rearrange("p (n t) -> p n t", t=BLOCK),
                                  psS[:, :, :].rearrange("p a (n t) -> p (a n) t", t=BLOCK),
                                  drop[:, 0:NBLK].unsqueeze(2).broadcast_to([P, NBLK, BLOCK]), ALU.add))
            own.link(dve.tensor_tensor(Pslc[:, PAST:PAST + 1], psM[:, NBLK:NBLK + 1], drop[:, NBLK:NBLK + 1], ALU.add))
            own.link(dve.tensor_reduce(nm[:, 2:3], Pslc[:, :], AX, ALU.max))
            dve.tensor_scalar(nm[:, 2:3], nm[:, 2:3], -1.0, None, ALU.mult).then_inc(shifted, 1)
            dve.wait_ge(expd, 2)
            own.link(dve.reciprocal(sm[:, 1:2], sm[:, 1:2]))
            own.link(dve.tensor_tensor(sm[:, 1:2], sm[:, 1:2], g[:, 2:3], ALU.mult))
            own(dve.tensor_scalar(Pwin[:, :], Pwin[:, :], sm[:, 1:2], None, ALU.mult))
            dve.wait_ge(expd, 3)
            own.link(dve.reciprocal(sm[:, 2:3], sm[:, 2:3]))
            own.link(dve.tensor_tensor(sm[:, 2:3], sm[:, 2:3], g[:, 1:2], ALU.mult))
            own(dve.tensor_scalar(Pslc[:, :], Pslc[:, :], sm[:, 2:3], None, ALU.mult))


def sample_values(c, d, Ps, vcS, Vnew):
    nc = c.nc
    Pslc, Pwin, Pcmp, _ = Ps
    PG = 8
    turns = [Pslc[:, j * P:(j + 1) * P] for j in range(16)] + [Pwin[:, j * P:(j + 1) * P] for j in range(4)] + \
            [Pcmp[:, par, :] for par in range(2)]
    with ExitStack() as ctx:
        sem = lambda n: nc.alloc_semaphore(f"sv_{n}")
        sb = lambda n, s: ctx.enter_context(nc.sbuf_tensor(f"sv_{n}", s, F32))
        PT = sb("probsT", [P, len(turns), P])
        PTn = sb("probsT_new", [1, P])
        Vn = sb("v_new", [1, NB, 2 * P])
        wv = sb("win_v", [P, NB, 4, 2 * P])
        vb = sb("v_pages", [P, 2, PG, 2 * P])
        ps_t = [ctx.enter_context(nc.psum_tensor(f"sv_t{j}", [P, 512], F32)) for j in range(2)]
        po = ctx.enter_context(nc.psum_tensor("sv_o", [P, P], F32))
        vn_in, wv_in, patched, out_done, turned, moved, mixed, picked = [sem(n) for n in
            ("v_new_in", "win_in", "win_patched", "win_out", "turned", "moved", "mixed", "picked")]
        v_in = [sem(f"pages{s}_in") for s in range(2)]
        v_used = [sem(f"pages{s}_used") for s in range(2)]
        block = ctx.enter_context(nc.Block())
        rounds = (len(turns) + 4) // 4

        @block.sync
        def _(sp):
            sp.dma_start(wv[:, :, :, :], d["win_v"]).then_inc(wv_in, 16)
            for b in range(NB):
                sp.dma_start(Vn[0:1, b, :], Vnew[b:b + 1, 0:2 * P]).then_inc(vn_in, 16)
            sp.wait_ge(wv_in, 16)
            for b in range(NB):
                sp.dma_start(wv[P - 1:P, b, 3, :], Vnew[b:b + 1, 2 * P:4 * P]).then_inc(patched, 16)
            for n in range(NB * PAGES // PG):
                s = n % 2
                if n >= 2:
                    sp.wait_ge(v_used[s], n // 2)
                with sp.Fori(0, PG) as i:
                    page = sp.value_load(c.pages[0:1, bass.ds(i + n * PG, 1)], min_val=0, max_val=POOL - 1)
                    sp.dma_start(vb[:, s, bass.ds(i, 1), :].rearrange("p o n -> p (o n)"),
                                 d["slc_v"][bass.ds(page, 1)].rearrange("o p n -> p (o n)")).then_inc(v_in[s], 16)
            sp.wait_ge(patched, 16 * NB)
            sp.dma_start(d["win_v_out"], wv[:, :, :, :]).then_inc(out_done, 16)
            sp.wait_ge(out_done, 16)

        @block.tensor
        def _(pe):
            for r in range(rounds):
                if r >= 2:
                    pe.wait_ge(moved, r - 1)
                for j in range(r * 4, min(r * 4 + 4, len(turns))):
                    mm = pe.transpose(ps_t[r % 2][:, (j % 4) * P:(j % 4 + 1) * P], turns[j], c.ident[:, :])
                if r == rounds - 1:
                    j = len(turns)
                    mm = pe.transpose(ps_t[r % 2][0:1, (j % 4) * P:(j % 4 + 1) * P], Pslc[:, PAST:PAST + 1], c.ident[:, :])
                mm.then_inc(turned, 1)
            pe.wait_ge(moved, rounds + 1)
            cols = lambda ap, g: ap.rearrange("p (b n) -> p b n", b=NB)[:, :, g * 8:(g + 1) * 8]
            first = True
            for g in range(GP):
                for par in range(2):
                    pe.matmul(cols(po[:, :], g), vcS[:, (g * 2 + par) * P:(g * 2 + par + 1) * P],
                              cols(PT[:, 20 + par, :], g), start=first, stop=False, skip_group_check=True)
                    first = False
            pe.wait_ge(vn_in, 16 * NB)
            pe.wait_ge(patched, 16 * NB)
            for b in range(NB):
                for g in range(GP):
                    q = slice(b * HEADS + g * 8, b * HEADS + g * 8 + 8)
                    for j in range(4):
                        pe.matmul(po[:, q], wv[:, b, j, g * P:(g + 1) * P], PT[:, 16 + j, q], start=False, stop=False,
                                  skip_group_check=True)
                    pe.matmul(po[:, q], Vn[0:1, b, g * P:(g + 1) * P], PTn[0:1, q], start=False, stop=False,
                              skip_group_check=True)
            for n in range(NB * PAGES // PG):
                s, b = n % 2, n * PG // PAGES
                pe.wait_ge(v_in[s], 16 * PG * (n // 2 + 1))
                for j in range(PG):
                    tile = (n * PG) % PAGES + j
                    for g in range(GP):
                        q = slice(b * HEADS + g * 8, b * HEADS + g * 8 + 8)
                        mm = pe.matmul(po[:, q], vb[:, s, j, g * P:(g + 1) * P], PT[:, tile, q], start=False,
                                       stop=(n == NB * PAGES // PG - 1 and j == PG - 1), skip_group_check=True)
                mm.then_inc(v_used[s], 1)

        @block.vector
        def _(dve):
            for r in range(rounds):
                dve.wait_ge(turned, r + 1)
                k = min(4, len(turns) - r * 4)
                dve.tensor_copy(PT[:, r * 4:r * 4 + k, :], ps_t[r % 2][:, 0:k * P].rearrange("p (k n) -> p k n", n=P))\
                   .then_inc(moved, 1)
                if r == rounds - 1:
                    j = len(turns) % 4
                    dve.tensor_copy(PTn[0:1, :], ps_t[r % 2][0:1, j * P:(j + 1) * P]).then_inc(moved, 1)
            n = NB * PAGES // PG
            dve.wait_ge(v_used[(n - 1) % 2], n // 2)
            for g2 in range(2):
                rows = slice(g2 * HD, (g2 + 1) * HD)
                dve.tensor_copy(c.XW[rows, :, SEQ:T],
                                po[rows, :].rearrange("p (b c g) -> p c b g", c=8, g=2)[:, :, :, g2]).then_inc(picked, 1)


def hgrn_gates(c, HT, d, K, L):
    nc = c.nc
    with ExitStack() as ctx:
        sem = lambda n: nc.alloc_semaphore(f"hg_{n}")
        sb = lambda n, s: ctx.enter_context(nc.sbuf_tensor(f"hg_{n}", s, F32))
        lg = sb("logits", [P, 2, HH])
        mx = sb("max", [P, HH])
        lb = sb("lb", [P, HH])
        om = sb("one_minus_lb", [P, HH])
        loaded, shifted, expd, sig, own_done, f_done, ln_done = [sem(n) for n in
            ("loaded", "shifted", "exp", "sigmoids", "chain", "f", "logs")]
        block = ctx.enter_context(nc.Block())

        @block.sync
        def _(sp):
            sp.dma_start(lg[:, :, :], d["lb_logits"]).then_inc(loaded, 16)

        @block.scalar
        def _(act):
            act.activation(HT[:, 8:16, :], HT[:, 8:16, :], ACT.Sigmoid).then_inc(sig, 1)
            act.activation(HT[:, 24:32, :], HT[:, 24:32, :], ACT.Sigmoid).then_inc(sig, 1)
            act.activation(HT[:, 0:8, :], HT[:, 0:8, :], ACT.Silu).then_inc(sig, 1)
            act.wait_ge(shifted, 1)
            act.activation(lg[:, :, :], lg[:, :, :], ACT.Exp).then_inc(expd, 1)
            act.wait_ge(f_done, HH)
            act.activation(L[:, :, :], HT[:, 8:16, :], ACT.Ln).then_inc(ln_done, 1)

        @block.vector
        def _(dve):
            own = Seq(dve, own_done)
            dve.wait_ge(loaded, 16)
            own.link(dve.tensor_tensor(mx[:, :], lg[:, 0, :], lg[:, 1, :], ALU.max))
            dve.tensor_tensor(lg[:, :, :], lg[:, :, :], mx[:, :].unsqueeze(1).broadcast_to([P, 2, HH]),
                              ALU.subtract).then_inc(shifted, 1)
            dve.wait_ge(expd, 1)
            own.link(dve.tensor_tensor(mx[:, :], lg[:, 0, :], lg[:, 1, :], ALU.add))
            own.link(dve.reciprocal(mx[:, :], mx[:, :]))
            own.link(dve.tensor_tensor(lg[:, :, :], lg[:, :, :], mx[:, :].unsqueeze(1).broadcast_to([P, 2, HH]), ALU.mult))
            own.link(dve.tensor_tensor(lb[:, :], lg[:, 0, :], lg[:, 1, :], ALU.add))
            own.link(dve.tensor_tensor(lb[:, :], lb[:, :], lg[:, 0, :], ALU.subtract))
            own.link(dve.tensor_scalar(om[:, :], lb[:, :], -1.0, 1.0, ALU.mult, ALU.add))
            dve.wait_ge(sig, 1)
            for h in range(HH):
                dve.tensor_scalar(HT[:, 8 + h, :], HT[:, 8 + h, :], om[:, h:h + 1], lb[:, h:h + 1], ALU.mult, ALU.add)\
                   .then_inc(f_done, 1)
            dve.wait_ge(f_done, HH)
            own(dve.tensor_scalar(K[:, :, :], HT[:, 8:16, :], -1.0, 1.0, ALU.mult, ALU.add))


def hgrn_prompt(c, HT, d, K, L):
    nc = c.nc
    fine = [16, 8, 4, 2, 1, 0]
    with ExitStack() as ctx:
        sem = lambda n: nc.alloc_semaphore(f"hp_{n}")
        sb = lambda n, s, t=F32: ctx.enter_context(nc.sbuf_tensor(f"hp_{n}", s, t))
        q, k, v, G = [sb(n, [P, SEQ]) for n in ("q", "k", "v", "G")]
        reset = sb("reset", [P, SEQ])
        Dl = [sb(f"diff{j}", [P, SEQ]) for j in range(2)]
        M = {m: sb(f"m{m}", [P, SEQ]) for m in LEVELS + [1]}
        eG, ke = sb("eG", [P, SEQ]), sb("ke", [P, SEQ])
        qe = sb("qe", [P, SEQ])
        vt, kt = sb("v_tok", [P, SEQ]), sb("ke_tok", [P, SEQ])
        A = sb("A", [P, SEQ])
        masks = sb("masks", [P, len(fine), P], I32)
        S = [sb(f"S{j}", [P, P]) for j in range(2)]
        Sout = sb("S_out", [P, HH, P])
        ps_a = ctx.enter_context(nc.psum_tensor("hp_a", [P, 512], F32))
        ps_f = [ctx.enter_context(nc.psum_tensor(f"hp_f{j}", [P, 512], F32)) for j in range(2)]
        ps_t = [ctx.enter_context(nc.psum_tensor(f"hp_t{j}", [P, 512], F32)) for j in range(2)]
        ps_o = ctx.enter_context(nc.psum_tensor("hp_o", [P, 512], F32))
        ps_s = ctx.enter_context(nc.psum_tensor("hp_s", [P, 512], F32))
        const_in, cleared, staged, own_done, diff, expd, mult, turned, turned_out, coarse, coarse_out, fine_done, \
            fine_out, s_new, s_out, o_done, o_out, saved = [sem(n) for n in
            ("const_in", "cleared", "staged", "chain", "diffs", "exps", "products", "turned", "turned_out", "coarse",
             "coarse_out", "fine", "fine_out", "state_products", "states", "outputs", "outputs_out", "saved")]
        block = ctx.enter_context(nc.Block())
        waited = sem("waited")
        tiles = lambda a: a.rearrange("p (i t) -> p i t", i=TILES)
        NL = len(LEVELS)
        NE = NL + 2

        @block.sync
        def _(sp):
            sp.dma_start(masks[:, :, :], d["level_masks"]).then_inc(const_in, 16)
            sp.dma_start(reset[:, :], d["tile_reset"]).then_inc(const_in, 16)
            sp.wait_ge(s_out, HH * TILES)
            sp.dma_start(d["hgrn_p_out"], Sout[:, :, :]).then_inc(saved, 16)
            sp.wait_ge(saved, 16)

        @block.gpsimd
        def _(pool):
            pool.memset(A[:, :], 0.0).then_inc(cleared, 1)
            pool.sem_inc(o_out, 1)
            with pool.Fori(0, HH) as h:
                pool.wait_ge(o_out, h + 1)
                own = Seq(pool, staged, h * 3)
                for dst, src, at in ((q, HT, 0), (k, K, 0), (v, HT, 16)):
                    own.link(pool.tensor_copy(dst[:, :], src[:, bass.ds(h + at, 1), 0:SEQ].rearrange("p o t -> p (o t)")))

        def halves(a, m):
            b = a.rearrange("p (n two m) -> p n two m", two=2, m=m)
            return b[:, :, 0, :], b[:, :, 1, :]

        @block.vector
        def _(dve):
            dve.wait_ge(const_in, 32)
            with dve.Fori(0, HH) as h:
                own = Seq(dve, own_done, h * 1)
                dve.wait_ge(o_out, h + 1)
                own.link(dve.tensor_tensor_scan(G[:, :], reset[:, :], L[:, bass.ds(h, 1), 0:SEQ]
                                                .rearrange("p o t -> p (o t)"), 0.0, ALU.mult, ALU.add))
                dve.wait_ge(staged, h * 3 + 3)

                def diffs(n):
                    dl = Dl[n % 2]
                    if n < NL:
                        m = LEVELS[n]
                        g0, g1 = halves(G[:, :], m)
                        d0, d1 = halves(dl[:, :], m)
                        ref = g0[:, :, m - 1:m].broadcast_to([P, SEQ // (2 * m), m])
                        dve.tensor_tensor(d0, ref, g0, ALU.subtract).then_inc(diff, 1)
                        dve.tensor_tensor(d1, g1, ref, ALU.subtract).then_inc(diff, 1)
                    else:
                        end = tiles(G[:, :])[:, :, P - 1:P].broadcast_to([P, TILES, P])
                        dve.tensor_tensor(tiles(dl[:, :]), end, tiles(G[:, :]), ALU.subtract).then_inc(diff, 1)

                def mults(n):
                    dl = Dl[n % 2]
                    dve.wait_ge(expd, h * NE + (n + 1))
                    if n < NL:
                        m = LEVELS[n]
                        d0, d1 = halves(dl[:, :], m)
                        m0, m1 = halves(M[m][:, :], m)
                        dve.tensor_tensor(m0, d0, halves(k[:, :], m)[0], ALU.mult).then_inc(mult, 1)
                        dve.tensor_tensor(m1, d1, halves(q[:, :], m)[1], ALU.mult).then_inc(mult, 1)
                    else:
                        dve.tensor_tensor(ke[:, :], dl[:, :], k[:, :], ALU.mult).then_inc(mult, 1)

                diffs(0)
                for n in range(NL + 1):
                    if n + 1 <= NL:
                        if n + 1 >= 2:
                            dve.wait_ge(mult, h * (2 * NL + 4) + 2 * n)
                        diffs(n + 1)
                    mults(n)
                m0, m1 = halves(M[1][:, :], 1)
                dve.tensor_copy(m0, halves(k[:, :], 1)[0]).then_inc(mult, 1)
                dve.tensor_tensor(m1, halves(q[:, :], 1)[1],
                                  HT[:, bass.ds(h + 8, 1), 1:SEQ:2].rearrange("p o t -> p (o t)").unsqueeze(2),
                                  ALU.mult).then_inc(mult, 1)
                dve.wait_ge(expd, h * NE + NE)
                dve.tensor_tensor(qe[:, :], eG[:, :], q[:, :], ALU.mult).then_inc(mult, 1)
                dve.wait_ge(turned, h * 2 + 1)
                dve.tensor_copy(vt[:, :], ps_t[0][:, :]).then_inc(turned_out, 1)
                for n in range(len(fine)):
                    dve.wait_ge(cleared, 1)
                    dve.wait_ge(fine_done, h * len(fine) + (n + 1))
                    if n == 0:
                        dve.wait_ge(coarse_out, h * 3 + 3)
                    if n:
                        dve.wait_ge(fine_out, h * len(fine) + n)
                    dve.sem_inc(waited, 1)
                    dve.copy_predicated(tiles(A[:, :]), masks[:, n, :].unsqueeze(1).broadcast_to([P, TILES, P]),
                                        tiles(ps_f[n % 2][:, :])).then_inc(fine_out, 1)
                dve.wait_ge(turned, h * 2 + 2)
                dve.tensor_copy(kt[:, :], ps_t[1][:, :]).then_inc(turned_out, 1)
                for i in range(TILES):
                    dve.wait_ge(s_new, h * TILES + (i + 1))
                    dst = S[(i + 1) % 2][:, :] if i < TILES - 1 else Sout[:, bass.ds(h, 1), :].rearrange("p o n -> p (o n)")
                    if i == 0:
                        dve.tensor_copy(dst, ps_s[:, 0:P]).then_inc(s_out, 1)
                    else:
                        dve.wait_ge(s_out, h * TILES + i)
                        dve.scalar_tensor_tensor(dst, S[i % 2][:, :], eG[:, (i + 1) * P - 1:(i + 1) * P],
                                                 ps_s[:, 0:P], ALU.mult, ALU.add).then_inc(s_out, 1)

        @block.scalar
        def _(act):
            with act.Fori(0, HH) as h:
                for n in range(NL + 1):
                    act.wait_ge(diff, h * (2 * NL + 1) + (2 * (n + 1) if n < NL else 2 * NL + 1))
                    act.activation(Dl[n % 2][:, :], Dl[n % 2][:, :], ACT.Exp).then_inc(expd, 1)
                act.activation(eG[:, :], G[:, :], ACT.Exp).then_inc(expd, 1)
                act.wait_ge(coarse, h + 1)
                act.wait_ge(cleared, 1)
                A4, a4 = tiles(A[:, :]), tiles(ps_a[:, :])
                for r0, r1, t0, t1 in ((0, 64, 64, 128), (0, 32, 32, 64), (64, 96, 96, 128)):
                    act.activation(A4[r0:r1, :, t0:t1], a4[r0:r1, :, t0:t1], ACT.Copy).then_inc(coarse_out, 1)
                act.wait_ge(o_done, h + 1)
                act.activation(c.XW[:, bass.ds(h, 1), 0:SEQ].rearrange("p o t -> p (o t)"), ps_o[:, :], ACT.Copy)\
                   .then_inc(o_out, 1)

        @block.tensor
        def _(pe):
            with pe.Fori(0, HH) as h:
                pe.wait_ge(staged, h * 3 + 3)
                for i in range(TILES):
                    mm = pe.transpose(ps_t[0][:, i * P:(i + 1) * P], v[:, i * P:(i + 1) * P], c.ident[:, :])
                mm.then_inc(turned, 1)
                base = h * (2 * NL + 4)
                for n, m in enumerate((64, 32)):
                    pe.wait_ge(mult, base + 2 * (n + 1))
                    for i in range(TILES):
                        for b in range(P // (2 * m)):
                            s0 = b * 2 * m
                            mm = pe.matmul(ps_a[s0:s0 + m, i * P + s0 + m:i * P + s0 + 2 * m],
                                           M[m][:, i * P + s0:i * P + s0 + m],
                                           M[m][:, i * P + s0 + m:i * P + s0 + 2 * m], start=True, stop=True)
                mm.then_inc(coarse, 1)
                for n, m in enumerate(fine):
                    pe.wait_ge(mult, base + (2 * (n + 3) if m > 1 else 2 * NL + 3))
                    if n >= 2:
                        pe.wait_ge(fine_out, h * len(fine) + (n - 1))
                    a, b = (M[m], M[m]) if m else (k, q)
                    for i in range(TILES):
                        mm = pe.matmul(ps_f[n % 2][:, i * P:(i + 1) * P], a[:, i * P:(i + 1) * P],
                                       b[:, i * P:(i + 1) * P], start=True, stop=True)
                    mm.then_inc(fine_done, 1)
                for i in range(TILES):
                    mm = pe.transpose(ps_t[1][:, i * P:(i + 1) * P], ke[:, i * P:(i + 1) * P], c.ident[:, :])
                mm.then_inc(turned, 1)
                pe.wait_ge(mult, base + 2 * NL + 4)
                pe.wait_ge(turned_out, h * 2 + 2)
                pe.wait_ge(fine_out, h * len(fine) + len(fine))
                pe.wait_ge(coarse_out, h * 3 + 3)
                for i in range(TILES):
                    t = slice(i * P, (i + 1) * P)
                    if i:
                        pe.wait_ge(s_out, h * TILES + i)
                    pe.matmul(ps_s[:, 0:P], kt[:, t], vt[:, t], start=True, stop=True).then_inc(s_new, 1)
                    mm = pe.matmul(ps_o[:, t], vt[:, t], A[:, t], start=True, stop=i == 0)
                    if i:
                        mm = pe.matmul(ps_o[:, t], S[i % 2][:, :], qe[:, t], start=False, stop=True)
                mm.then_inc(o_done, 1)


def hgrn_sample(c, HT, d, K):
    nc = c.nc
    with ExitStack() as ctx:
        sem = lambda n: nc.alloc_semaphore(f"hs_{n}")
        sb = lambda n, s: ctx.enter_context(nc.sbuf_tensor(f"hs_{n}", s, F32))
        S0 = sb("state", [P, NB, HH, P])
        rows = sb("rows", [NB, 2, HH, P])
        vm = sb("v_masked", [NB, 2, NB, P])
        eye = sb("eye", [NB, NB])
        ps_t = ctx.enter_context(nc.psum_tensor("hs_t", [NB, 2, HH, P], F32))
        ps_k = ctx.enter_context(nc.psum_tensor("hs_k", [P, NB, P], F32))
        ps_o = ctx.enter_context(nc.psum_tensor("hs_o", [P, HH, NB], F32))
        loaded, turned, own_done, masked, outer, stepped, mixed, picked, saved = [sem(n) for n in
            ("loaded", "turned", "chain", "v_masked", "outer", "stepped", "mixed", "picked", "saved")]
        block = ctx.enter_context(nc.Block())

        @block.sync
        def _(sp):
            sp.dma_start(S0[:, :, :, :], d["state_hgrn"]).then_inc(loaded, 16)
            sp.wait_ge(stepped, HH)
            sp.dma_start(d["hgrn_s_out"], S0[:, :, :, :]).then_inc(saved, 16)
            sp.wait_ge(saved, 16)

        @block.tensor
        def _(pe):
            for h in range(HH):
                pe.transpose(ps_t[:, 0, h, :], K[:, h, SEQ:T], c.ident[:, :])
                mm = pe.transpose(ps_t[:, 1, h, :], HT[:, 16 + h, SEQ:T], c.ident[:, :])
            mm.then_inc(turned, 1)
            for h in range(HH):
                pe.wait_ge(masked, h + 1)
                if h:
                    pe.wait_ge(stepped, h)
                for j in range(2):
                    mm = pe.matmul(ps_k[:, 4 * j:4 * j + 4, :], rows[:, 0, h, :], vm[:, h % 2, 4 * j:4 * j + 4, :],
                                   start=True, stop=True)
                mm.then_inc(outer, 1)
            pe.wait_ge(stepped, HH)
            for h in range(HH):
                for b in range(NB):
                    mm = pe.matmul(ps_o[:, h, b:b + 1], S0[:, b, h, :], HT[:, h, SEQ + b:SEQ + b + 1], start=True, stop=True)
            mm.then_inc(mixed, 1)

        @block.vector
        def _(dve):
            own = Seq(dve, own_done)
            dve.wait_ge(turned, 1)
            own.link(dve.tensor_copy(rows[:, :, :, :], ps_t[:, :, :, :]))
            dve.wait_ge(loaded, 16)
            for h in range(HH):
                if h >= 2:
                    dve.wait_ge(outer, h - 1)
                dve.tensor_tensor(vm[:, h % 2], rows[:, 1, h, :].unsqueeze(1).broadcast_to([NB, NB, P]),
                                  c.ident[0:NB, 0:NB].unsqueeze(2).broadcast_to([NB, NB, P]), ALU.mult).then_inc(masked, 1)
                own.link(dve.tensor_tensor(S0[:, :, h, :], S0[:, :, h, :],
                                           HT[:, 8 + h, SEQ:T].unsqueeze(2).broadcast_to([P, NB, P]), ALU.mult))
                dve.wait_ge(outer, h + 1)
                dve.tensor_tensor(S0[:, :, h, :], S0[:, :, h, :], ps_k[:, :, :], ALU.add).then_inc(stepped, 1)
            dve.wait_ge(mixed, 1)
            dve.tensor_copy(c.XW[:, :, SEQ:T], ps_o[:, :, :]).then_inc(picked, 1)


def hgrn_norm(c, HT, sq, R, onw):
    nc = c.nc
    with ExitStack() as ctx:
        sem = lambda n: nc.alloc_semaphore(f"hn_{n}")
        ps = [ctx.enter_context(nc.psum_tensor(f"hn_ps{j}", [P, 2, 512], F32)) for j in range(2)]
        squared, summed, mean_in, rooted, own_done = [sem(n) for n in ("squares", "sums", "means", "roots", "chain")]
        block = ctx.enter_context(nc.Block())

        @block.tensor
        def _(pe):
            for h in range(HH):
                pe.wait_ge(squared, h + 1)
                if h >= 2:
                    pe.wait_ge(mean_in, h - 1)
                for x in range(2):
                    mm = pe.matmul(ps[h % 2][:, x, 0:TH], c.ones[:, :], sq[:, h, x * TH:(x + 1) * TH], start=True, stop=True)
                mm.then_inc(summed, 1)

        @block.scalar
        def _(act):
            for h in range(HH):
                act.activation(sq[:, h, :], c.XW[:, h, :], ACT.Square).then_inc(squared, 1)
            for h in range(HH):
                act.wait_ge(mean_in, h + 1)
                act.activation(R[:, h, :], R[:, h, :], ACT.Sqrt).then_inc(rooted, 1)

        @block.vector
        def _(dve):
            own = Seq(dve, own_done)
            for h in range(HH):
                dve.wait_ge(summed, h + 1)
                dve.tensor_scalar(pairs(R[:, h, :]), ps[h % 2][:, :, 0:TH], 1.0 / P, EPS, ALU.mult, ALU.add)\
                   .then_inc(mean_in, 1)
            for h in range(HH):
                dve.wait_ge(rooted, h + 1)
                own.link(dve.reciprocal(R[:, h, :], R[:, h, :]))
                own.link(dve.scalar_tensor_tensor(c.XW[:, h, :], c.XW[:, h, :], onw[:, 0:1], R[:, h, :], ALU.mult, ALU.mult))
                own(dve.tensor_tensor(c.XW[:, h, :], c.XW[:, h, :], HT[:, 24 + h, :], ALU.mult))


def program(nc, d):
    with ExitStack() as top:
        c = Core(nc, top)
        c.pages = top.enter_context(nc.sbuf_tensor("pages", [1, NB * PAGES], I32))
        onw = top.enter_context(nc.sbuf_tensor("hgrn_norm_w", [P, 1], F32))
        loaded = top.enter_context(nc.semaphore("setup_loaded"))
        with nc.Block() as block:
            @block.sync
            def _(sp):
                for dst, src in ((c.X[:, :, :], "x"), (c.nw[:, :, :, :], "norm_w"), (c.ident[:, :], "ident"),
                                 (c.pages[:, :], "page_table"), (onw[:, :], "hgrn_norm_w")):
                    sp.dma_start(dst, d[src]).then_inc(loaded, 16)
                for s in range(RING):
                    load_tile(sp, c, d["nsa_w_in"], s, s, KC)
                sp.wait_ge(loaded, 80)

            @block.gpsimd
            def _(pool):
                pool.memset(c.ones[:, :], 1.0)
                for s in range(RING):
                    pool.sem_inc(c.psum_free[s], 1)
        c.loads = [1] * RING

        def swiglu(layer, nxt):
            with ExitStack() as ctx:
                sb = lambda n, s: ctx.enter_context(nc.sbuf_tensor(f"ffn{layer}_{n}", s, F32))
                H = sb("h", [P, FF, T])
                sems = [[nc.alloc_semaphore(f"ffn{layer}_{n}{m}") for m in range(2)]
                        for n in ("a_in", "a_silu", "g_in", "product")]
                with ExitStack() as inner:
                    a_t = inner.enter_context(nc.sbuf_tensor(f"ffn{layer}_a", [P, 2, T], F32))
                    g_t = inner.enter_context(nc.sbuf_tensor(f"ffn{layer}_g", [P, 2, T], F32))
                    linear(c, f"gu{layer}", d[f"w_gu{layer}"], 2 * FF, 1, KC, c.XW, evac_swiglu(c, H, a_t, g_t, sems),
                           (d[f"w_down{layer}"], SUBK))
                mixed_and_normed(f"down{layer}", d[f"w_down{layer}"], 2, SUBK, H, nxt,
                                 c.nw[:, layer, 3], c.nw[:, 1, 0] if layer == 0 else None)

        def mixed_and_normed(name, w, subs, kcs, src, nxt, w_post, w_pre):
            with ExitStack() as ctx:
                Y = ctx.enter_context(nc.sbuf_tensor(f"{name}_y", [P, KC, T], F32))
                ssq = ctx.enter_context(nc.sbuf_tensor(f"{name}_ssq", [P, T], F32))
                sq = ctx.enter_context(nc.sbuf_tensor(f"{name}_sq", [P, T], F32))
                sems = [nc.alloc_semaphore(f"{name}_{n}") for n in ("squared", "added")]
                linear(c, name, w, KC, subs, kcs, src, evac_squares(c, Y, sq, ssq, sems), nxt)
                norm_step(c, f"{name}_norm", ssq, sq, (Y, w_post), w_pre)

        with ExitStack() as ctx:
            ssq = ctx.enter_context(nc.sbuf_tensor("in_ssq", [P, T], F32))
            norm_step(c, "in_norm", ssq, None, None, c.nw[:, 0, 0])

        with ExitStack() as nsa:
            nsa.enter_context(nc.cleanup_on_exit())
            sb = lambda n, s: nsa.enter_context(nc.sbuf_tensor(n, s, F32))
            HT = sb("HT", [P, NSA_UNITS, T])
            linear(c, "nsa_in", d["nsa_w_in"], NSA_UNITS, 1, KC, c.XW, evac_scaled(c, HT, 48), (d["nsa_w_out"], KC), 48)
            kcT = sb("kcT", [P, NB * PAGES * 4])
            kcBD = sb("kcBD", [P, GP, 2, PBLK])
            vcS = sb("vcS", [P, 4 * P])
            Vnew = sb("Vnew", [NB, 4 * P])
            tabs = sb("tabs", [N_BUCKETS + 1, 16 + P])
            with ExitStack() as pr:
                sp_ = lambda n, s: pr.enter_context(nc.sbuf_tensor(n, s, F32))
                BDv = sp_("BDv", [P, 8, 2, HD])
                compress(c, HT, d, kcT, kcBD, vcS, BDv)
                Otok = sp_("Otok", [P, TILES, D_MODEL])
                Vtok = sp_("Vtok", [P, TILES, 4 * P])
                gT = sp_("gT", [P, TILES, 48])
                T_bias = sp_("T_bias", [P, HEADS, SEQ])
                with ExitStack() as bc:
                    biasC = bc.enter_context(nc.sbuf_tensor("biasC", [P, TILES, HEADS, PBLK], F32))
                    attention_setup(c, HT, d, tabs, T_bias, biasC, Vtok, gT, Vnew)
                    prompt_compressed(c, HT, kcBD, BDv, biasC, gT, Otok)
                prompt_attention(c, HT, T_bias, Vtok, gT, Otok)
                turn_outputs(c, Otok)
            with ExitStack() as sa:
                ss = lambda n, s: sa.enter_context(nc.sbuf_tensor(n, s, F32))
                Ps = (ss("Pslc", [P, PAST + 1]), ss("Pwin", [P, WIN]), ss("Pcmp", [P, 2, P]), None)
                bmask, gsum = ss("bmask", [P, NB]), ss("gsum", [P, P])
                with ExitStack() as pp:
                    psS = pp.enter_context(nc.psum_tensor("psS", [P, 4, 512], F32))
                    psW = pp.enter_context(nc.psum_tensor("psW", [P, 512], F32))
                    psM = pp.enter_context(nc.psum_tensor("psM", [P, 512], F32))
                    cin = nc.alloc_semaphore("sample_consts")
                    with nc.Block() as block:
                        @block.sync
                        def _(sp):
                            sp.dma_start(bmask[:, :], d["batch_mask"]).then_inc(cin, 16)
                            sp.dma_start(gsum[:, :], d["group_sum"]).then_inc(cin, 16)
                            sp.wait_ge(cin, 32)
                    sample_scores(c, HT, d, tabs, kcT, psS, psW, psM)
                    sample_softmax(c, d, Ps, psS, psW, psM, (bmask, gsum))
                sample_values(c, d, Ps, vcS, Vnew)
        mixed_and_normed("nsa_out", d["nsa_w_out"], 1, KC, c.XW, (d["w_gu0"], KC), c.nw[:, 0, 1], c.nw[:, 0, 2])
        swiglu(0, (d["hgrn_w_in"], KC))
        with ExitStack() as hg:
            hg.enter_context(nc.cleanup_on_exit())
            sb = lambda n, s: hg.enter_context(nc.sbuf_tensor(n, s, F32))
            HT = sb("HT2", [P, HGRN_UNITS, T])
            linear(c, "hgrn_in", d["hgrn_w_in"], HGRN_UNITS, 1, KC, c.XW, evac_scaled(c, HT), (d["hgrn_w_out"], KC))
            K = sb("K", [P, HH, T])
            L = sb("L", [P, HH, T])
            hgrn_gates(c, HT, d, K, L)
            hgrn_prompt(c, HT, d, K, L)
            hgrn_sample(c, HT, d, K)
            hgrn_norm(c, HT, K, L, onw)
        mixed_and_normed("hgrn_out", d["hgrn_w_out"], 1, KC, c.XW, (d["w_gu1"], KC), c.nw[:, 1, 1], c.nw[:, 1, 2])
        swiglu(1, None)
        out_done = top.enter_context(nc.semaphore("y_out"))
        with nc.Block() as block:
            @block.sync
            def _(sp):
                sp.dma_start(d["y"], c.X[:, :, :]).then_inc(out_done, 16)
                sp.wait_ge(out_done, 16)



def bucket(n):
    n = np.asarray(n)
    m = N_BUCKETS // 2
    nf = np.maximum(n, 1).astype(np.float32)
    r = np.log(nf / np.float32(m)).astype(np.float32) / np.float32(np.log(MAX_DISTANCE / m))
    large = m + (r * np.float32(N_BUCKETS - m)).astype(np.int32)
    return np.where(n < 0, -1, np.where(n < m, n, np.minimum(large, N_BUCKETS - 1)))


def onehot(n):
    b = bucket(n)
    b = np.where(b < 0, N_BUCKETS, b)
    return (np.arange(N_BUCKETS + 1)[:, None] == b[None, :]).astype(np.float32)


def unit_tiles(w, subs, kcs):
    K, N = w.shape
    a = w.reshape(subs, kcs, P, N // P, P)
    return np.ascontiguousarray(a.transpose(3, 0, 2, 1, 4).reshape(N // P * subs, P, kcs * P))


def shape_constants():
    s = np.arange(P)
    out = {
        "ident": np.eye(P, dtype=np.float32),
        "onehot_rows": np.ascontiguousarray(np.stack([onehot(511 - np.arange(1024)), onehot(np.arange(1024) - 511)], 1)),
        "onehot_sample": np.concatenate([onehot(PAST - np.arange(PAST)), onehot(WIN - 1 - np.arange(WIN)),
                                         onehot(PAST - (BLOCK * np.arange(NBLK) + BLOCK - 1)), onehot([0])], 1),
        "head_mask": np.kron(np.eye(16, dtype=np.float32), np.ones((PBLK, 1), np.float32)),
        "batch_mask": np.kron(np.eye(NB, dtype=np.float32), np.ones((HEADS, 1), np.float32)),
        "tile_reset": np.ascontiguousarray(np.broadcast_to((np.arange(SEQ) % P != 0).astype(np.float32), (P, SEQ))),
    }
    h = np.arange(P)
    key = (h // HEADS) * 100 + (h % HEADS // 8) * 10 + h % 2
    out["group_sum"] = (key[:, None] == key[None, :]).astype(np.float32)
    masks = []
    for m in (16, 8, 4, 2, 1):
        masks.append((s[:, None] // (2 * m) == s[None, :] // (2 * m)) & (s[:, None] % (2 * m) < m)
                     & (s[None, :] % (2 * m) >= m))
    masks.append(s[:, None] == s[None, :])
    out["level_masks"] = np.ascontiguousarray(np.stack(masks, 1).astype(np.int32))
    return out


def kernel(x_prompt, x_sample, cache_cmp_kv, cache_slc_kv, state_win_kv, state_hgrn, page_table, norm_w, nsa_w_in,
           nsa_w_out, nsa_cmp_pe, nsa_cmp_w1, nsa_cmp_w2, rel_bias, hgrn_w_in, hgrn_w_out, hgrn_norm_w,
           hgrn_lb_logits, ffn_w_gu, ffn_w_down):
    import concourse.bacc as bacc
    from concourse.bass_utils import run_bass_kernel_spmd

    A = lambda a: np.asarray(a)
    C = np.ascontiguousarray
    a = shape_constants()
    x = np.concatenate([A(x_prompt)[0], A(x_sample)[:, 0]], 0)
    a["x"] = C(x.T.reshape(KC, P, T).transpose(1, 0, 2))
    a["norm_w"] = C(A(norm_w).reshape(2, 4, KC, P).transpose(3, 0, 1, 2))
    a["page_table"] = A(page_table).reshape(1, NB * PAGES)
    a["hgrn_norm_w"] = C(A(hgrn_norm_w)[0].reshape(P, 1))
    w = A(nsa_w_in)[0]
    nq, nkv = HEADS * HD, 6 * KVH * HD
    wq = w[:, :nq].reshape(D_MODEL, GP, 2, REP, HD).transpose(0, 1, 3, 2, 4).reshape(D_MODEL, nq)
    wg = w[:, nq + nkv:].reshape(D_MODEL, 3, GP, 2, REP).transpose(0, 1, 2, 4, 3).reshape(D_MODEL, 48)
    w = np.concatenate([wq, w[:, nq:nq + nkv], wg, np.zeros((D_MODEL, 80), np.float32)], 1)
    a["nsa_w_in"] = unit_tiles(w, 1, KC)
    wo = A(nsa_w_out)[0].reshape(GP, 2, REP, HD, D_MODEL).transpose(0, 2, 1, 3, 4).reshape(nq, D_MODEL)
    a["nsa_w_out"] = unit_tiles(wo, 1, KC)
    a["hgrn_w_in"] = unit_tiles(A(hgrn_w_in)[0], 1, KC)
    a["hgrn_w_out"] = unit_tiles(A(hgrn_w_out)[0], 1, KC)
    for l in range(2):
        gu = A(ffn_w_gu)[l].reshape(D_MODEL, 2, FF, P).transpose(0, 2, 1, 3).reshape(D_MODEL, 2 * D_FF)
        a[f"w_gu{l}"] = unit_tiles(gu, 1, KC)
        a[f"w_down{l}"] = unit_tiles(A(ffn_w_down)[l], 2, SUBK)
    cc = A(cache_cmp_kv)[0].reshape(POOL, P, 2, GP, 2, HD)
    a["cache_cmp"] = C(cc.transpose(2, 0, 4, 5, 3, 1).reshape(2, POOL, P, GP * P))
    cs = A(cache_slc_kv)[0].reshape(POOL, P, 2, GP, 2, HD)
    a["slc_k"] = C(cs[:, :, 0].transpose(0, 3, 4, 2, 1).reshape(POOL, P, GP * P))
    a["slc_v"] = C(cs[:, :, 1].reshape(POOL, P, 2 * P))
    sw = np.roll(A(state_win_kv)[0], -1, axis=1)
    sw = sw.reshape(NB, WIN, 2, GP, 2, HD)
    a["win_k"] = C(sw[:, :, 0].transpose(3, 4, 0, 2, 1).reshape(P, NB, GP, WIN))
    a["win_v"] = C(sw[:, :, 1].reshape(NB, 4, P, 2 * P).transpose(2, 0, 1, 3))
    w1 = A(nsa_cmp_w1)[0].reshape(2, 2, 32, HD, HD)
    bd = np.zeros((2, 2, 2, HD, 32, 2, HD), np.float32)
    w2 = np.zeros((2, HD, 2, 2, HD), np.float32)
    for g in range(2):
        bd[:, :, g, :, :, g, :] = w1.transpose(0, 1, 3, 2, 4)
        w2[g, :, :, g, :] = A(nsa_cmp_w2)[0].transpose(1, 0, 2)
    a["cmp_w1"] = bd.reshape(2, 2, P, 32 * P)
    a["cmp_w2"] = w2.reshape(P, 2, P)
    pe = A(nsa_cmp_pe)[0].transpose(2, 0, 1)
    a["cmp_pe"] = C(np.concatenate([pe, pe], 0))
    tab = np.concatenate([A(rel_bias).reshape(N_BUCKETS, GP, 2, REP).transpose(0, 1, 3, 2).reshape(N_BUCKETS, 16),
                          np.full((1, 16), NEG, np.float32)], 0)
    a["tabs"] = C(np.concatenate([tab] * (NB + 1), 1))
    a["lb_logits"] = C(A(hgrn_lb_logits).reshape(2, HH, P).transpose(2, 0, 1))
    a["state_hgrn"] = C(A(state_hgrn)[0].transpose(2, 0, 1, 3))

    nc = bacc.Bacc("TRN2", target_bir_lowering=False, num_devices=1)
    d = {n: nc.dram_tensor(f"in_{n}", v.shape, mybir.dt.from_np(v.dtype), kind="ExternalInput").ap()
         for n, v in a.items()}
    outs = {"y": (P, KC, T), "kv_out": (P, 12, T), "win_k_out": (P, NB, GP, WIN), "win_v_out": (P, NB, 4, 2 * P),
            "hgrn_p_out": (P, HH, P), "hgrn_s_out": (P, NB, HH, P)}
    for n, s in outs.items():
        d[n] = nc.dram_tensor(f"out_{n}", s, F32, kind="ExternalOutput").ap()
    d["gate_scratch"] = nc.dram_tensor("gate_scratch", (48, NB), F32, kind="Internal").ap()
    d["bias_skew"] = nc.dram_tensor("bias_skew", (P, HEADS, SKEW), F32, kind="Internal").ap()
    d["bias_scratch"] = nc.dram_tensor("bias_scratch", (16, 1024), F32, kind="Internal").ap()
    program(nc, d)
    r = run_bass_kernel_spmd(nc, [{f"in_{n}": v for n, v in a.items()}], core_ids=[0]).results[0]
    o = {n: np.asarray(r[f"out_{n}"]) for n in outs}
    y = o["y"].transpose(2, 1, 0).reshape(T, D_MODEL)
    kv = o["kv_out"].reshape(2, HD, 3, 2, GP, T).transpose(2, 5, 3, 4, 0, 1).reshape(3, T, 2, KVH, HD)
    wk = o["win_k_out"].reshape(2, HD, NB, GP, WIN).transpose(2, 4, 3, 0, 1).reshape(NB, WIN, KVH, HD)
    wv = o["win_v_out"].transpose(1, 2, 0, 3).reshape(NB, WIN, KVH, HD)
    return (C(y[None, :SEQ]), C(y[SEQ:, None]), C(kv[0][None, None, :SEQ]), C(kv[1][None, None, :SEQ]),
            C(kv[2][None, None, :SEQ]), C(o["hgrn_p_out"].transpose(1, 0, 2)[None, None]),
            C(kv[0][None, SEQ:, None]), C(kv[1][None, SEQ:, None]), C(np.stack([wk, wv], 2)[None]),
            C(o["hgrn_s_out"].transpose(1, 2, 0, 3)[None]))
```

```python
from contextlib import ExitStack

import numpy as np

import concourse.bass as bass
from concourse import mybir

F32 = mybir.dt.float32
F32R = mybir.dt.float32r
I32 = mybir.dt.int32
ALU = mybir.AluOpType
ACT = mybir.ActivationFunctionType
AX = mybir.AxisListType.X

P = 128
D_MODEL = 1024
KC = D_MODEL // P
SEQ = 512
NB = 8
T = SEQ + NB
TH = T // 2
TILES = SEQ // P
PAST = 2048
PAGES = PAST // P
POOL = 160
HEADS, KVH, HD = 16, 4, 64
GP = KVH // 2
REP = HEADS // KVH
BLOCK = 64
NBLK = PAST // BLOCK
PBLK = SEQ // BLOCK
WIN = 512
N_BUCKETS = 32
MAX_DISTANCE = 1024
D_FF = 2816
FF = D_FF // P
HH = 8
NSA_UNITS = 21
HGRN_UNITS = 32
EPS = 1e-6
NEG = -1e30
FLOOR = -1e20
Q_U, CK_U, CV_U, SK_U, SV_U, WK_U, WV_U, GATE_U = 0, 8, 10, 12, 14, 16, 18, 20
RING = 4
SUBK = 11
SKEW = SEQ + P
LEVELS = [64, 32, 16, 8, 4, 2]


class Seq:

    def __init__(self, eng, sem, base=0):
        self.eng, self.sem, self.base, self.n = eng, sem, base, 0

    def __call__(self, ins):
        ins.then_inc(self.sem, 1)
        self.n += 1
        return self.n

    def wait(self, n=None):
        self.eng.wait_ge(self.sem, self.base + (self.n if n is None else n))

    def link(self, ins):
        self(ins)
        self.wait()


class Core:

    def __init__(self, nc, ctx):
        self.nc = nc
        sb = lambda n, s, d=F32: ctx.enter_context(nc.sbuf_tensor(n, s, d))
        sem = lambda n: ctx.enter_context(nc.semaphore(n))
        self.X = sb("X", [P, KC, T])
        self.rstd = sb("rstd", [P, T])
        self.ring = sb("ring", [P, RING, SUBK * P])
        self.nw = sb("nw", [P, 2, 4, KC])
        self.ident = sb("ident", [P, P])
        self.ones = sb("ones", [P, P])
        self.loaded = [sem(f"weights_loaded{s}") for s in range(RING)]
        self.hi_cut = [sem(f"high_part_cut{s}") for s in range(RING)]
        self.lo_cut = [sem(f"rest_cut{s}") for s in range(RING)]
        self.tile_done = [sem(f"weights_used{s}") for s in range(RING)]
        self.psum_free = [sem(f"unit_evacuated{s}") for s in range(RING)]
        self.loads = [0] * RING
        self.done = [0] * RING
        self.freed = [1] * RING


def pairs(ap):
    return ap.rearrange("p (h t) -> p h t", h=2)


def load_tile(eng, c, w, s, index, kcs):
    dst = c.ring[:, s, 0:kcs * P]
    src = w[bass.ds(index, 1)] if not isinstance(index, int) else w[index:index + 1]
    eng.dma_start(dst, src.rearrange("o p n -> p (o n)")).then_inc(c.loaded[s], 16)


def load_pages(eng, c, dst, src, first, count, loaded):
    with eng.Fori(0, count // 4) as i:
        for x in range(4):
            page = eng.value_load(c.pages[0:1, bass.ds(i * 4 + (first + x), 1)], min_val=0, max_val=POOL - 1)
            eng.dma_start(dst[:, bass.ds(i * 4 + x, 1), :].rearrange("p o n -> p (o n)"),
                          src[bass.ds(page, 1)].rearrange("o p n -> p (o n)")).then_inc(loaded, 16)


def linear(c, name, w, n_units, subs, kcs, src, evac, nxt, scale=None, beside=None):
    nc = c.nc
    tiles = n_units * subs
    loops, rest = tiles // RING, tiles % RING
    per = RING // subs
    base_load, base_done, base_free = list(c.loads), list(c.done), list(c.freed)
    cut_here = not isinstance(src, tuple)
    with ExitStack() as ctx:
        ps = [ctx.enter_context(nc.psum_tensor(f"{name}_ps{j}", [P, 2, 512], F32)) for j in range(per)]
        wh = ctx.enter_context(nc.sbuf_tensor(f"{name}_w_hi", [P, 2, kcs * P], F32R))
        wl = ctx.enter_context(nc.sbuf_tensor(f"{name}_w_lo", [P, 2, kcs * P], F32R))
        if cut_here:
            xh, xl = [ctx.enter_context(nc.sbuf_tensor(f"{name}_x_{n}", [P, kcs, T], F32R)) for n in ("hi", "lo")]
            x_hi, x_lo = [nc.alloc_semaphore(f"{name}_x_{n}_cut") for n in ("hi", "lo")]
        else:
            xh, xl = src
        block = ctx.enter_context(nc.Block())

        def rounds(eng, cut, first_done=None):
            def step(i, s):
                if cut is not None:
                    cut(i, s)
                if isinstance(i, int) and i == 0 and s == 0:
                    if first_done is not None:
                        first_done()
                    return
                r, q = (i, s - 1) if s else (i - 1, RING - 1)
                if q % subs == subs - 1:
                    evac(eng, ps, q // subs, r, ready)

            evac(eng, ps, None, 0, ready)
            for s in range(RING):
                step(0, s)
            if loops > 1:
                with eng.Fori(1, loops) as i:
                    for s in range(RING):
                        step(i, s)
            for s in range(rest):
                step(loops, s)
            r, q = (loops, rest - 1) if rest else (loops - 1, RING - 1)
            evac(eng, ps, q // subs, r, ready)

        def ready(eng, j, i):
            s = j * subs + subs - 1
            eng.wait_ge(c.tile_done[s], i + (base_done[s] + 1))

        def slot_free(eng, i, s):
            if s >= 2:
                eng.wait_ge(c.tile_done[s - 2], i + (base_done[s - 2] + 1))
            elif not (isinstance(i, int) and i == 0):
                eng.wait_ge(c.tile_done[s + 2], i + base_done[s + 2])

        @block.sync
        def _(sp):
            if loops > 1:
                with sp.Fori(0, loops - 1) as i:
                    for s in range(RING):
                        sp.wait_ge(c.lo_cut[s], i + (base_done[s] + 1))
                        load_tile(sp, c, w, s, i * RING + (RING + s), kcs)
                        if beside is not None:
                            beside(sp, i * RING + s)
            for s in range(RING):
                sp.wait_ge(c.lo_cut[s], base_done[s] + loops)
                if s < rest:
                    load_tile(sp, c, w, s, loops * RING + s, kcs)
                    sp.wait_ge(c.lo_cut[s], base_done[s] + loops + 1)
                if nxt is not None:
                    load_tile(sp, c, nxt[0], s, s, nxt[1])

        @block.scalar
        def _(act):
            def cut(i, s):
                act.wait_ge(c.loaded[s], i * 16 + 16 * base_load[s])
                slot_free(act, i, s)
                act.activation(wh[:, s % 2, :], c.ring[:, s, 0:kcs * P], ACT.Copy).then_inc(c.hi_cut[s], 1)

            def cut_source():
                for k in range(kcs):
                    act.activation(xh[:, k, :], src[:, k, :], ACT.Copy,
                                   scale=1.0 if scale is None else scale[:, k:k + 1]).then_inc(x_hi, 1)

            rounds(act, cut, cut_source if cut_here else None)

        @block.vector
        def _(dve):
            def cut(i, s):
                dve.wait_ge(c.loaded[s], i * 16 + 16 * base_load[s])
                slot_free(dve, i, s)
                dve.wait_ge(c.hi_cut[s], i + (base_done[s] + 1))
                dve.tensor_tensor(wl[:, s % 2, :], c.ring[:, s, 0:kcs * P], wh[:, s % 2, :].bitcast(F32),
                                  ALU.subtract).then_inc(c.lo_cut[s], 1)

            def cut_source():
                for k in range(kcs):
                    dve.wait_ge(x_hi, k + 1)
                    hi = xh[:, k, :].bitcast(F32)
                    if scale is None:
                        dve.tensor_tensor(xl[:, k, :], src[:, k, :], hi, ALU.subtract).then_inc(x_lo, 1)
                    else:
                        dve.scalar_tensor_tensor(xl[:, k, :], src[:, k, :], scale[:, k:k + 1], hi, ALU.mult,
                                                 ALU.subtract).then_inc(x_lo, 1)

            rounds(dve, cut, cut_source if cut_here else None)

        @block.gpsimd
        def _(pool):
            rounds(pool, None)

        @block.tensor
        def _(pe):
            def one(s, i, first=False):
                j, sub = s // subs, s % subs
                pe.wait_ge(c.lo_cut[s], i + (base_done[s] + 1))
                if sub == 0:
                    pe.wait_ge(c.psum_free[j], i + base_free[j])
                for k in range(kcs):
                    if first and cut_here:
                        pe.wait_ge(x_lo, k + 1)
                    a, x = slice(k * P, (k + 1) * P), sub * kcs + k
                    for part, (wt, xt) in enumerate(((wh, xh), (wh, xl), (wl, xh))):
                        for h in range(2):
                            last = pe.matmul(ps[j][:, h, 0:TH], wt[:, s % 2, a], xt[:, x, h * TH:(h + 1) * TH],
                                             start=(sub == 0 and k == 0 and part == 0),
                                             stop=(sub == subs - 1 and k == kcs - 1 and part == 2))
                last.then_inc(c.tile_done[s], 1)

            one(0, 0, first=True)
            for s in range(1, RING):
                one(s, 0)
            if loops > 1:
                with pe.Fori(1, loops) as i:
                    for s in range(RING):
                        one(s, i)
            for s in range(rest):
                one(s, loops)

    for s in range(RING):
        c.done[s] += loops + (s < rest)
        c.loads[s] += loops - 1 + (s < rest) + (nxt is not None)
        if s < per:
            c.freed[s] += loops + (s < rest // subs)


def evac_scaled(c, dst, per=RING):
    def evac(eng, ps, j, i, ready):
        if eng is not c.nc.vector or j is None:
            return
        ready(eng, j, i)
        if isinstance(i, int):
            eng.tensor_tensor(pairs(dst[:, i * per + j, :]), ps[j][:, :, 0:TH], pairs(c.rstd[:, :]), ALU.mult)\
               .then_inc(c.psum_free[j], 1)
        else:
            eng.tensor_tensor(dst[:, bass.ds(i * per + j, 1), :].rearrange("p o (h t) -> p (o h) t", h=2),
                              ps[j][:, :, 0:TH], pairs(c.rstd[:, :]), ALU.mult).then_inc(c.psum_free[j], 1)
    return evac


def evac_swiglu(c, Hh, Hl, a_t, g_t, prod, sems):
    a_act, made, used = sems
    base_free = list(c.freed)

    def evac(eng, ps, j, i, ready):
        if j is None:
            if eng is c.nc.gpsimd:
                for m in range(2):
                    eng.sem_inc(used[m], 1)
            return
        m, is_g = j // 2, j % 2
        if eng is c.nc.vector:
            ready(eng, j, i)
            eng.wait_ge(used[m], i + 1)
            eng.tensor_tensor(pairs((g_t if is_g else a_t)[:, m, :]), ps[j][:, :, 0:TH], pairs(c.rstd[:, :]),
                              ALU.mult).then_inc(c.psum_free[j], 1)
        if eng is c.nc.scalar and not is_g:
            eng.wait_ge(c.psum_free[j], i + (base_free[j] + 1))
            eng.activation(a_t[:, m, :], a_t[:, m, :], ACT.Silu).then_inc(a_act[m], 1)
        if eng is c.nc.gpsimd and is_g:
            hi, lo = [x[:, i * 2 + m, :] if isinstance(i, int) else
                      x[:, bass.ds(i * 2 + m, 1), :].rearrange("p o t -> p (o t)") for x in (Hh, Hl)]
            eng.wait_ge(a_act[m], i + 1)
            eng.wait_ge(c.psum_free[j], i + (base_free[j] + 1))
            at = i * 4 + 2 * m
            eng.tensor_tensor(prod[:, :], a_t[:, m, :], g_t[:, m, :], ALU.mult).then_inc(made, 1)
            eng.wait_ge(made, at + 1)
            eng.tensor_tensor(hi, a_t[:, m, :], g_t[:, m, :], ALU.mult).then_inc(made, 1)
            eng.wait_ge(made, at + 2)
            eng.tensor_tensor(lo, prod[:, :], hi.bitcast(F32), ALU.subtract).then_inc(used[m], 1)
            eng.wait_ge(used[m], i + 2)
    return evac


def evac_squares(c, dst, sq, ssq, sems, per):
    squared, added = sems
    base_free = list(c.freed)

    def evac(eng, ps, j, i, ready):
        if j is None:
            if eng is c.nc.vector:
                eng.memset(ssq[:, :], 0.0).then_inc(added, 1)
            return
        if eng is c.nc.scalar:
            ready(eng, j, i)
            out = pairs(dst[:, i * per + j, :]) if isinstance(i, int) else \
                dst[:, bass.ds(i * per + j, 1), :].rearrange("p o (h t) -> p (o h) t", h=2)
            eng.activation(out, ps[j][:, :, 0:TH], ACT.Copy).then_inc(c.psum_free[j], 1)
        if eng is c.nc.vector:
            eng.wait_ge(c.psum_free[j], i + (base_free[j] + 1))
            v = dst[:, i * per + j, :] if isinstance(i, int) else \
                dst[:, bass.ds(i * per + j, 1), :].rearrange("p o t -> p (o t)")
            eng.wait_ge(added, i * per + (j + 1))
            eng.tensor_tensor(sq[:, :], v, v, ALU.mult).then_inc(squared, 1)
            eng.wait_ge(squared, i * per + (j + 1))
            eng.tensor_tensor(ssq[:, :], ssq[:, :], sq[:, :], ALU.add).then_inc(added, 1)
    return evac


def norm_step(c, name, ssq=None, post=None, pre=True):
    nc = c.nc
    with ExitStack() as ctx:
        sem = lambda n: nc.alloc_semaphore(f"{name}_{n}")
        summed, mean_in, rooted, own_done, scaled, squared, added = [sem(n) for n in
            ("token_sums", "inverse_means", "roots", "dve_chain", "scaled", "squares", "squares_added")]
        x_new = [sem(f"x_new{j}") for j in range(2)]
        ps = [ctx.enter_context(nc.psum_tensor(f"{name}_ps{j}", [P, 2, 512], F32)) for j in range(2)]
        sq = ctx.enter_context(nc.sbuf_tensor(f"{name}_squares", [P, 2, T], F32))
        y = ctx.enter_context(nc.sbuf_tensor(f"{name}_scaled", [P, 2, T], F32))
        block = ctx.enter_context(nc.Block())

        @block.tensor
        def _(pe):
            if post is not None:
                for h in range(2):
                    mm = pe.matmul(ps[0][:, h, 0:TH], c.ones[:, :], ssq[:, h * TH:(h + 1) * TH], start=True, stop=True)
                mm.then_inc(summed, 1)
            if pre:
                for k in range(KC):
                    pe.wait_ge(squared, k + 1)
                    for h in range(2):
                        mm = pe.matmul(ps[1][:, h, 0:TH], c.ones[:, :], sq[:, k % 2, h * TH:(h + 1) * TH],
                                       start=k == 0, stop=k == KC - 1)
                    mm.then_inc(added, 1)

        @block.scalar
        def _(act):
            if post is not None:
                act.wait_ge(mean_in, 1)
                act.activation(c.rstd[:, :], c.rstd[:, :], ACT.Sqrt).then_inc(rooted, 1)
            if pre:
                for k in range(KC):
                    if post is not None:
                        act.wait_ge(x_new[k % 2], k // 2 + 1)
                    if k >= 2:
                        act.wait_ge(added, k - 1)
                    act.activation(sq[:, k % 2, :], c.X[:, k, :], ACT.Square).then_inc(squared, 1)
                act.wait_ge(mean_in, 2 if post is not None else 1)
                act.activation(c.rstd[:, :], c.rstd[:, :], ACT.Sqrt).then_inc(rooted, 1)

        @block.gpsimd
        def _(pool):
            if post is not None:
                for k in range(1, KC, 2):
                    pool.wait_ge(scaled, k + 1)
                    pool.tensor_tensor(c.X[:, k, :], c.X[:, k, :], y[:, 1, :], ALU.add).then_inc(x_new[1], 1)
                    pool.wait_ge(x_new[1], k // 2 + 1)

        @block.vector
        def _(dve):
            own = Seq(dve, own_done)

            def inverse_mean(j):
                own.link(dve.tensor_scalar(pairs(c.rstd[:, :]), ps[j][:, :, 0:TH], 1.0 / D_MODEL, EPS, ALU.mult, ALU.add))
                dve.reciprocal(c.rstd[:, :], c.rstd[:, :]).then_inc(mean_in, 1)

            if post is not None:
                dve.wait_ge(summed, 1)
                inverse_mean(0)
                dve.wait_ge(rooted, 1)
                for k in range(KC):
                    if k >= 3 and k % 2:
                        dve.wait_ge(x_new[1], k // 2)
                    dve.scalar_tensor_tensor(y[:, k % 2, :], post[0][:, k, :], post[1][:, k:k + 1], c.rstd[:, :],
                                             ALU.mult, ALU.mult).then_inc(scaled, 1)
                    if k % 2 == 0:
                        dve.wait_ge(scaled, k + 1)
                        dve.tensor_tensor(c.X[:, k, :], c.X[:, k, :], y[:, 0, :], ALU.add).then_inc(x_new[0], 1)
                        dve.wait_ge(x_new[0], k // 2 + 1)
            if pre:
                dve.wait_ge(added, KC)
                inverse_mean(1)


PAGES_A_CHUNK = 32


def compress(c, HT, d, rows, first_in, kcT, kcBD, vcS, BDv):
    nc = c.nc
    CH = PAGES_A_CHUNK
    NCH = NB * PAGES // CH
    with ExitStack() as ctx:
        sem = lambda n: nc.alloc_semaphore(f"cmp_{n}")
        sb = lambda n, s: ctx.enter_context(nc.sbuf_tensor(f"cmp_{n}", s, F32))
        w1 = sb("w1", [P, 2, BLOCK // 2, P])
        free = sb("small", [P, 1802])
        HN = NB * PAGES * 4 + 2 * PBLK
        hid = free[:, 0:2 * HN].rearrange("p (a n) -> p a n", a=2)
        hid_rep = free[:, 2 * HN:2 * HN + P].rearrange("p (a b n) -> p a b n", a=GP, b=8)
        v_rep = free[:, 2 * HN + P:2 * HN + 2 * P]
        pe_in = free[:, 1400:1528].rearrange("p (a n) -> p a n", a=2)
        w2 = free[:, 1528:1784].rearrange("p (a n) -> p a n", a=2)
        pe_w = free[:, 1784:1786]
        mask = free[:, 1786:1802]
        ps_c = [ctx.enter_context(nc.psum_tensor(f"cmp_ps{j}", [P, 512], F32)) for j in range(2)]
        ps_p = ctx.enter_context(nc.psum_tensor("cmp_psp", [P, 512], F32))
        ps_k = ctx.enter_context(nc.psum_tensor("cmp_psk", [P, 512], F32))
        ps_q = ctx.enter_context(nc.psum_tensor("cmp_psq", [P, 512], F32))
        ps_v = ctx.enter_context(nc.psum_tensor("cmp_psv", [P, 512], F32))
        small, w1_in = sem("small_loaded"), [sem(f"w1_half{h}_loaded") for h in range(2)]
        rows_in = [sem(f"rows{s}_loaded") for s in range(2)]
        w1_used = sem("w1_half0_used")
        prompt_done, pe_done, pe_out = sem("prompt_products"), sem("pe_products"), sem("pe_copied")
        chunk_done = [sem(f"chunk{s}_products") for s in range(2)]
        chunk_out = [sem(f"chunk{s}_silu") for s in range(2)]
        prompt_out, second, moved, own_done = sem("prompt_silu"), sem("second_products"), sem("rep_ready"), sem("chain")
        block = ctx.enter_context(nc.Block())

        def load_chunk(eng, g, half):
            eng.wait_ge(chunk_done[g % 2], g // 2)
            load_pages(eng, c, rows[:, g % 2, half * (CH // 2):(half + 1) * (CH // 2)], d["cache_cmp"][g // NCH],
                       (g % NCH) * CH + half * (CH // 2), CH // 2, rows_in[g % 2])

        @block.sync
        def _(sp):
            sp.dma_start(pe_in[:, :, :], d["cmp_pe"]).then_inc(small, 16)
            sp.dma_start(w2[:, :, :], d["cmp_w2"]).then_inc(small, 16)
            sp.dma_start(mask[:, :], d["head_mask"]).then_inc(small, 16)
            def load_w1(kv, h):
                sp.dma_start(w1[:, h].rearrange("p t n -> p (t n)"), d["cmp_w1"][kv, h]).then_inc(w1_in[h], 16)

            load_w1(0, 0)
            load_w1(0, 1)
            for g in range(2, 2 * NCH):
                if g == NCH + 1:
                    sp.wait_ge(w1_used, 1)
                    load_w1(1, 0)
                    sp.wait_ge(chunk_done[1], NCH // 2)
                    load_w1(1, 1)
                load_chunk(sp, g, 0)

        @block.tensor
        def _(pe):
            pe.wait_ge(small, 48)
            for kv in range(2):
                for h in range(2):
                    pe.wait_ge(w1_in[h], 16 * (kv + 1))
                if kv:
                    pe.wait_ge(prompt_out, 1)
                for t in range(BLOCK):
                    mm = pe.matmul(ps_p[:, 0:16], w1[:, t // 32, t % 32, :],
                                   HT[:, CK_U + 2 * kv:CK_U + 2 * kv + 2, t:SEQ:BLOCK], start=t == 0, stop=t == BLOCK - 1)
                mm.then_inc(prompt_done, 1)
                for t in range(BLOCK):
                    mm = pe.matmul(ps_p[:, 16:17], w1[:, t // 32, t % 32, :], pe_in[:, kv, t:t + 1],
                                   start=t == 0, stop=t == BLOCK - 1)
                mm.then_inc(pe_done, 1)
                for ch in range(NCH):
                    s = ch % 2
                    n = kv * (NCH // 2) + ch // 2
                    if n == 0:
                        pe.wait_ge(first_in, 16 * 2 * CH)
                    else:
                        pe.wait_ge(rows_in[s], 16 * CH * n)
                    if n:
                        pe.wait_ge(chunk_out[s], n)
                    v = rows[:, s].rearrange("p g (c t) -> p g c t", t=BLOCK)
                    for t in range(BLOCK):
                        mm = pe.matmul(ps_c[s][:, 0:P], w1[:, t // 32, t % 32, :], v[:, :, :, t],
                                       start=t == 0, stop=t == BLOCK - 1)
                        if ch == NCH - 1 and t == 31 and kv == 0:
                            mm.then_inc(w1_used, 1)
                    mm.then_inc(chunk_done[s], 1)
            pe.wait_ge(chunk_out[0], NCH)
            pe.wait_ge(chunk_out[1], NCH)
            pe.wait_ge(prompt_out, 2)
            pe.matmul(ps_k[:, :], w2[:, 0, :], hid[:, 0, 0:512], start=True, stop=True).then_inc(second, 1)
            pe.matmul(ps_q[:, 0:16], w2[:, 0, :], hid[:, 0, 512:528], start=True, stop=True).then_inc(second, 1)
            for j in range(4):
                mm = pe.matmul(ps_v[:, j * P:(j + 1) * P], hid[:, 1, j:512:4], w2[:, 1, :], start=True, stop=True)
            mm.then_inc(second, 1)
            pe.wait_ge(moved, 1)
            pe.matmul(ps_c[0][:, 0:P], hid_rep[:, :, :, :].rearrange("p a b n -> p (a b n)"), w2[:, 1, :],
                      start=True, stop=True).then_inc(second, 1)

        @block.scalar
        def _(act):
            for kv in range(2):
                act.wait_ge(pe_done, kv + 1)
                act.activation(pe_w[:, kv:kv + 1], ps_p[:, 16:17], ACT.Copy).then_inc(pe_out, 1)
                act.wait_ge(pe_out, kv + 1)
                act.activation(hid[:, kv, 512:528], ps_p[:, 0:16], ACT.Silu, bias=pe_w[:, kv:kv + 1])\
                   .then_inc(prompt_out, 1)
                for ch in range(NCH):
                    s = ch % 2
                    act.wait_ge(chunk_done[s], kv * (NCH // 2) + ch // 2 + 1)
                    act.activation(hid[:, kv, ch * P:(ch + 1) * P], ps_c[s][:, 0:P], ACT.Silu,
                                   bias=pe_w[:, kv:kv + 1]).then_inc(chunk_out[s], 1)
                    if kv * NCH + ch + 2 < 2 * NCH:
                        load_chunk(act, kv * NCH + ch + 2, 1)

        @block.vector
        def _(dve):
            own = Seq(dve, own_done)
            own.link(dve.memset(kcBD[:, :, :, :], 0.0))
            dve.wait_ge(prompt_out, 2)
            dve.tensor_copy(hid_rep[:, :, :, :], hid[:, 1, 512:528].rearrange("p (g n) -> p g n", g=GP)
                            .unsqueeze(2).broadcast_to([P, GP, 8, PBLK])).then_inc(moved, 1)
            dve.wait_ge(second, 1)
            own(dve.tensor_copy(kcT[:, :], ps_k[:, :]))
            dve.wait_ge(second, 2)
            for g2 in range(2):
                rows_g = slice(g2 * HD, (g2 + 1) * HD)
                own(dve.tensor_copy(kcBD[rows_g, :, g2, :], ps_q[rows_g, 0:16].rearrange("p (g n) -> p g n", g=GP)))
            dve.wait_ge(second, 3)
            own(dve.tensor_copy(vcS[:, :], ps_v[:, :]))
            dve.wait_ge(second, 4)
            own.link(dve.tensor_copy(v_rep[:, :], ps_c[0][:, 0:P]))
            dve.wait_ge(small, 48)
            for g2 in range(2):
                own(dve.tensor_tensor(BDv[:, :, g2, :],
                                      v_rep[:, g2 * HD:(g2 + 1) * HD].unsqueeze(1).broadcast_to([P, 8, HD]),
                                      mask[:, :].rearrange("p (c g) -> p c g", g=2)[:, :, g2].unsqueeze(2)
                                      .broadcast_to([P, 8, HD]), ALU.mult))


def attention_setup(c, HT, d, tabs, T_bias, biasC, Vtok, gT, Vnew):
    nc = c.nc
    with ExitStack() as ctx:
        sem = lambda n: nc.alloc_semaphore(f"set_{n}")
        sb = lambda n, s: ctx.enter_context(nc.sbuf_tensor(f"set_{n}", s, F32))
        oh = sb("onehot", [N_BUCKETS + 1, 2, 1024])
        R = sb("bias_row", [16, 1024])
        sg = sb("gates", [48, T])
        ps = [ctx.enter_context(nc.psum_tensor(f"set_ps{j}", [P, 512], F32)) for j in range(6)]
        loaded, scaled, gated, row_ready, row_out, t_in = [sem(n) for n in
            ("loaded", "q_scaled", "gates", "bias_row", "bias_row_out", "bias_tiles_in")]
        made, moved, gate_out = sem("psum_ready"), sem("psum_moved"), sem("gates_out")
        block = ctx.enter_context(nc.Block())

        @block.sync
        def _(sp):
            sp.dma_start(oh[:, :, :], d["onehot_rows"]).then_inc(loaded, 16)
            sp.dma_start(tabs[:, :], d["tabs"]).then_inc(loaded, 16)
            sp.dma_start(d["kv_out"], HT[:, CK_U:GATE_U, :]).then_inc(gate_out, 16)
            sp.wait_ge(gated, 1)
            sp.dma_start(d["gate_scratch"], sg[:, SEQ:T]).then_inc(gate_out, 16)
            sp.wait_ge(moved, 2)
            sp.dma_start(d["bias_scratch"], R[:, :]).then_inc(row_out, 16)
            sp.wait_ge(row_out, 16)
            sp.dma_start(d["bias_skew"], bass.AP(d["bias_scratch"].tensor, 0, [[0, P], [1024, HEADS], [1, SKEW]]))\
              .then_inc(t_in, 16)
            sp.wait_ge(t_in, 16)
            sp.dma_start(T_bias[:, :, :], bass.AP(d["bias_skew"].tensor, P - 1, [[HEADS * SKEW - 1, P], [SKEW, HEADS], [1, SEQ]]))\
              .then_inc(t_in, 16)
            sp.wait_ge(t_in, 32)
            sp.wait_ge(gate_out, 32)

        @block.tensor
        def _(pe):
            pe.wait_ge(loaded, 32)
            for j in range(2):
                pe.matmul(ps[j][0:16, :], tabs[:, 0:16], oh[:, 0, j * 512:(j + 1) * 512], start=True, stop=True)\
                  .then_inc(made, 1)
            for i in range(TILES):
                for n in range(PBLK):
                    at = P * i - BLOCK * n - (BLOCK - 1) + 511
                    mm = pe.matmul(ps[2][:, (i * PBLK + n) * 16:(i * PBLK + n + 1) * 16], oh[:, 1, at:at + P],
                                   tabs[:, 0:16], start=True, stop=True)
            mm.then_inc(made, 1)
            pe.wait_ge(gated, 1)
            for i in range(TILES):
                mm = pe.transpose(ps[3][:, i * 48:(i + 1) * 48], sg[:, i * P:(i + 1) * P], c.ident[0:48, 0:48])
            mm.then_inc(made, 1)
            for j, u in enumerate((SV_U, SV_U + 1, WV_U, WV_U + 1)):
                mm = pe.transpose(ps[4][0:NB, j * P:(j + 1) * P], HT[:, u, SEQ:T], c.ident[:, :])
            mm.then_inc(made, 1)
            for i in range(TILES):
                b = ps[5] if i % 2 == 0 else ps[0]
                if i == 1:
                    pe.wait_ge(moved, 2)
                if i >= 2:
                    pe.wait_ge(moved, 4 + i)
                for j, u in enumerate((SV_U, SV_U + 1, WV_U, WV_U + 1)):
                    mm = pe.transpose(b[:, j * P:(j + 1) * P], HT[:, u, i * P:(i + 1) * P], c.ident[:, :])
                mm.then_inc(made, 1)

        @block.scalar
        def _(act):
            act.activation(sg[:, :], HT[0:48, GATE_U, :], ACT.Sigmoid).then_inc(gated, 1)

        @block.vector
        def _(dve):
            dve.tensor_scalar(HT[:, 0:8, :], HT[:, 0:8, :], HD ** -0.5, None, ALU.mult).then_inc(scaled, 1)
            for j in range(2):
                dve.wait_ge(made, j + 1)
                dve.tensor_copy(R[:, j * 512:(j + 1) * 512], ps[j][0:16, :]).then_inc(moved, 1)
            dve.wait_ge(made, 3)
            dve.tensor_copy(biasC[:, :, :, :], ps[2][:, :].rearrange("p (i n h) -> p i h n", i=TILES, n=PBLK))\
               .then_inc(moved, 1)
            dve.wait_ge(made, 4)
            dve.tensor_copy(gT[:, :, :], ps[3][:, 0:192].rearrange("p (i n) -> p i n", i=TILES)).then_inc(moved, 1)
            dve.wait_ge(made, 5)
            dve.tensor_copy(Vnew[:, :], ps[4][0:NB, :]).then_inc(moved, 1)
            for i in range(TILES):
                dve.wait_ge(made, 6 + i)
                dve.tensor_copy(Vtok[:, i, :], (ps[5] if i % 2 == 0 else ps[0])[:, :]).then_inc(moved, 1)


def prompt_compressed(c, HT, kcBD, BDv, biasC, gT, Otok):
    nc = c.nc
    with ExitStack() as ctx:
        sem = lambda n: nc.alloc_semaphore(f"pc_{n}")
        sb = lambda n, s: ctx.enter_context(nc.sbuf_tensor(f"pc_{n}", s, F32))
        S = sb("scores", [P, TILES * HEADS, PBLK])
        mx = sb("max", [P, TILES * HEADS])
        sm = sb("sum", [P, TILES * HEADS])
        PT = sb("probsT", [P, SEQ])
        ps_s = ctx.enter_context(nc.psum_tensor("pc_ps", [P, 512], F32))
        ps_t = ctx.enter_context(nc.psum_tensor("pc_pt", [P, 512], F32))
        ps_o = [ctx.enter_context(nc.psum_tensor(f"pc_po{j}", [P, 2, 512], F32)) for j in range(2)]
        scores, shifted, expd, probs, turned, turned_out, outs, outs_moved, own_done = [sem(n) for n in
            ("scores", "shifted", "exp", "probs", "turned", "turned_out", "outs", "outs_moved", "chain")]
        block = ctx.enter_context(nc.Block())
        wide = lambda a: a.unsqueeze(2).broadcast_to([P, TILES * HEADS, PBLK])

        @block.tensor
        def _(pe):
            for i in range(TILES):
                for u in range(8):
                    at = (i * 8 + u) * 16
                    mm = pe.matmul(ps_s[:, at:at + 16], HT[:, u, i * P:(i + 1) * P],
                                   kcBD[:, u // REP].rearrange("p g n -> p (g n)"), start=True, stop=True)
            mm.then_inc(scores, 1)
            pe.wait_ge(probs, 1)
            for i in range(TILES):
                mm = pe.transpose(ps_t[:, i * P:(i + 1) * P],
                                  S[:, i * HEADS:(i + 1) * HEADS, :].rearrange("p h n -> p (h n)"), c.ident[:, :])
            mm.then_inc(turned, 1)
            pe.wait_ge(turned_out, 1)
            for i in range(TILES):
                if i >= 2:
                    pe.wait_ge(outs_moved, i - 1)
                for j in range(2):
                    mm = pe.matmul(ps_o[i % 2][:, j, :], PT[:, i * P:(i + 1) * P],
                                   BDv[:, 4 * j:4 * j + 4].rearrange("p c g n -> p (c g n)"), start=True, stop=True)
                mm.then_inc(outs, 1)

        @block.scalar
        def _(act):
            act.wait_ge(shifted, 1)
            act.activation(S[:, :, :], S[:, :, :], ACT.Exp).then_inc(expd, 1)

        @block.vector
        def _(dve):
            own = Seq(dve, own_done)
            dve.wait_ge(scores, 1)
            own.link(dve.tensor_tensor(S[:, :, :], ps_s[:, :].rearrange("p (m n) -> p m n", n=PBLK),
                                       biasC[:, :, :, :].rearrange("p i h n -> p (i h) n"), ALU.add))
            own.link(dve.tensor_reduce(mx[:, :], S[:, :, :], AX, ALU.max))
            own.link(dve.tensor_scalar(mx[:, :], mx[:, :], FLOOR, None, ALU.max))
            dve.tensor_tensor(S[:, :, :], S[:, :, :], wide(mx[:, :]), ALU.subtract).then_inc(shifted, 1)
            dve.wait_ge(expd, 1)
            own.link(dve.tensor_reduce(sm[:, :], S[:, :, :], AX, ALU.add))
            own.link(dve.tensor_scalar(sm[:, :], sm[:, :], 1e-30, None, ALU.max))
            own.link(dve.reciprocal(sm[:, :], sm[:, :]))
            own.link(dve.tensor_tensor(sm[:, :].rearrange("p (i h) -> p i h", i=TILES),
                                       sm[:, :].rearrange("p (i h) -> p i h", i=TILES), gT[:, :, 0:16], ALU.mult))
            dve.tensor_tensor(S[:, :, :], S[:, :, :], wide(sm[:, :]), ALU.mult).then_inc(probs, 1)
            dve.wait_ge(turned, 1)
            dve.tensor_copy(PT[:, :], ps_t[:, :]).then_inc(turned_out, 1)
            for i in range(TILES):
                dve.wait_ge(outs, i + 1)
                dve.tensor_copy(Otok[:, i, :], ps_o[i % 2][:, :, :].rearrange("p a b -> p (a b)")).then_inc(outs_moved, 1)


def prompt_attention(c, HT, T_bias, Vtok, gT, Otok):
    nc = c.nc
    items = [(s, g2, br, i) for s in range(2) for g2 in range(2) for br in range(2) for i in range(TILES)]
    N = len(items)
    with ExitStack() as ctx:
        sem = lambda n: nc.alloc_semaphore(f"pa_{n}")
        sb = lambda n, s: ctx.enter_context(nc.sbuf_tensor(f"pa_{n}", s, F32))
        Qs = [sb(f"q{s}", [P, 2, SEQ]) for s in range(2)]
        Tb = [sb(f"bias{s}", [P, 2, SEQ]) for s in range(2)]
        Sb = [sb(f"scores{j}", [P, SEQ]) for j in range(3)]
        E = [sb(f"exp{j}", [P, SEQ]) for j in range(3)]
        ET = [sb(f"expT{j}", [P, SEQ]) for j in range(2)]
        nm = sb("neg_max", [P, 2 * 16])
        rs = sb("row_sum", [P, 2 * 16])
        sc = sb("scale", [P, 2, 16])
        tmp = sb("tmp", [P, 16, HD])
        ps_s = [ctx.enter_context(nc.psum_tensor(f"pa_s{j}", [P, 512], F32)) for j in range(2)]
        ps_t = [ctx.enter_context(nc.psum_tensor(f"pa_t{j}", [P, 512], F32)) for j in range(2)]
        ps_o = [ctx.enter_context(nc.psum_tensor(f"pa_o{j}", [P, 2, 512], F32)) for j in range(2)]
        staged, cleared = [sem(f"chunk{s}_staged") for s in range(2)], sem("cleared")
        scored, biased, expd, turned, turned_out, mixed, merged, own_done = [sem(n) for n in
            ("scores", "biased", "exp", "turned", "turned_out", "mixed", "merged", "chain")]
        block = ctx.enter_context(nc.Block())
        waited = sem("waited")
        n_merge = 6

        @block.gpsimd
        def _(pool):
            for s in range(2):
                pool.memset(Qs[s][:, :, :], 0.0).then_inc(cleared, 1)
            pool.wait_ge(cleared, 2)
            with pool.Fori(0, GP) as gp:
                with pool.Fori(0, 2) as rr:
                    for s in range(2):
                        pool.wait_ge(merged, (gp * 4 + rr * 2) + (s + 1))
                        u = gp * REP + rr * 2 + s
                        own = Seq(pool, staged[s], (gp * 2 + rr) * 4)
                        for g2 in range(2):
                            rows = slice(g2 * HD, (g2 + 1) * HD)
                            own.link(pool.tensor_copy(Qs[s][rows, g2, :], HT[rows, bass.ds(u, 1), 0:SEQ]
                                                      .rearrange("p o t -> p (o t)")))
                            own.link(pool.tensor_copy(Tb[s][:, g2, :], T_bias[:, bass.ds(u * 2 + g2, 1), :]
                                                      .rearrange("p o t -> p (o t)")))

        @block.tensor
        def _(pe):
            with pe.Fori(0, GP) as gp:
                with pe.Fori(0, 2) as rr:
                    it = gp * 2 + rr
                    for n in range(N + 2):
                        if n < N:
                            s, g2, br, i = items[n]
                            if n % 16 == 0:
                                pe.wait_ge(staged[s], it * 4 + 4)
                            if n >= 2:
                                pe.wait_ge(biased, it * N + (n - 1))
                            pe.matmul(ps_s[n % 2][:, 0:(i + 1) * P], Qs[s][:, g2, i * P:(i + 1) * P],
                                      HT[:, bass.ds(gp + (SK_U + 4 * br), 1), 0:(i + 1) * P]
                                      .rearrange("p o t -> p (o t)"), start=True, stop=True).then_inc(scored, 1)
                        if 1 <= n <= N:
                            m = n - 1
                            s, g2, br, i = items[m]
                            pe.wait_ge(expd, it * N + (m + 1))
                            if m >= 2:
                                pe.wait_ge(turned_out, it * N + (m - 1))
                            for j in range(i + 1):
                                mm = pe.transpose(ps_t[m % 2][:, j * P:(j + 1) * P], E[m % 3][:, j * P:(j + 1) * P],
                                                  c.ident[:, :])
                            mm.then_inc(turned, 1)
                        if n >= 2:
                            m = n - 2
                            s, g2, br, i = items[m]
                            pe.wait_ge(turned_out, it * N + (m + 1))
                            if m % 16 == 0:
                                pe.wait_ge(merged, it * 2 + (s + 1))
                            at = (br * 2 + g2) * TILES + i
                            out = ps_o[s][:, at // 8, (at % 8) * HD:(at % 8 + 1) * HD]
                            for j in range(i + 1):
                                v = Vtok[:, j, :].rearrange("p (b n) -> p b n", b=2)[:, br, :]
                                mm = pe.matmul(out, ET[m % 2][:, j * P:(j + 1) * P],
                                               v[:, bass.ds(gp * P + g2 * HD, HD)], start=j == 0, stop=j == i)
                            mm.then_inc(mixed, 1)

        @block.scalar
        def _(act):
            with act.Fori(0, GP) as gp:
                with act.Fori(0, 2) as rr:
                    it = gp * 2 + rr
                    for n, (s, g2, br, i) in enumerate(items):
                        act.wait_ge(biased, it * N + (n + 1))
                        if n >= 3:
                            act.wait_ge(turned, it * N + (n - 2))
                        w = (i + 1) * P
                        k = s * 16 + (br * 2 + g2) * TILES + i
                        act.activation(E[n % 3][:, 0:w], Sb[n % 3][:, 0:w], ACT.Exp, bias=nm[:, k:k + 1], scale=-1.0,
                                       accum_out=rs[:, k:k + 1]).then_inc(expd, 1)

        @block.vector
        def _(dve):
            dve.sem_inc(merged, 1)
            dve.sem_inc(merged, 1)
            with dve.Fori(0, GP) as gp:
                with dve.Fori(0, 2) as rr:
                    it = gp * 2 + rr
                    own = Seq(dve, own_done, it * (2 * n_merge))

                    def merge(s):
                        dve.wait_ge(mixed, it * N + 16 * (s + 1))
                        k = slice(s * 16, (s + 1) * 16)
                        own.link(dve.reciprocal(sc[:, s, :], rs[:, k]))
                        for br in range(2):
                            g = gT[:, :, 16 * (br + 1):16 * (br + 2)].rearrange("p i (c g) -> p c g i", g=2)
                            o = sc[:, s, 8 * br:8 * br + 8].rearrange("p (g i) -> p g i", g=2)
                            own(dve.tensor_tensor(o, o, g[:, bass.ds(gp * REP + rr * 2 + s, 1)]
                                                  .rearrange("p o g i -> p (o g) i"), ALU.mult))
                        own.wait()
                        own.link(dve.tensor_tensor(tmp[:, :, :], ps_o[s][:, :, :].rearrange("p a (b n) -> p (a b) n", n=HD),
                                                   sc[:, s, :].unsqueeze(2).broadcast_to([P, 16, HD]), ALU.mult))
                        own.link(dve.tensor_tensor(tmp[:, 0:8, :], tmp[:, 0:8, :], tmp[:, 8:16, :], ALU.add))
                        o = Otok[:, :, :].rearrange("p i (c n) -> p c i n", n=P)[:, bass.ds(gp * REP + rr * 2 + s, 1)]\
                            .rearrange("p o i n -> p (o i) n")
                        for g2 in range(2):
                            og = o[:, :, g2 * HD:(g2 + 1) * HD]
                            ins = dve.tensor_tensor(og, og, tmp[:, 4 * g2:4 * g2 + 4, :], ALU.add)
                            if g2 == 0:
                                own.link(ins)
                            else:
                                ins.then_inc(merged, 1)

                    for n in range(N + 1):
                        if n < N:
                            s, g2, br, i = items[n]
                            w = (i + 1) * P
                            k = s * 16 + (br * 2 + g2) * TILES + i
                            dve.wait_ge(cleared, 2)
                            dve.wait_ge(scored, it * N + (n + 1))
                            if n >= 3:
                                dve.wait_ge(expd, it * N + (n - 2))
                            dve.sem_inc(waited, 1)
                            dve.tensor_tensor_reduce(Sb[n % 3][:, 0:w], ps_s[n % 2][:, 0:w],
                                                     Tb[s][:, g2, SEQ - w:SEQ], -1.0, 3e38, ALU.add, ALU.min,
                                                     nm[:, k:k + 1]).then_inc(biased, 1)
                        if n >= 1:
                            m = n - 1
                            s, g2, br, i = items[m]
                            dve.wait_ge(turned, it * N + (m + 1))
                            if m >= 2:
                                dve.wait_ge(mixed, it * N + (m - 1))
                            dve.tensor_copy(ET[m % 2][:, 0:(i + 1) * P], ps_t[m % 2][:, 0:(i + 1) * P])\
                               .then_inc(turned_out, 1)
                        if n == 20:
                            merge(0)
                    merge(1)
                    assert own.n == 2 * (n_merge)


def turn_outputs(c, Otok):
    nc = c.nc
    with ExitStack() as ctx:
        ps = [ctx.enter_context(nc.psum_tensor(f"to_ps{j}", [P, 512], F32)) for j in range(2)]
        turned = nc.alloc_semaphore("to_turned")
        moved = nc.alloc_semaphore("to_moved")
        block = ctx.enter_context(nc.Block())

        @block.tensor
        def _(pe):
            for u in range(KC):
                if u >= 2:
                    pe.wait_ge(moved, u - 1)
                for i in range(TILES):
                    mm = pe.transpose(ps[u % 2][:, i * P:(i + 1) * P], Otok[:, i, u * P:(u + 1) * P], c.ident[:, :])
                mm.then_inc(turned, 1)

        @block.vector
        def _(dve):
            for u in range(KC):
                dve.wait_ge(turned, u + 1)
                dve.tensor_copy(c.XW[:, u, 0:SEQ], ps[u % 2][:, :]).then_inc(moved, 1)


def sample_scores(c, HT, d, tabs, kcT, psS, psW, psM, consts):
    nc = c.nc
    PG = 8
    with ExitStack() as ctx:
        sem = lambda n: nc.alloc_semaphore(f"ss_{n}")
        sb = lambda n, s: ctx.enter_context(nc.sbuf_tensor(f"ss_{n}", s, F32))
        oh = sb("onehot", [N_BUCKETS + 1, PAST + WIN + NBLK + 1])
        wk = sb("win_k", [P, NB, GP, WIN])
        kb = sb("k_pages", [P, 2, PG, GP * P])
        qz = sb("q_padded", [P, NB * 272])
        loaded, wk_in, patched, out_done, cleared, q_in = [sem(n) for n in
            ("loaded", "win_in", "win_patched", "win_out", "cleared", "q_in")]
        k_in = [sem(f"pages{s}_in") for s in range(2)]
        k_used = [sem(f"pages{s}_used") for s in range(2)]
        block = ctx.enter_context(nc.Block())
        q_of = lambda b, g: qz[:, (b * GP + g) * P:(b * GP + g + 1) * P]

        @block.sync
        def _(sp):
            sp.dma_start(oh[:, :], d["onehot_sample"]).then_inc(loaded, 16)
            sp.dma_start(consts[0][:, :], d["batch_mask"]).then_inc(loaded, 16)
            sp.dma_start(consts[1][:, :], d["group_sum"]).then_inc(loaded, 16)
            sp.dma_start(wk[:, :, :, :], d["win_k"]).then_inc(wk_in, 16)
            for n in range(NB * PAGES // PG):
                s = n % 2
                if n >= 2:
                    sp.wait_ge(k_used[s], n // 2)
                load_pages(sp, c, kb[:, s, 0:PG // 2], d["slc_k"], n * PG, PG // 2, k_in[s])
            sp.wait_ge(patched, 1)
            sp.dma_start(d["win_k_out"], wk[:, :, :, :]).then_inc(out_done, 16)
            sp.wait_ge(out_done, 16)

        @block.scalar
        def _(act):
            for n in range(NB * PAGES // PG):
                s = n % 2
                if n >= 2:
                    act.wait_ge(k_used[s], n // 2)
                load_pages(act, c, kb[:, s, PG // 2:PG], d["slc_k"], n * PG + PG // 2, PG // 2, k_in[s])

        @block.gpsimd
        def _(pool):
            pool.memset(qz[:, :], 0.0).then_inc(cleared, 1)

        @block.vector
        def _(dve):
            dve.wait_ge(wk_in, 16)
            dve.tensor_copy(wk[:, :, :, WIN - 1], HT[:, WK_U:WK_U + 2, SEQ:T].rearrange("p g b -> p b g"))\
               .then_inc(patched, 1)
            dve.wait_ge(cleared, 1)
            v = qz[:, :].rearrange("p (b x) -> p b x", x=272)
            for g2 in range(2):
                rows = slice(g2 * HD, (g2 + 1) * HD)
                for g in range(GP):
                    at = g * 136 + g2
                    dve.tensor_copy(v[rows, :, at:at + 7:2], HT[rows, g * REP:(g + 1) * REP, SEQ:T]
                                    .rearrange("p r b -> p b r")).then_inc(q_in, 1)

        @block.tensor
        def _(pe):
            pe.wait_ge(loaded, 48)
            tab = tabs[:, 16:16 + P]
            for j in range(4):
                pe.matmul(psS[:, j, :], tab, oh[:, j * 512:(j + 1) * 512], start=True, stop=False, skip_group_check=True)
            pe.matmul(psW[:, :], tab, oh[:, PAST:PAST + WIN], start=True, stop=False, skip_group_check=True)
            pe.matmul(psM[:, 0:NBLK + 1], tab, oh[:, PAST + WIN:], start=True, stop=False, skip_group_check=True)
            pe.wait_ge(q_in, 4)
            pe.wait_ge(patched, 1)
            for b in range(NB):
                for g in range(GP):
                    last = b == NB - 1 and g == GP - 1
                    pe.matmul(psW[:, :], q_of(b, g), wk[:, b, g, :], start=False, stop=last, skip_group_check=True)
                    pe.matmul(psM[:, 0:NBLK], q_of(b, g),
                              kcT[:, b * PAGES * 4:(b + 1) * PAGES * 4].rearrange("p (n x) -> p n x", x=4)[:, :, 2 * g:2 * g + 2],
                              start=False, stop=last, skip_group_check=True)
                    pe.matmul(psM[:, NBLK:NBLK + 1], q_of(b, g), HT[:, SK_U + g, SEQ + b:SEQ + b + 1],
                              start=False, stop=last, skip_group_check=True)
            for n in range(NB * PAGES // PG):
                s, b = n % 2, n * PG // PAGES
                pe.wait_ge(k_in[s], 16 * PG * (n // 2 + 1))
                for j in range(PG // 4):
                    bank = (n * PG % PAGES) // 4 + j
                    for g in range(GP):
                        mm = pe.matmul(psS[:, bank, :], q_of(b, g), kb[:, s, 4 * j:4 * j + 4, g * P:(g + 1) * P],
                                       start=False, stop=(b == NB - 1 and g == GP - 1), skip_group_check=True)
                mm.then_inc(k_used[s], 1)


def sample_softmax(c, d, Ps, psS, psW, psM, consts):
    nc = c.nc
    Pslc, Pwin, Pcmp, Pnew = Ps
    bmask, gsum = consts
    with ExitStack() as ctx:
        sem = lambda n: nc.alloc_semaphore(f"sx_{n}")
        sb = lambda n, s: ctx.enter_context(nc.sbuf_tensor(f"sx_{n}", s, F32))
        ps_i = ctx.enter_context(nc.psum_tensor("sx_ps", [P, 512], F32))
        g = sb("gates", [P, 3])
        nm = sb("neg_max", [P, 4])
        sm = sb("sums", [P, 4])
        new_e = sb("new_e", [P, 2])
        pc = sb("cmp", [P, NBLK])
        pcg = sb("cmp_gated", [P, NBLK])
        score = sb("score", [P, NBLK + 1])
        top = sb("top", [P, 8])
        drop = sb("drop", [P, NBLK + 1])
        g_in, own_done, shifted, expd, cmp_ready, summed = [sem(n) for n in
            ("gates_in", "chain", "max_ready", "exp", "cmp_ready", "group_sums")]
        block = ctx.enter_context(nc.Block())

        @block.sync
        def _(sp):
            with nc.allow_non_contiguous_dma(reason="384 numbers"):
                for b in range(NB):
                    sp.dma_start(g[b * HEADS:(b + 1) * HEADS, :],
                                 d["gate_scratch"].rearrange("(r h) b -> b h r", r=3)[b]).then_inc(g_in, 16)

        @block.tensor
        def _(pe):
            pe.wait_ge(cmp_ready, 1)
            pe.matmul(ps_i[:, 0:NBLK], gsum[:, :], pc[:, :], start=True, stop=True).then_inc(summed, 1)

        @block.scalar
        def _(act):
            act.wait_ge(shifted, 1)
            act.activation(pc[:, :], psM[:, 0:NBLK], ACT.Exp, bias=nm[:, 0:1], accum_out=sm[:, 0:1]).then_inc(expd, 1)
            act.wait_ge(shifted, 2)
            act.activation(Pwin[:, :], psW[:, :], ACT.Exp, bias=nm[:, 1:2], accum_out=sm[:, 1:2]).then_inc(expd, 1)
            act.wait_ge(shifted, 3)
            act.activation(Pslc[:, :], Pslc[:, :], ACT.Exp, bias=nm[:, 2:3], accum_out=sm[:, 2:3]).then_inc(expd, 1)

        @block.vector
        def _(dve):
            own = Seq(dve, own_done)
            own.link(dve.tensor_reduce(nm[:, 0:1], psM[:, 0:NBLK], AX, ALU.max))
            dve.tensor_scalar(nm[:, 0:1], nm[:, 0:1], -1.0, None, ALU.mult).then_inc(shifted, 1)
            own.link(dve.tensor_reduce(nm[:, 1:2], psW[:, :], AX, ALU.max))
            dve.tensor_scalar(nm[:, 1:2], nm[:, 1:2], -1.0, None, ALU.mult).then_inc(shifted, 1)
            dve.wait_ge(expd, 1)
            own.link(dve.reciprocal(sm[:, 3:4], sm[:, 0:1]))
            dve.tensor_scalar(pc[:, :], pc[:, :], sm[:, 3:4], None, ALU.mult).then_inc(cmp_ready, 1)
            dve.wait_ge(g_in, 16 * NB)
            dve.wait_ge(cmp_ready, 1)
            own.link(dve.tensor_scalar(pcg[:, :], pc[:, :], g[:, 0:1], None, ALU.mult))
            for par in range(2):
                own(dve.tensor_tensor(Pcmp[:, par].rearrange("p (b n) -> p b n", b=NB),
                                      pcg[:, par:NBLK:2].unsqueeze(1).broadcast_to([P, NB, PAGES]),
                                      bmask[:, :].unsqueeze(2).broadcast_to([P, NB, PAGES]), ALU.mult))
            dve.wait_ge(summed, 1)
            own.link(dve.tensor_copy(score[:, 0:NBLK], ps_i[:, 0:NBLK]))
            own(dve.memset(score[:, 0:1], 1e4))
            own.link(dve.memset(score[:, NBLK - 1:NBLK + 1], 1e4))
            for r in range(2):
                own.link(dve.max(top[:, :], score[:, :]))
                own.link(dve.match_replace(score[:, :], top[:, :], score[:, :], NEG))
            own.link(dve.tensor_scalar(drop[:, :], score[:, :], FLOOR, NEG, ALU.is_gt, ALU.mult))
            own(dve.tensor_tensor(Pslc[:, 0:PAST].rearrange("p (n t) -> p n t", t=BLOCK),
                                  psS[:, :, :].rearrange("p a (n t) -> p (a n) t", t=BLOCK),
                                  drop[:, 0:NBLK].unsqueeze(2).broadcast_to([P, NBLK, BLOCK]), ALU.add))
            own.link(dve.tensor_tensor(Pslc[:, PAST:PAST + 1], psM[:, NBLK:NBLK + 1], drop[:, NBLK:NBLK + 1], ALU.add))
            own.link(dve.tensor_reduce(nm[:, 2:3], Pslc[:, :], AX, ALU.max))
            dve.tensor_scalar(nm[:, 2:3], nm[:, 2:3], -1.0, None, ALU.mult).then_inc(shifted, 1)
            dve.wait_ge(expd, 2)
            own.link(dve.reciprocal(sm[:, 1:2], sm[:, 1:2]))
            own.link(dve.tensor_tensor(sm[:, 1:2], sm[:, 1:2], g[:, 2:3], ALU.mult))
            own(dve.tensor_scalar(Pwin[:, :], Pwin[:, :], sm[:, 1:2], None, ALU.mult))
            dve.wait_ge(expd, 3)
            own.link(dve.reciprocal(sm[:, 2:3], sm[:, 2:3]))
            own.link(dve.tensor_tensor(sm[:, 2:3], sm[:, 2:3], g[:, 1:2], ALU.mult))
            own(dve.tensor_scalar(Pslc[:, :], Pslc[:, :], sm[:, 2:3], None, ALU.mult))


def sample_values(c, d, Ps, vcS, Vnew):
    nc = c.nc
    Pslc, Pwin, Pcmp, _ = Ps
    PG = 8
    turns = [Pslc[:, j * P:(j + 1) * P] for j in range(16)] + [Pwin[:, j * P:(j + 1) * P] for j in range(4)] + \
            [Pcmp[:, par, :] for par in range(2)]
    with ExitStack() as ctx:
        sem = lambda n: nc.alloc_semaphore(f"sv_{n}")
        sb = lambda n, s: ctx.enter_context(nc.sbuf_tensor(f"sv_{n}", s, F32))
        PT = sb("probsT", [P, len(turns), P])
        PTn = sb("probsT_new", [1, P])
        Vn = sb("v_new", [1, NB, 2 * P])
        wv = sb("win_v", [P, NB, 4, 2 * P])
        vb = sb("v_pages", [P, 2, PG, 2 * P])
        ps_t = [ctx.enter_context(nc.psum_tensor(f"sv_t{j}", [P, 512], F32)) for j in range(2)]
        po = ctx.enter_context(nc.psum_tensor("sv_o", [P, P], F32))
        vn_in, wv_in, patched, out_done, turned, moved, mixed, picked = [sem(n) for n in
            ("v_new_in", "win_in", "win_patched", "win_out", "turned", "moved", "mixed", "picked")]
        v_in = [sem(f"pages{s}_in") for s in range(2)]
        v_used = [sem(f"pages{s}_used") for s in range(2)]
        block = ctx.enter_context(nc.Block())
        rounds = (len(turns) + 4) // 4

        @block.sync
        def _(sp):
            sp.dma_start(wv[:, :, :, :], d["win_v"]).then_inc(wv_in, 16)
            for b in range(NB):
                sp.dma_start(Vn[0:1, b, :], Vnew[b:b + 1, 0:2 * P]).then_inc(vn_in, 16)
            sp.wait_ge(wv_in, 16)
            for b in range(NB):
                sp.dma_start(wv[P - 1:P, b, 3, :], Vnew[b:b + 1, 2 * P:4 * P]).then_inc(patched, 16)
            for n in range(NB * PAGES // PG):
                s = n % 2
                if n >= 2:
                    sp.wait_ge(v_used[s], n // 2)
                load_pages(sp, c, vb[:, s, 0:PG // 2], d["slc_v"], n * PG, PG // 2, v_in[s])
            sp.wait_ge(patched, 16 * NB)
            sp.dma_start(d["win_v_out"], wv[:, :, :, :]).then_inc(out_done, 16)
            sp.wait_ge(out_done, 16)

        @block.scalar
        def _(act):
            for n in range(NB * PAGES // PG):
                s = n % 2
                if n >= 2:
                    act.wait_ge(v_used[s], n // 2)
                load_pages(act, c, vb[:, s, PG // 2:PG], d["slc_v"], n * PG + PG // 2, PG // 2, v_in[s])

        @block.tensor
        def _(pe):
            for r in range(rounds):
                if r >= 2:
                    pe.wait_ge(moved, r - 1)
                for j in range(r * 4, min(r * 4 + 4, len(turns))):
                    mm = pe.transpose(ps_t[r % 2][:, (j % 4) * P:(j % 4 + 1) * P], turns[j], c.ident[:, :])
                if r == rounds - 1:
                    j = len(turns)
                    mm = pe.transpose(ps_t[r % 2][0:1, (j % 4) * P:(j % 4 + 1) * P], Pslc[:, PAST:PAST + 1], c.ident[:, :])
                mm.then_inc(turned, 1)
            pe.wait_ge(moved, rounds + 1)
            cols = lambda ap, g: ap.rearrange("p (b n) -> p b n", b=NB)[:, :, g * 8:(g + 1) * 8]
            first = True
            for g in range(GP):
                for par in range(2):
                    pe.matmul(cols(po[:, :], g), vcS[:, (g * 2 + par) * P:(g * 2 + par + 1) * P],
                              cols(PT[:, 20 + par, :], g), start=first, stop=False, skip_group_check=True)
                    first = False
            pe.wait_ge(vn_in, 16 * NB)
            pe.wait_ge(patched, 16 * NB)
            for b in range(NB):
                for g in range(GP):
                    q = slice(b * HEADS + g * 8, b * HEADS + g * 8 + 8)
                    for j in range(4):
                        pe.matmul(po[:, q], wv[:, b, j, g * P:(g + 1) * P], PT[:, 16 + j, q], start=False, stop=False,
                                  skip_group_check=True)
                    pe.matmul(po[:, q], Vn[0:1, b, g * P:(g + 1) * P], PTn[0:1, q], start=False, stop=False,
                              skip_group_check=True)
            for n in range(NB * PAGES // PG):
                s, b = n % 2, n * PG // PAGES
                pe.wait_ge(v_in[s], 16 * PG * (n // 2 + 1))
                for j in range(PG):
                    tile = (n * PG) % PAGES + j
                    for g in range(GP):
                        q = slice(b * HEADS + g * 8, b * HEADS + g * 8 + 8)
                        mm = pe.matmul(po[:, q], vb[:, s, j, g * P:(g + 1) * P], PT[:, tile, q], start=False,
                                       stop=(n == NB * PAGES // PG - 1 and j == PG - 1), skip_group_check=True)
                mm.then_inc(v_used[s], 1)

        @block.vector
        def _(dve):
            for r in range(rounds):
                dve.wait_ge(turned, r + 1)
                k = min(4, len(turns) - r * 4)
                dve.tensor_copy(PT[:, r * 4:r * 4 + k, :], ps_t[r % 2][:, 0:k * P].rearrange("p (k n) -> p k n", n=P))\
                   .then_inc(moved, 1)
                if r == rounds - 1:
                    j = len(turns) % 4
                    dve.tensor_copy(PTn[0:1, :], ps_t[r % 2][0:1, j * P:(j + 1) * P]).then_inc(moved, 1)
            n = NB * PAGES // PG
            dve.wait_ge(v_used[(n - 1) % 2], n // 2)
            for g2 in range(2):
                rows = slice(g2 * HD, (g2 + 1) * HD)
                dve.tensor_copy(c.XW[rows, :, SEQ:T],
                                po[rows, :].rearrange("p (b c g) -> p c b g", c=8, g=2)[:, :, :, g2]).then_inc(picked, 1)


def hgrn_gates(c, HT, d, K, L):
    nc = c.nc
    with ExitStack() as ctx:
        sem = lambda n: nc.alloc_semaphore(f"hg_{n}")
        sb = lambda n, s: ctx.enter_context(nc.sbuf_tensor(f"hg_{n}", s, F32))
        lg = sb("logits", [P, 2, HH])
        mx = sb("max", [P, HH])
        lb = sb("lb", [P, HH])
        om = sb("one_minus_lb", [P, HH])
        loaded, shifted, expd, sig, own_done, f_done, ln_done = [sem(n) for n in
            ("loaded", "shifted", "exp", "sigmoids", "chain", "f", "logs")]
        block = ctx.enter_context(nc.Block())

        @block.sync
        def _(sp):
            sp.dma_start(lg[:, :, :], d["lb_logits"]).then_inc(loaded, 16)

        @block.scalar
        def _(act):
            act.activation(HT[:, 8:16, :], HT[:, 8:16, :], ACT.Sigmoid).then_inc(sig, 1)
            act.activation(HT[:, 24:32, :], HT[:, 24:32, :], ACT.Sigmoid).then_inc(sig, 1)
            act.activation(HT[:, 0:8, :], HT[:, 0:8, :], ACT.Silu).then_inc(sig, 1)
            act.wait_ge(shifted, 1)
            act.activation(lg[:, :, :], lg[:, :, :], ACT.Exp).then_inc(expd, 1)
            act.wait_ge(f_done, HH)
            act.activation(L[:, :, :], HT[:, 8:16, :], ACT.Ln).then_inc(ln_done, 1)

        @block.vector
        def _(dve):
            own = Seq(dve, own_done)
            dve.wait_ge(loaded, 16)
            own.link(dve.tensor_tensor(mx[:, :], lg[:, 0, :], lg[:, 1, :], ALU.max))
            dve.tensor_tensor(lg[:, :, :], lg[:, :, :], mx[:, :].unsqueeze(1).broadcast_to([P, 2, HH]),
                              ALU.subtract).then_inc(shifted, 1)
            dve.wait_ge(expd, 1)
            own.link(dve.tensor_tensor(mx[:, :], lg[:, 0, :], lg[:, 1, :], ALU.add))
            own.link(dve.reciprocal(mx[:, :], mx[:, :]))
            own.link(dve.tensor_tensor(lg[:, :, :], lg[:, :, :], mx[:, :].unsqueeze(1).broadcast_to([P, 2, HH]), ALU.mult))
            own.link(dve.tensor_tensor(lb[:, :], lg[:, 0, :], lg[:, 1, :], ALU.add))
            own.link(dve.tensor_tensor(lb[:, :], lb[:, :], lg[:, 0, :], ALU.subtract))
            own.link(dve.tensor_scalar(om[:, :], lb[:, :], -1.0, 1.0, ALU.mult, ALU.add))
            dve.wait_ge(sig, 1)
            for h in range(HH):
                dve.tensor_scalar(HT[:, 8 + h, :], HT[:, 8 + h, :], om[:, h:h + 1], lb[:, h:h + 1], ALU.mult, ALU.add)\
                   .then_inc(f_done, 1)
            dve.wait_ge(f_done, HH)
            own(dve.tensor_scalar(K[:, :, :], HT[:, 8:16, :], -1.0, 1.0, ALU.mult, ALU.add))


def hgrn_prompt(c, HT, d, K, L):
    nc = c.nc
    fine = [16, 8, 4, 2, 1, 0]
    with ExitStack() as ctx:
        sem = lambda n: nc.alloc_semaphore(f"hp_{n}")
        sb = lambda n, s, t=F32: ctx.enter_context(nc.sbuf_tensor(f"hp_{n}", s, t))
        q, k, v, G = [sb(n, [P, SEQ]) for n in ("q", "k", "v", "G")]
        reset = sb("reset", [P, SEQ])
        Dl = [sb(f"diff{j}", [P, SEQ]) for j in range(2)]
        M = {m: sb(f"m{m}", [P, SEQ]) for m in LEVELS + [1]}
        eG, ke = sb("eG", [P, SEQ]), sb("ke", [P, SEQ])
        qe = sb("qe", [P, SEQ])
        vt, kt = sb("v_tok", [P, SEQ]), sb("ke_tok", [P, SEQ])
        A = sb("A", [P, SEQ])
        masks = sb("masks", [P, len(fine), P], I32)
        S = [sb(f"S{j}", [P, P]) for j in range(2)]
        Sout = sb("S_out", [P, HH, P])
        ps_a = ctx.enter_context(nc.psum_tensor("hp_a", [P, 512], F32))
        ps_f = [ctx.enter_context(nc.psum_tensor(f"hp_f{j}", [P, 512], F32)) for j in range(2)]
        ps_t = [ctx.enter_context(nc.psum_tensor(f"hp_t{j}", [P, 512], F32)) for j in range(2)]
        ps_o = ctx.enter_context(nc.psum_tensor("hp_o", [P, 512], F32))
        ps_s = ctx.enter_context(nc.psum_tensor("hp_s", [P, 512], F32))
        const_in, cleared, staged, own_done, diff, expd, mult, turned, turned_out, coarse, coarse_out, fine_done, \
            fine_out, s_new, s_out, o_done, o_out, saved = [sem(n) for n in
            ("const_in", "cleared", "staged", "chain", "diffs", "exps", "products", "turned", "turned_out", "coarse",
             "coarse_out", "fine", "fine_out", "state_products", "states", "outputs", "outputs_out", "saved")]
        block = ctx.enter_context(nc.Block())
        waited = sem("waited")
        tiles = lambda a: a.rearrange("p (i t) -> p i t", i=TILES)
        NL = len(LEVELS)
        NE = NL + 2

        @block.sync
        def _(sp):
            sp.dma_start(masks[:, :, :], d["level_masks"]).then_inc(const_in, 16)
            sp.dma_start(reset[:, :], d["tile_reset"]).then_inc(const_in, 16)
            sp.wait_ge(s_out, HH * TILES)
            sp.dma_start(d["hgrn_p_out"], Sout[:, :, :]).then_inc(saved, 16)
            sp.wait_ge(saved, 16)

        @block.gpsimd
        def _(pool):
            pool.memset(A[:, :], 0.0).then_inc(cleared, 1)
            pool.sem_inc(o_out, 1)
            with pool.Fori(0, HH) as h:
                pool.wait_ge(o_out, h + 1)
                own = Seq(pool, staged, h * 3)
                for dst, src, at in ((q, HT, 0), (k, K, 0), (v, HT, 16)):
                    own.link(pool.tensor_copy(dst[:, :], src[:, bass.ds(h + at, 1), 0:SEQ].rearrange("p o t -> p (o t)")))

        def halves(a, m):
            b = a.rearrange("p (n two m) -> p n two m", two=2, m=m)
            return b[:, :, 0, :], b[:, :, 1, :]

        @block.vector
        def _(dve):
            dve.wait_ge(const_in, 32)
            with dve.Fori(0, HH) as h:
                own = Seq(dve, own_done, h * 1)
                dve.wait_ge(o_out, h + 1)
                own.link(dve.tensor_tensor_scan(G[:, :], reset[:, :], L[:, bass.ds(h, 1), 0:SEQ]
                                                .rearrange("p o t -> p (o t)"), 0.0, ALU.mult, ALU.add))
                dve.wait_ge(staged, h * 3 + 3)

                def diffs(n):
                    dl = Dl[n % 2]
                    if n < NL:
                        m = LEVELS[n]
                        g0, g1 = halves(G[:, :], m)
                        d0, d1 = halves(dl[:, :], m)
                        ref = g0[:, :, m - 1:m].broadcast_to([P, SEQ // (2 * m), m])
                        dve.tensor_tensor(d0, ref, g0, ALU.subtract).then_inc(diff, 1)
                        dve.tensor_tensor(d1, g1, ref, ALU.subtract).then_inc(diff, 1)
                    else:
                        end = tiles(G[:, :])[:, :, P - 1:P].broadcast_to([P, TILES, P])
                        dve.tensor_tensor(tiles(dl[:, :]), end, tiles(G[:, :]), ALU.subtract).then_inc(diff, 1)

                def mults(n):
                    dl = Dl[n % 2]
                    dve.wait_ge(expd, h * NE + (n + 1))
                    if n < NL:
                        m = LEVELS[n]
                        d0, d1 = halves(dl[:, :], m)
                        m0, m1 = halves(M[m][:, :], m)
                        dve.tensor_tensor(m0, d0, halves(k[:, :], m)[0], ALU.mult).then_inc(mult, 1)
                        dve.tensor_tensor(m1, d1, halves(q[:, :], m)[1], ALU.mult).then_inc(mult, 1)
                    else:
                        dve.tensor_tensor(ke[:, :], dl[:, :], k[:, :], ALU.mult).then_inc(mult, 1)

                diffs(0)
                for n in range(NL + 1):
                    if n + 1 <= NL:
                        if n + 1 >= 2:
                            dve.wait_ge(mult, h * (2 * NL + 4) + 2 * n)
                        diffs(n + 1)
                    mults(n)
                m0, m1 = halves(M[1][:, :], 1)
                dve.tensor_copy(m0, halves(k[:, :], 1)[0]).then_inc(mult, 1)
                dve.tensor_tensor(m1, halves(q[:, :], 1)[1],
                                  HT[:, bass.ds(h + 8, 1), 1:SEQ:2].rearrange("p o t -> p (o t)").unsqueeze(2),
                                  ALU.mult).then_inc(mult, 1)
                dve.wait_ge(expd, h * NE + NE)
                dve.tensor_tensor(qe[:, :], eG[:, :], q[:, :], ALU.mult).then_inc(mult, 1)
                dve.wait_ge(turned, h * 2 + 1)
                dve.tensor_copy(vt[:, :], ps_t[0][:, :]).then_inc(turned_out, 1)
                for n in range(len(fine)):
                    dve.wait_ge(cleared, 1)
                    dve.wait_ge(fine_done, h * len(fine) + (n + 1))
                    if n == 0:
                        dve.wait_ge(coarse_out, h * 3 + 3)
                    if n:
                        dve.wait_ge(fine_out, h * len(fine) + n)
                    dve.sem_inc(waited, 1)
                    dve.copy_predicated(tiles(A[:, :]), masks[:, n, :].unsqueeze(1).broadcast_to([P, TILES, P]),
                                        tiles(ps_f[n % 2][:, :])).then_inc(fine_out, 1)
                dve.wait_ge(turned, h * 2 + 2)
                dve.tensor_copy(kt[:, :], ps_t[1][:, :]).then_inc(turned_out, 1)
                for i in range(TILES):
                    dve.wait_ge(s_new, h * TILES + (i + 1))
                    dst = S[(i + 1) % 2][:, :] if i < TILES - 1 else Sout[:, bass.ds(h, 1), :].rearrange("p o n -> p (o n)")
                    if i == 0:
                        dve.tensor_copy(dst, ps_s[:, 0:P]).then_inc(s_out, 1)
                    else:
                        dve.wait_ge(s_out, h * TILES + i)
                        dve.scalar_tensor_tensor(dst, S[i % 2][:, :], eG[:, (i + 1) * P - 1:(i + 1) * P],
                                                 ps_s[:, 0:P], ALU.mult, ALU.add).then_inc(s_out, 1)

        @block.scalar
        def _(act):
            with act.Fori(0, HH) as h:
                for n in range(NL + 1):
                    act.wait_ge(diff, h * (2 * NL + 1) + (2 * (n + 1) if n < NL else 2 * NL + 1))
                    act.activation(Dl[n % 2][:, :], Dl[n % 2][:, :], ACT.Exp).then_inc(expd, 1)
                act.activation(eG[:, :], G[:, :], ACT.Exp).then_inc(expd, 1)
                act.wait_ge(coarse, h + 1)
                act.wait_ge(cleared, 1)
                A4, a4 = tiles(A[:, :]), tiles(ps_a[:, :])
                for r0, r1, t0, t1 in ((0, 64, 64, 128), (0, 32, 32, 64), (64, 96, 96, 128)):
                    act.activation(A4[r0:r1, :, t0:t1], a4[r0:r1, :, t0:t1], ACT.Copy).then_inc(coarse_out, 1)
                act.wait_ge(o_done, h + 1)
                act.activation(c.XW[:, bass.ds(h, 1), 0:SEQ].rearrange("p o t -> p (o t)"), ps_o[:, :], ACT.Copy)\
                   .then_inc(o_out, 1)

        @block.tensor
        def _(pe):
            with pe.Fori(0, HH) as h:
                pe.wait_ge(staged, h * 3 + 3)
                for i in range(TILES):
                    mm = pe.transpose(ps_t[0][:, i * P:(i + 1) * P], v[:, i * P:(i + 1) * P], c.ident[:, :])
                mm.then_inc(turned, 1)
                base = h * (2 * NL + 4)
                for n, m in enumerate((64, 32)):
                    pe.wait_ge(mult, base + 2 * (n + 1))
                    for i in range(TILES):
                        for b in range(P // (2 * m)):
                            s0 = b * 2 * m
                            mm = pe.matmul(ps_a[s0:s0 + m, i * P + s0 + m:i * P + s0 + 2 * m],
                                           M[m][:, i * P + s0:i * P + s0 + m],
                                           M[m][:, i * P + s0 + m:i * P + s0 + 2 * m], start=True, stop=True)
                mm.then_inc(coarse, 1)
                for n, m in enumerate(fine):
                    pe.wait_ge(mult, base + (2 * (n + 3) if m > 1 else 2 * NL + 3))
                    if n >= 2:
                        pe.wait_ge(fine_out, h * len(fine) + (n - 1))
                    a, b = (M[m], M[m]) if m else (k, q)
                    for i in range(TILES):
                        mm = pe.matmul(ps_f[n % 2][:, i * P:(i + 1) * P], a[:, i * P:(i + 1) * P],
                                       b[:, i * P:(i + 1) * P], start=True, stop=True)
                    mm.then_inc(fine_done, 1)
                for i in range(TILES):
                    mm = pe.transpose(ps_t[1][:, i * P:(i + 1) * P], ke[:, i * P:(i + 1) * P], c.ident[:, :])
                mm.then_inc(turned, 1)
                pe.wait_ge(mult, base + 2 * NL + 4)
                pe.wait_ge(turned_out, h * 2 + 2)
                pe.wait_ge(fine_out, h * len(fine) + len(fine))
                pe.wait_ge(coarse_out, h * 3 + 3)
                for i in range(TILES):
                    t = slice(i * P, (i + 1) * P)
                    if i:
                        pe.wait_ge(s_out, h * TILES + i)
                    pe.matmul(ps_s[:, 0:P], kt[:, t], vt[:, t], start=True, stop=True).then_inc(s_new, 1)
                    mm = pe.matmul(ps_o[:, t], vt[:, t], A[:, t], start=True, stop=i == 0)
                    if i:
                        mm = pe.matmul(ps_o[:, t], S[i % 2][:, :], qe[:, t], start=False, stop=True)
                mm.then_inc(o_done, 1)


def hgrn_sample(c, HT, d, K):
    nc = c.nc
    with ExitStack() as ctx:
        sem = lambda n: nc.alloc_semaphore(f"hs_{n}")
        sb = lambda n, s: ctx.enter_context(nc.sbuf_tensor(f"hs_{n}", s, F32))
        S0 = sb("state", [P, NB, HH, P])
        rows = sb("rows", [NB, 2, HH, P])
        vm = sb("v_masked", [NB, 2, NB, P])
        eye = sb("eye", [NB, NB])
        ps_t = ctx.enter_context(nc.psum_tensor("hs_t", [NB, 2, HH, P], F32))
        ps_k = ctx.enter_context(nc.psum_tensor("hs_k", [P, NB, P], F32))
        ps_o = ctx.enter_context(nc.psum_tensor("hs_o", [P, HH, NB], F32))
        loaded, turned, own_done, masked, outer, stepped, mixed, picked, saved = [sem(n) for n in
            ("loaded", "turned", "chain", "v_masked", "outer", "stepped", "mixed", "picked", "saved")]
        block = ctx.enter_context(nc.Block())

        @block.sync
        def _(sp):
            sp.dma_start(S0[:, :, :, :], d["state_hgrn"]).then_inc(loaded, 16)
            sp.wait_ge(stepped, HH)
            sp.dma_start(d["hgrn_s_out"], S0[:, :, :, :]).then_inc(saved, 16)
            sp.wait_ge(saved, 16)

        @block.tensor
        def _(pe):
            for h in range(HH):
                pe.transpose(ps_t[:, 0, h, :], K[:, h, SEQ:T], c.ident[:, :])
                mm = pe.transpose(ps_t[:, 1, h, :], HT[:, 16 + h, SEQ:T], c.ident[:, :])
            mm.then_inc(turned, 1)
            for h in range(HH):
                pe.wait_ge(masked, h + 1)
                if h:
                    pe.wait_ge(stepped, h)
                for j in range(2):
                    mm = pe.matmul(ps_k[:, 4 * j:4 * j + 4, :], rows[:, 0, h, :], vm[:, h % 2, 4 * j:4 * j + 4, :],
                                   start=True, stop=True)
                mm.then_inc(outer, 1)
            pe.wait_ge(stepped, HH)
            for h in range(HH):
                for b in range(NB):
                    mm = pe.matmul(ps_o[:, h, b:b + 1], S0[:, b, h, :], HT[:, h, SEQ + b:SEQ + b + 1], start=True, stop=True)
            mm.then_inc(mixed, 1)

        @block.vector
        def _(dve):
            own = Seq(dve, own_done)
            dve.wait_ge(turned, 1)
            own.link(dve.tensor_copy(rows[:, :, :, :], ps_t[:, :, :, :]))
            dve.wait_ge(loaded, 16)
            for h in range(HH):
                if h >= 2:
                    dve.wait_ge(outer, h - 1)
                dve.tensor_tensor(vm[:, h % 2], rows[:, 1, h, :].unsqueeze(1).broadcast_to([NB, NB, P]),
                                  c.ident[0:NB, 0:NB].unsqueeze(2).broadcast_to([NB, NB, P]), ALU.mult).then_inc(masked, 1)
                own.link(dve.tensor_tensor(S0[:, :, h, :], S0[:, :, h, :],
                                           HT[:, 8 + h, SEQ:T].unsqueeze(2).broadcast_to([P, NB, P]), ALU.mult))
                dve.wait_ge(outer, h + 1)
                dve.tensor_tensor(S0[:, :, h, :], S0[:, :, h, :], ps_k[:, :, :], ALU.add).then_inc(stepped, 1)
            dve.wait_ge(mixed, 1)
            dve.tensor_copy(c.XW[:, :, SEQ:T], ps_o[:, :, :]).then_inc(picked, 1)


def hgrn_norm(c, HT, sq, R, onw):
    nc = c.nc
    with ExitStack() as ctx:
        sem = lambda n: nc.alloc_semaphore(f"hn_{n}")
        ps = [ctx.enter_context(nc.psum_tensor(f"hn_ps{j}", [P, 2, 512], F32)) for j in range(2)]
        squared, summed, mean_in, rooted, own_done = [sem(n) for n in ("squares", "sums", "means", "roots", "chain")]
        block = ctx.enter_context(nc.Block())

        @block.tensor
        def _(pe):
            for h in range(HH):
                pe.wait_ge(squared, h + 1)
                if h >= 2:
                    pe.wait_ge(mean_in, h - 1)
                for x in range(2):
                    mm = pe.matmul(ps[h % 2][:, x, 0:TH], c.ones[:, :], sq[:, h, x * TH:(x + 1) * TH], start=True, stop=True)
                mm.then_inc(summed, 1)

        @block.scalar
        def _(act):
            for h in range(HH):
                act.activation(sq[:, h, :], c.XW[:, h, :], ACT.Square).then_inc(squared, 1)
            for h in range(HH):
                act.wait_ge(mean_in, h + 1)
                act.activation(R[:, h, :], R[:, h, :], ACT.Sqrt).then_inc(rooted, 1)

        @block.vector
        def _(dve):
            own = Seq(dve, own_done)
            for h in range(HH):
                dve.wait_ge(summed, h + 1)
                dve.tensor_scalar(pairs(R[:, h, :]), ps[h % 2][:, :, 0:TH], 1.0 / P, EPS, ALU.mult, ALU.add)\
                   .then_inc(mean_in, 1)
            for h in range(HH):
                dve.wait_ge(rooted, h + 1)
                own.link(dve.reciprocal(R[:, h, :], R[:, h, :]))
                own.link(dve.scalar_tensor_tensor(c.XW[:, h, :], c.XW[:, h, :], onw[:, 0:1], R[:, h, :], ALU.mult, ALU.mult))
                own(dve.tensor_tensor(c.XW[:, h, :], c.XW[:, h, :], HT[:, 24 + h, :], ALU.mult))


def program(nc, d):
    with ExitStack() as top:
        c = Core(nc, top)
        c.pages = top.enter_context(nc.sbuf_tensor("pages", [1, NB * PAGES], I32))
        onw = top.enter_context(nc.sbuf_tensor("hgrn_norm_w", [P, 1], F32))
        loaded = top.enter_context(nc.semaphore("setup_loaded"))
        with nc.Block() as block:
            @block.sync
            def _(sp):
                for dst, src in ((c.X[:, :, :], "x"), (c.nw[:, :, :, :], "norm_w"), (c.ident[:, :], "ident"),
                                 (c.pages[:, :], "page_table"), (onw[:, :], "hgrn_norm_w")):
                    sp.dma_start(dst, d[src]).then_inc(loaded, 16)
                for s in range(RING):
                    load_tile(sp, c, d["nsa_w_in"], s, s, KC)
                sp.wait_ge(loaded, 80)

            @block.gpsimd
            def _(pool):
                pool.memset(c.ones[:, :], 1.0)
                for s in range(RING):
                    pool.sem_inc(c.psum_free[s], 1)
        c.loads = [1] * RING

        def swiglu(layer, nxt):
            with ExitStack() as ctx:
                Hh, Hl = [ctx.enter_context(nc.sbuf_tensor(f"ffn{layer}_h_{n}", [P, FF, T], F32R)) for n in ("hi", "lo")]
                with ExitStack() as inner:
                    sb = lambda n, s: inner.enter_context(nc.sbuf_tensor(f"ffn{layer}_{n}", s, F32))
                    a_t, g_t, prod = sb("a", [P, 2, T]), sb("g", [P, 2, T]), sb("product", [P, T])
                    sems = ([nc.alloc_semaphore(f"ffn{layer}_silu{m}") for m in range(2)],
                            nc.alloc_semaphore(f"ffn{layer}_made"),
                            [nc.alloc_semaphore(f"ffn{layer}_used{m}") for m in range(2)])
                    linear(c, f"gu{layer}", d[f"w_gu{layer}"], 2 * FF, 1, KC, c.X,
                           evac_swiglu(c, Hh, Hl, a_t, g_t, prod, sems), (d[f"w_down{layer}"], SUBK), c.nw[:, layer, 2])
                mixed_and_normed(f"down{layer}", d[f"w_down{layer}"], 2, SUBK, (Hh, Hl), nxt, c.nw[:, layer, 3],
                                 layer == 0)

        def mixed_and_normed(name, w, subs, kcs, src, nxt, w_post, pre):
            with ExitStack() as ctx:
                Y = ctx.enter_context(nc.sbuf_tensor(f"{name}_y", [P, KC, T], F32))
                ssq = ctx.enter_context(nc.sbuf_tensor(f"{name}_ssq", [P, T], F32))
                with ExitStack() as inner:
                    sq = inner.enter_context(nc.sbuf_tensor(f"{name}_sq", [P, T], F32))
                    sems = [nc.alloc_semaphore(f"{name}_{n}") for n in ("squared", "added")]
                    linear(c, name, w, KC, subs, kcs, src, evac_squares(c, Y, sq, ssq, sems, RING // subs), nxt)
                norm_step(c, f"{name}_norm", ssq, (Y, w_post), pre)

        with ExitStack() as nsa:
            nsa.enter_context(nc.cleanup_on_exit())
            sb = lambda n, s: nsa.enter_context(nc.sbuf_tensor(n, s, F32))
            norm_step(c, "in_norm")
            HT = sb("HT", [P, NSA_UNITS, T])
            kcT = sb("kcT", [P, NB * PAGES * 4])
            kcBD = sb("kcBD", [P, GP, 2, PBLK])
            vcS = sb("vcS", [P, 4 * P])
            Vnew = sb("Vnew", [NB, 4 * P])
            BDv = sb("BDv", [P, 8, 2, HD])
            with ExitStack() as cm:
                rows = cm.enter_context(nc.sbuf_tensor("cmp_rows", [P, 2, PAGES_A_CHUNK, 256], F32))
                first_in = nc.alloc_semaphore("cmp_first_rows_loaded")

                def first_chunks(sp, step):
                    flat = rows[:, :, :, :].rearrange("p a g n -> p (a g) n")
                    for x in range(4):
                        page = sp.value_load(c.pages[0:1, bass.ds(step * 4 + x, 1)], min_val=0, max_val=POOL - 1)
                        sp.dma_start(flat[:, bass.ds(step * 4 + x, 1), :].rearrange("p o n -> p (o n)"),
                                     d["cache_cmp"][0, bass.ds(page, 1)].rearrange("o p n -> p (o n)"))\
                          .then_inc(first_in, 16)

                linear(c, "nsa_in", d["nsa_w_in"], NSA_UNITS, 1, KC, c.X, evac_scaled(c, HT), (d["nsa_w_out"], KC),
                       c.nw[:, 0, 0], beside=first_chunks)
                compress(c, HT, d, rows, first_in, kcT, kcBD, vcS, BDv)
            tabs = sb("tabs", [N_BUCKETS + 1, 16 + P])
            c.XW = sb("attention_out", [P, KC, T])
            with ExitStack() as pr:
                sp_ = lambda n, s: pr.enter_context(nc.sbuf_tensor(n, s, F32))
                Otok = sp_("Otok", [P, TILES, D_MODEL])
                Vtok = sp_("Vtok", [P, TILES, 4 * P])
                gT = sp_("gT", [P, TILES, 48])
                T_bias = sp_("T_bias", [P, HEADS, SEQ])
                with ExitStack() as bc:
                    biasC = bc.enter_context(nc.sbuf_tensor("biasC", [P, TILES, HEADS, PBLK], F32))
                    attention_setup(c, HT, d, tabs, T_bias, biasC, Vtok, gT, Vnew)
                    prompt_compressed(c, HT, kcBD, BDv, biasC, gT, Otok)
                prompt_attention(c, HT, T_bias, Vtok, gT, Otok)
                turn_outputs(c, Otok)
            with ExitStack() as sa:
                ss = lambda n, s: sa.enter_context(nc.sbuf_tensor(n, s, F32))
                Ps = (ss("Pslc", [P, PAST + 1]), ss("Pwin", [P, WIN]), ss("Pcmp", [P, 2, P]), None)
                bmask, gsum = ss("bmask", [P, NB]), ss("gsum", [P, P])
                with ExitStack() as pp:
                    psS = pp.enter_context(nc.psum_tensor("psS", [P, 4, 512], F32))
                    psW = pp.enter_context(nc.psum_tensor("psW", [P, 512], F32))
                    psM = pp.enter_context(nc.psum_tensor("psM", [P, 512], F32))
                    sample_scores(c, HT, d, tabs, kcT, psS, psW, psM, (bmask, gsum))
                    sample_softmax(c, d, Ps, psS, psW, psM, (bmask, gsum))
                sample_values(c, d, Ps, vcS, Vnew)
            mixed_and_normed("nsa_out", d["nsa_w_out"], 1, KC, c.XW, (d["w_gu0"], KC), c.nw[:, 0, 1], True)
        with nc.cleanup_on_exit():
            swiglu(0, (d["hgrn_w_in"], KC))
        with ExitStack() as hg:
            hg.enter_context(nc.cleanup_on_exit())
            sb = lambda n, s: hg.enter_context(nc.sbuf_tensor(n, s, F32))
            HT = sb("HT2", [P, HGRN_UNITS, T])
            linear(c, "hgrn_in", d["hgrn_w_in"], HGRN_UNITS, 1, KC, c.X, evac_scaled(c, HT), (d["hgrn_w_out"], KC),
                   c.nw[:, 1, 0])
            c.XW = sb("mixer_out", [P, KC, T])
            with ExitStack() as kl:
                K = kl.enter_context(nc.sbuf_tensor("K", [P, HH, T], F32))
                L = kl.enter_context(nc.sbuf_tensor("L", [P, HH, T], F32))
                hgrn_gates(c, HT, d, K, L)
                hgrn_prompt(c, HT, d, K, L)
                hgrn_sample(c, HT, d, K)
                hgrn_norm(c, HT, K, L, onw)
            mixed_and_normed("hgrn_out", d["hgrn_w_out"], 1, KC, c.XW, (d["w_gu1"], KC), c.nw[:, 1, 1], True)
        with nc.cleanup_on_exit():
            swiglu(1, None)
        out_done = top.enter_context(nc.semaphore("y_out"))
        with nc.Block() as block:
            @block.sync
            def _(sp):
                sp.dma_start(d["y"], c.X[:, :, :]).then_inc(out_done, 16)
                sp.wait_ge(out_done, 16)



def bucket(n):
    n = np.asarray(n)
    m = N_BUCKETS // 2
    nf = np.maximum(n, 1).astype(np.float32)
    r = np.log(nf / np.float32(m)).astype(np.float32) / np.float32(np.log(MAX_DISTANCE / m))
    large = m + (r * np.float32(N_BUCKETS - m)).astype(np.int32)
    return np.where(n < 0, -1, np.where(n < m, n, np.minimum(large, N_BUCKETS - 1)))


def onehot(n):
    b = bucket(n)
    b = np.where(b < 0, N_BUCKETS, b)
    return (np.arange(N_BUCKETS + 1)[:, None] == b[None, :]).astype(np.float32)


def unit_tiles(w, subs, kcs):
    K, N = w.shape
    a = w.reshape(subs, kcs, P, N // P, P)
    return np.ascontiguousarray(a.transpose(3, 0, 2, 1, 4).reshape(N // P * subs, P, kcs * P))


def shape_constants():
    s = np.arange(P)
    out = {
        "ident": np.eye(P, dtype=np.float32),
        "onehot_rows": np.ascontiguousarray(np.stack([onehot(511 - np.arange(1024)), onehot(np.arange(1024) - 511)], 1)),
        "onehot_sample": np.concatenate([onehot(PAST - np.arange(PAST)), onehot(WIN - 1 - np.arange(WIN)),
                                         onehot(PAST - (BLOCK * np.arange(NBLK) + BLOCK - 1)), onehot([0])], 1),
        "head_mask": np.kron(np.eye(16, dtype=np.float32), np.ones((PBLK, 1), np.float32)),
        "batch_mask": np.kron(np.eye(NB, dtype=np.float32), np.ones((HEADS, 1), np.float32)),
        "tile_reset": np.ascontiguousarray(np.broadcast_to((np.arange(SEQ) % P != 0).astype(np.float32), (P, SEQ))),
    }
    h = np.arange(P)
    key = (h // HEADS) * 100 + (h % HEADS // 8) * 10 + h % 2
    out["group_sum"] = (key[:, None] == key[None, :]).astype(np.float32)
    masks = []
    for m in (16, 8, 4, 2, 1):
        masks.append((s[:, None] // (2 * m) == s[None, :] // (2 * m)) & (s[:, None] % (2 * m) < m)
                     & (s[None, :] % (2 * m) >= m))
    masks.append(s[:, None] == s[None, :])
    out["level_masks"] = np.ascontiguousarray(np.stack(masks, 1).astype(np.int32))
    return out


def kernel(x_prompt, x_sample, cache_cmp_kv, cache_slc_kv, state_win_kv, state_hgrn, page_table, norm_w, nsa_w_in,
           nsa_w_out, nsa_cmp_pe, nsa_cmp_w1, nsa_cmp_w2, rel_bias, hgrn_w_in, hgrn_w_out, hgrn_norm_w,
           hgrn_lb_logits, ffn_w_gu, ffn_w_down):
    import concourse.bacc as bacc
    from concourse.bass_utils import run_bass_kernel_spmd

    A = lambda a: np.asarray(a)
    C = np.ascontiguousarray
    a = shape_constants()
    x = np.concatenate([A(x_prompt)[0], A(x_sample)[:, 0]], 0)
    a["x"] = C(x.T.reshape(KC, P, T).transpose(1, 0, 2))
    a["norm_w"] = C(A(norm_w).reshape(2, 4, KC, P).transpose(3, 0, 1, 2))
    a["page_table"] = A(page_table).reshape(1, NB * PAGES)
    a["hgrn_norm_w"] = C(A(hgrn_norm_w)[0].reshape(P, 1))
    w = A(nsa_w_in)[0]
    nq, nkv = HEADS * HD, 6 * KVH * HD
    wq = w[:, :nq].reshape(D_MODEL, GP, 2, REP, HD).transpose(0, 1, 3, 2, 4).reshape(D_MODEL, nq)
    wg = w[:, nq + nkv:].reshape(D_MODEL, 3, GP, 2, REP).transpose(0, 1, 2, 4, 3).reshape(D_MODEL, 48)
    w = np.concatenate([wq, w[:, nq:nq + nkv], wg, np.zeros((D_MODEL, 80), np.float32)], 1)
    a["nsa_w_in"] = unit_tiles(w, 1, KC)
    wo = A(nsa_w_out)[0].reshape(GP, 2, REP, HD, D_MODEL).transpose(0, 2, 1, 3, 4).reshape(nq, D_MODEL)
    a["nsa_w_out"] = unit_tiles(wo, 1, KC)
    a["hgrn_w_in"] = unit_tiles(A(hgrn_w_in)[0], 1, KC)
    a["hgrn_w_out"] = unit_tiles(A(hgrn_w_out)[0], 1, KC)
    for l in range(2):
        gu = A(ffn_w_gu)[l].reshape(D_MODEL, 2, FF, P).transpose(0, 2, 1, 3).reshape(D_MODEL, 2 * D_FF)
        a[f"w_gu{l}"] = unit_tiles(gu, 1, KC)
        a[f"w_down{l}"] = unit_tiles(A(ffn_w_down)[l], 2, SUBK)
    cc = A(cache_cmp_kv)[0].reshape(POOL, P, 2, GP, 2, HD)
    a["cache_cmp"] = C(cc.transpose(2, 0, 4, 5, 3, 1).reshape(2, POOL, P, GP * P))
    cs = A(cache_slc_kv)[0].reshape(POOL, P, 2, GP, 2, HD)
    a["slc_k"] = C(cs[:, :, 0].transpose(0, 3, 4, 2, 1).reshape(POOL, P, GP * P))
    a["slc_v"] = C(cs[:, :, 1].reshape(POOL, P, 2 * P))
    sw = np.roll(A(state_win_kv)[0], -1, axis=1)
    sw = sw.reshape(NB, WIN, 2, GP, 2, HD)
    a["win_k"] = C(sw[:, :, 0].transpose(3, 4, 0, 2, 1).reshape(P, NB, GP, WIN))
    a["win_v"] = C(sw[:, :, 1].reshape(NB, 4, P, 2 * P).transpose(2, 0, 1, 3))
    w1 = A(nsa_cmp_w1)[0].reshape(2, 2, 32, HD, HD)
    bd = np.zeros((2, 2, 2, HD, 32, 2, HD), np.float32)
    w2 = np.zeros((2, HD, 2, 2, HD), np.float32)
    for g in range(2):
        bd[:, :, g, :, :, g, :] = w1.transpose(0, 1, 3, 2, 4)
        w2[g, :, :, g, :] = A(nsa_cmp_w2)[0].transpose(1, 0, 2)
    a["cmp_w1"] = bd.reshape(2, 2, P, 32 * P)
    a["cmp_w2"] = w2.reshape(P, 2, P)
    pe = A(nsa_cmp_pe)[0].transpose(2, 0, 1)
    a["cmp_pe"] = C(np.concatenate([pe, pe], 0))
    tab = np.concatenate([A(rel_bias).reshape(N_BUCKETS, GP, 2, REP).transpose(0, 1, 3, 2).reshape(N_BUCKETS, 16),
                          np.full((1, 16), NEG, np.float32)], 0)
    a["tabs"] = C(np.concatenate([tab] * (NB + 1), 1))
    a["lb_logits"] = C(A(hgrn_lb_logits).reshape(2, HH, P).transpose(2, 0, 1))
    a["state_hgrn"] = C(A(state_hgrn)[0].transpose(2, 0, 1, 3))

    nc = bacc.Bacc("TRN2", target_bir_lowering=False, num_devices=1)
    d = {n: nc.dram_tensor(f"in_{n}", v.shape, mybir.dt.from_np(v.dtype), kind="ExternalInput").ap()
         for n, v in a.items()}
    outs = {"y": (P, KC, T), "kv_out": (P, 12, T), "win_k_out": (P, NB, GP, WIN), "win_v_out": (P, NB, 4, 2 * P),
            "hgrn_p_out": (P, HH, P), "hgrn_s_out": (P, NB, HH, P)}
    for n, s in outs.items():
        d[n] = nc.dram_tensor(f"out_{n}", s, F32, kind="ExternalOutput").ap()
    d["gate_scratch"] = nc.dram_tensor("gate_scratch", (48, NB), F32, kind="Internal").ap()
    d["bias_skew"] = nc.dram_tensor("bias_skew", (P, HEADS, SKEW), F32, kind="Internal").ap()
    d["bias_scratch"] = nc.dram_tensor("bias_scratch", (16, 1024), F32, kind="Internal").ap()
    program(nc, d)
    r = run_bass_kernel_spmd(nc, [{f"in_{n}": v for n, v in a.items()}], core_ids=[0]).results[0]
    o = {n: np.asarray(r[f"out_{n}"]) for n in outs}
    y = o["y"].transpose(2, 1, 0).reshape(T, D_MODEL)
    kv = o["kv_out"].reshape(2, HD, 3, 2, GP, T).transpose(2, 5, 3, 4, 0, 1).reshape(3, T, 2, KVH, HD)
    wk = o["win_k_out"].reshape(2, HD, NB, GP, WIN).transpose(2, 4, 3, 0, 1).reshape(NB, WIN, KVH, HD)
    wv = o["win_v_out"].transpose(1, 2, 0, 3).reshape(NB, WIN, KVH, HD)
    return (C(y[None, :SEQ]), C(y[SEQ:, None]), C(kv[0][None, None, :SEQ]), C(kv[1][None, None, :SEQ]),
            C(kv[2][None, None, :SEQ]), C(o["hgrn_p_out"].transpose(1, 0, 2)[None, None]),
            C(kv[0][None, SEQ:, None]), C(kv[1][None, SEQ:, None]), C(np.stack([wk, wv], 2)[None]),
            C(o["hgrn_s_out"].transpose(1, 2, 0, 3)[None]))
```

```python
from contextlib import ExitStack

import numpy as np

import concourse.bass as bass
from concourse import mybir

F32 = mybir.dt.float32
F32R = mybir.dt.float32r
I32 = mybir.dt.int32
ALU = mybir.AluOpType
ACT = mybir.ActivationFunctionType
AX = mybir.AxisListType.X

P = 128
D_MODEL = 1024
KC = D_MODEL // P
SEQ = 512
NB = 8
T = SEQ + NB
TH = T // 2
TILES = SEQ // P
PAST = 2048
PAGES = PAST // P
POOL = 160
HEADS, KVH, HD = 16, 4, 64
GP = KVH // 2
REP = HEADS // KVH
BLOCK = 64
NBLK = PAST // BLOCK
PBLK = SEQ // BLOCK
WIN = 512
N_BUCKETS = 32
MAX_DISTANCE = 1024
D_FF = 2816
FF = D_FF // P
HH = 8
NSA_UNITS = 21
HGRN_UNITS = 32
EPS = 1e-6
NEG = -1e30
FLOOR = -1e20
Q_U, CK_U, CV_U, SK_U, SV_U, WK_U, WV_U, GATE_U = 0, 8, 10, 12, 14, 16, 18, 20
RING = 4
SUBK = 11
SKEW = SEQ + P
LEVELS = [64, 32, 16, 8, 4, 2]


class Seq:

    def __init__(self, eng, sem, base=0):
        self.eng, self.sem, self.base, self.n = eng, sem, base, 0

    def __call__(self, ins):
        ins.then_inc(self.sem, 1)
        self.n += 1
        return self.n

    def wait(self, n=None):
        self.eng.wait_ge(self.sem, self.base + (self.n if n is None else n))

    def link(self, ins):
        self(ins)
        self.wait()


class Core:

    def __init__(self, nc, ctx):
        self.nc = nc
        sb = lambda n, s, d=F32: ctx.enter_context(nc.sbuf_tensor(n, s, d))
        sem = lambda n: ctx.enter_context(nc.semaphore(n))
        self.X = sb("X", [P, KC, T])
        self.rstd = sb("rstd", [P, T])
        self.ring = sb("ring", [P, RING, SUBK * P])
        self.nw = sb("nw", [P, 2, 4, KC])
        self.ident = sb("ident", [P, P])
        self.ones = sb("ones", [P, P])
        self.loaded = [sem(f"weights_loaded{s}") for s in range(RING)]
        self.hi_cut = [sem(f"high_part_cut{s}") for s in range(RING)]
        self.lo_cut = [sem(f"rest_cut{s}") for s in range(RING)]
        self.tile_done = [sem(f"weights_used{s}") for s in range(RING)]
        self.psum_free = [sem(f"unit_evacuated{s}") for s in range(RING)]
        self.loads = [0] * RING
        self.done = [0] * RING
        self.freed = [1] * RING


def pairs(ap):
    return ap.rearrange("p (h t) -> p h t", h=2)


def load_tile(eng, c, w, s, index, kcs):
    dst = c.ring[:, s, 0:kcs * P]
    src = w[bass.ds(index, 1)] if not isinstance(index, int) else w[index:index + 1]
    eng.dma_start(dst, src.rearrange("o p n -> p (o n)")).then_inc(c.loaded[s], 16)


def load_pages(eng, c, dst, src, first, count, loaded):
    def one(x):
        page = eng.value_load(c.pages[0:1, bass.ds(x + first, 1)], min_val=0, max_val=POOL - 1)
        eng.dma_start(dst[:, bass.ds(x, 1), :].rearrange("p o n -> p (o n)"),
                      src[bass.ds(page, 1)].rearrange("o p n -> p (o n)")).then_inc(loaded, 16)

    if count < 8:
        for x in range(count):
            one(x)
    else:
        with eng.Fori(0, count // 4) as i:
            for x in range(4):
                one(i * 4 + x)


def linear(c, name, w, n_units, subs, kcs, src, evac, nxt, scale=None, beside=None, norm=None):
    nc = c.nc
    tiles = n_units * subs
    loops, rest = tiles // RING, tiles % RING
    per = RING // subs
    base_load, base_done, base_free = list(c.loads), list(c.done), list(c.freed)
    cut_here = not isinstance(src, tuple)
    with ExitStack() as ctx:
        ps = [ctx.enter_context(nc.psum_tensor(f"{name}_ps{j}", [P, 2, 512], F32)) for j in range(per)]
        wh = ctx.enter_context(nc.sbuf_tensor(f"{name}_w_hi", [P, 2, kcs * P], F32R))
        wl = ctx.enter_context(nc.sbuf_tensor(f"{name}_w_lo", [P, 2, kcs * P], F32R))
        if cut_here:
            xh, xl = [ctx.enter_context(nc.sbuf_tensor(f"{name}_x_{n}", [P, kcs, T], F32R)) for n in ("hi", "lo")]
            x_hi, x_lo = [nc.alloc_semaphore(f"{name}_x_{n}_cut") for n in ("hi", "lo")]
        else:
            xh, xl = src
        post, ssq, y, sq = norm or (None, None, None, None)
        means = (norm is not None) + (post is not None)
        if norm is not None:
            summed, inverse, rooted, scaled, squared, added, own_done = [nc.alloc_semaphore(f"{name}_{n}") for n in
                ("token_sums", "inverse_means", "roots", "scaled", "squares", "squares_added", "chain")]
            x_new = [nc.alloc_semaphore(f"{name}_x_new{j}") for j in range(2)]
        block = ctx.enter_context(nc.Block())

        def rounds(eng, cut, first_done=None, tail=None):
            def step(i, s):
                if cut is not None:
                    cut(i, s)
                if isinstance(i, int) and i == 0 and s == 0:
                    if first_done is not None:
                        first_done()
                    return
                if isinstance(i, int) and i == 0 and s == 1 and tail is not None and norm is not None:
                    tail()
                r, q = (i, s - 1) if s else (i - 1, RING - 1)
                if q % subs == subs - 1:
                    evac(eng, ps, q // subs, r, ready)

            evac(eng, ps, None, 0, ready)
            for s in range(RING):
                step(0, s)
            if loops > 1:
                with eng.Fori(1, loops) as i:
                    for s in range(RING):
                        step(i, s)
            for s in range(rest):
                step(loops, s)
            r, q = (loops, rest - 1) if rest else (loops - 1, RING - 1)
            evac(eng, ps, q // subs, r, ready)

        def ready(eng, j, i):
            s = j * subs + subs - 1
            eng.wait_ge(c.tile_done[s], i + (base_done[s] + 1))

        def slot_free(eng, i, s):
            if s >= 2:
                eng.wait_ge(c.tile_done[s - 2], i + (base_done[s - 2] + 1))
            elif not (isinstance(i, int) and i == 0):
                eng.wait_ge(c.tile_done[s + 2], i + base_done[s + 2])

        @block.sync
        def _(sp):
            if loops > 1:
                with sp.Fori(0, loops - 1) as i:
                    for s in range(RING):
                        sp.wait_ge(c.lo_cut[s], i + (base_done[s] + 1))
                        load_tile(sp, c, w, s, i * RING + (RING + s), kcs)
                        if beside is not None:
                            beside(sp, i * RING + s)
            for s in range(RING):
                sp.wait_ge(c.lo_cut[s], base_done[s] + loops)
                if s < rest:
                    load_tile(sp, c, w, s, loops * RING + s, kcs)
                    sp.wait_ge(c.lo_cut[s], base_done[s] + loops + 1)
                if nxt is not None:
                    load_tile(sp, c, nxt[0], s, s, nxt[1])

        @block.scalar
        def _(act):
            def cut(i, s):
                act.wait_ge(c.loaded[s], i * 16 + 16 * base_load[s])
                slot_free(act, i, s)
                act.activation(wh[:, s % 2, :], c.ring[:, s, 0:kcs * P], ACT.Copy).then_inc(c.hi_cut[s], 1)

            def cut_source():
                if post is not None:
                    root(1)
                for k in range(kcs):
                    if post is not None:
                        act.wait_ge(x_new[k % 2], k // 2 + 1)
                    act.activation(xh[:, k, :], src[:, k, :], ACT.Copy,
                                   scale=1.0 if scale is None else scale[:, k:k + 1]).then_inc(x_hi, 1)
                    if norm is not None:
                        if k >= 2:
                            act.wait_ge(added, k - 1)
                        act.activation(sq[:, k % 2, :], src[:, k, :], ACT.Square).then_inc(squared, 1)

            def root(n):
                act.wait_ge(inverse, n)
                act.activation(c.rstd[:, :], c.rstd[:, :], ACT.Sqrt).then_inc(rooted, 1)

            rounds(act, cut, cut_source if cut_here else None, lambda: root(means))

        @block.vector
        def _(dve):
            def cut(i, s):
                dve.wait_ge(c.loaded[s], i * 16 + 16 * base_load[s])
                slot_free(dve, i, s)
                dve.wait_ge(c.hi_cut[s], i + (base_done[s] + 1))
                dve.tensor_tensor(wl[:, s % 2, :], c.ring[:, s, 0:kcs * P], wh[:, s % 2, :].bitcast(F32),
                                  ALU.subtract).then_inc(c.lo_cut[s], 1)

            def cut_source():
                if post is not None:
                    dve.wait_ge(summed, 1)
                    inverse_mean(ps[3])
                    dve.wait_ge(rooted, 1)
                for k in range(kcs):
                    if post is not None:
                        update(k)
                        if k:
                            rest_of(k - 1)
                    else:
                        rest_of(k)
                if post is not None:
                    rest_of(kcs - 1)

            def inverse_mean(sums):
                own.link(dve.tensor_scalar(pairs(c.rstd[:, :]), sums[:, :, 0:TH], 1.0 / D_MODEL, EPS, ALU.mult, ALU.add))
                dve.reciprocal(c.rstd[:, :], c.rstd[:, :]).then_inc(inverse, 1)

            def update(k):
                if k >= 3 and k % 2:
                    dve.wait_ge(x_new[1], k // 2)
                dve.scalar_tensor_tensor(y[:, k % 2, :], post[0][:, k, :], post[1][:, k:k + 1], c.rstd[:, :],
                                         ALU.mult, ALU.mult).then_inc(scaled, 1)
                if k % 2 == 0:
                    dve.wait_ge(scaled, k + 1)
                    dve.tensor_tensor(src[:, k, :], src[:, k, :], y[:, 0, :], ALU.add).then_inc(x_new[0], 1)
                    dve.wait_ge(x_new[0], k // 2 + 1)

            def tail():
                if post is not None:
                    dve.wait_ge(scaled, kcs)
                dve.wait_ge(added, kcs)
                inverse_mean(ps[2])
                dve.wait_ge(rooted, means)

            def rest_of(k):
                dve.wait_ge(x_hi, k + 1)
                hi = xh[:, k, :].bitcast(F32)
                if scale is None:
                    dve.tensor_tensor(xl[:, k, :], src[:, k, :], hi, ALU.subtract).then_inc(x_lo, 1)
                else:
                    dve.scalar_tensor_tensor(xl[:, k, :], src[:, k, :], scale[:, k:k + 1], hi, ALU.mult,
                                             ALU.subtract).then_inc(x_lo, 1)

            own = Seq(dve, own_done) if norm is not None else None
            rounds(dve, cut, cut_source if cut_here else None, tail)

        @block.gpsimd
        def _(pool):
            if post is not None:
                for k in range(1, kcs, 2):
                    pool.wait_ge(scaled, k + 1)
                    pool.tensor_tensor(src[:, k, :], src[:, k, :], y[:, 1, :], ALU.add).then_inc(x_new[1], 1)
                    pool.wait_ge(x_new[1], k // 2 + 1)
            rounds(pool, None)

        @block.tensor
        def _(pe):
            def one(s, i, first=False):
                j, sub = s // subs, s % subs
                pe.wait_ge(c.lo_cut[s], i + (base_done[s] + 1))
                if sub == 0:
                    pe.wait_ge(c.psum_free[j], i + base_free[j])
                for k in range(kcs):
                    if first and cut_here:
                        pe.wait_ge(x_lo, k + 1)
                    if first and norm is not None and k:
                        add_squares(k - 1)
                    a, x = slice(k * P, (k + 1) * P), sub * kcs + k
                    for part, (wt, xt) in enumerate(((wh, xh), (wh, xl), (wl, xh))):
                        for h in range(2):
                            last = pe.matmul(ps[j][:, h, 0:TH], wt[:, s % 2, a], xt[:, x, h * TH:(h + 1) * TH],
                                             start=(sub == 0 and k == 0 and part == 0),
                                             stop=(sub == subs - 1 and k == kcs - 1 and part == 2))
                last.then_inc(c.tile_done[s], 1)
                if first and norm is not None:
                    add_squares(kcs - 1)

            def token_sums(bank, squares, start, stop):
                for h in range(2):
                    mm = pe.matmul(bank[:, h, 0:TH], c.ones[:, :], squares[:, h * TH:(h + 1) * TH], start=start, stop=stop)
                return mm

            def add_squares(k):
                pe.wait_ge(squared, k + 1)
                token_sums(ps[2], sq[:, k % 2, :], k == 0, k == kcs - 1).then_inc(added, 1)

            if post is not None:
                token_sums(ps[3], ssq, True, True).then_inc(summed, 1)
            one(0, 0, first=True)
            for s in range(1, RING):
                if s == 2 and norm is not None:
                    pe.wait_ge(inverse, means)
                one(s, 0)
            if loops > 1:
                with pe.Fori(1, loops) as i:
                    for s in range(RING):
                        one(s, i)
            for s in range(rest):
                one(s, loops)

    for s in range(RING):
        c.done[s] += loops + (s < rest)
        c.loads[s] += loops - 1 + (s < rest) + (nxt is not None)
        if s < per:
            c.freed[s] += loops + (s < rest // subs)


def evac_scaled(c, dst, per=RING):
    def evac(eng, ps, j, i, ready):
        if eng is not c.nc.vector or j is None:
            return
        ready(eng, j, i)
        if isinstance(i, int):
            eng.tensor_tensor(pairs(dst[:, i * per + j, :]), ps[j][:, :, 0:TH], pairs(c.rstd[:, :]), ALU.mult)\
               .then_inc(c.psum_free[j], 1)
        else:
            eng.tensor_tensor(dst[:, bass.ds(i * per + j, 1), :].rearrange("p o (h t) -> p (o h) t", h=2),
                              ps[j][:, :, 0:TH], pairs(c.rstd[:, :]), ALU.mult).then_inc(c.psum_free[j], 1)
    return evac


def evac_swiglu(c, Hh, Hl, a_t, g_t, sems):
    a_act, made, used = sems
    base_free = list(c.freed)

    def evac(eng, ps, j, i, ready):
        if j is None:
            if eng is c.nc.gpsimd:
                for m in range(2):
                    eng.sem_inc(used[m], 1)
            return
        m, is_g = j // 2, j % 2
        if eng is c.nc.vector:
            ready(eng, j, i)
            eng.wait_ge(used[m], i + 1)
            eng.tensor_tensor(pairs((g_t if is_g else a_t)[:, m, :]), ps[j][:, :, 0:TH], pairs(c.rstd[:, :]),
                              ALU.mult).then_inc(c.psum_free[j], 1)
        if eng is c.nc.scalar and not is_g:
            eng.wait_ge(c.psum_free[j], i + (base_free[j] + 1))
            eng.activation(a_t[:, m, :], a_t[:, m, :], ACT.Silu).then_inc(a_act[m], 1)
        if eng is c.nc.gpsimd and is_g:
            hi, lo = [x[:, i * 2 + m, :] if isinstance(i, int) else
                      x[:, bass.ds(i * 2 + m, 1), :].rearrange("p o t -> p (o t)") for x in (Hh, Hl)]
            eng.wait_ge(a_act[m], i + 1)
            eng.wait_ge(c.psum_free[j], i + (base_free[j] + 1))
            at = i * 4 + 2 * m
            eng.tensor_tensor(hi, a_t[:, m, :], g_t[:, m, :], ALU.mult).then_inc(made, 1)
            eng.wait_ge(made, at + 1)
            eng.tensor_tensor(g_t[:, m, :], a_t[:, m, :], g_t[:, m, :], ALU.mult).then_inc(made, 1)
            eng.wait_ge(made, at + 2)
            eng.tensor_tensor(lo, g_t[:, m, :], hi.bitcast(F32), ALU.subtract).then_inc(used[m], 1)
            eng.wait_ge(used[m], i + 2)
    return evac


def evac_squares(c, dst, sq, ssq, sems, per):
    squared, added = sems
    base_free = list(c.freed)

    def evac(eng, ps, j, i, ready):
        if j is None:
            if eng is c.nc.vector:
                eng.memset(ssq[:, :], 0.0).then_inc(added, 1)
            return
        if eng is c.nc.scalar:
            ready(eng, j, i)
            out = pairs(dst[:, i * per + j, :]) if isinstance(i, int) else \
                dst[:, bass.ds(i * per + j, 1), :].rearrange("p o (h t) -> p (o h) t", h=2)
            eng.activation(out, ps[j][:, :, 0:TH], ACT.Copy).then_inc(c.psum_free[j], 1)
        if eng is c.nc.vector:
            eng.wait_ge(c.psum_free[j], i + (base_free[j] + 1))
            v = dst[:, i * per + j, :] if isinstance(i, int) else \
                dst[:, bass.ds(i * per + j, 1), :].rearrange("p o t -> p (o t)")
            eng.wait_ge(added, i * per + (j + 1))
            eng.tensor_tensor(sq[:, :], v, v, ALU.mult).then_inc(squared, 1)
            eng.wait_ge(squared, i * per + (j + 1))
            eng.tensor_tensor(ssq[:, :], ssq[:, :], sq[:, :], ALU.add).then_inc(added, 1)
    return evac


def norm_step(c, name, ssq, post, out=None):
    nc = c.nc
    with ExitStack() as ctx:
        sem = lambda n: nc.alloc_semaphore(f"{name}_{n}")
        summed, inverse, rooted, own_done, scaled, saved = [sem(n) for n in
            ("token_sums", "inverse_means", "roots", "dve_chain", "scaled", "saved")]
        x_new = [sem(f"x_new{j}") for j in range(2)]
        ps = ctx.enter_context(nc.psum_tensor(f"{name}_ps", [P, 2, 512], F32))
        y = ctx.enter_context(nc.sbuf_tensor(f"{name}_scaled", [P, 2, T], F32))
        block = ctx.enter_context(nc.Block())

        @block.sync
        def _(sp):
            if out is not None:
                for k in range(KC):
                    sp.wait_ge(x_new[k % 2], k // 2 + 1)
                    sp.dma_start(out[:, k, :], c.X[:, k, :]).then_inc(saved, 16)
                sp.wait_ge(saved, 16 * KC)

        @block.tensor
        def _(pe):
            for h in range(2):
                mm = pe.matmul(ps[:, h, 0:TH], c.ones[:, :], ssq[:, h * TH:(h + 1) * TH], start=True, stop=True)
            mm.then_inc(summed, 1)

        @block.scalar
        def _(act):
            act.wait_ge(inverse, 1)
            act.activation(c.rstd[:, :], c.rstd[:, :], ACT.Sqrt).then_inc(rooted, 1)

        @block.gpsimd
        def _(pool):
            for k in range(1, KC, 2):
                pool.wait_ge(scaled, k + 1)
                pool.tensor_tensor(c.X[:, k, :], c.X[:, k, :], y[:, 1, :], ALU.add).then_inc(x_new[1], 1)
                pool.wait_ge(x_new[1], k // 2 + 1)

        @block.vector
        def _(dve):
            own = Seq(dve, own_done)
            dve.wait_ge(summed, 1)
            own.link(dve.tensor_scalar(pairs(c.rstd[:, :]), ps[:, :, 0:TH], 1.0 / D_MODEL, EPS, ALU.mult, ALU.add))
            dve.reciprocal(c.rstd[:, :], c.rstd[:, :]).then_inc(inverse, 1)
            dve.wait_ge(rooted, 1)
            for k in range(KC):
                if k >= 3 and k % 2:
                    dve.wait_ge(x_new[1], k // 2)
                dve.scalar_tensor_tensor(y[:, k % 2, :], post[0][:, k, :], post[1][:, k:k + 1], c.rstd[:, :],
                                         ALU.mult, ALU.mult).then_inc(scaled, 1)
                if k % 2 == 0:
                    dve.wait_ge(scaled, k + 1)
                    dve.tensor_tensor(c.X[:, k, :], c.X[:, k, :], y[:, 0, :], ALU.add).then_inc(x_new[0], 1)
                    dve.wait_ge(x_new[0], k // 2 + 1)


PAGES_A_CHUNK = 32


def compress(c, HT, d, rows, first_in, kcT, kcBD, vcS, v_rep):
    nc = c.nc
    CH = PAGES_A_CHUNK
    NCH = NB * PAGES // CH
    with ExitStack() as ctx:
        sem = lambda n: nc.alloc_semaphore(f"cmp_{n}")
        sb = lambda n, s: ctx.enter_context(nc.sbuf_tensor(f"cmp_{n}", s, F32))
        w1 = sb("w1", [P, 2, BLOCK // 2, P])
        free = sb("small", [P, 1786])
        HN = NB * PAGES * 4 + 2 * PBLK
        hid = free[:, 0:2 * HN].rearrange("p (a n) -> p a n", a=2)
        hid_rep = free[:, 2 * HN:2 * HN + P].rearrange("p (a b n) -> p a b n", a=GP, b=8)
        pe_in = free[:, 1400:1528].rearrange("p (a n) -> p a n", a=2)
        w2 = free[:, 1528:1784].rearrange("p (a n) -> p a n", a=2)
        pe_w = free[:, 1784:1786]
        ps_c = [ctx.enter_context(nc.psum_tensor(f"cmp_ps{j}", [P, 512], F32)) for j in range(2)]
        ps_k = ctx.enter_context(nc.psum_tensor("cmp_psk", [P, 512], F32))
        ps_q = ctx.enter_context(nc.psum_tensor("cmp_psq", [P, 512], F32))
        ps_v = ctx.enter_context(nc.psum_tensor("cmp_psv", [P, 512], F32))
        small, w1_in = sem("small_loaded"), [sem(f"w1_half{h}_loaded") for h in range(2)]
        rows_in = [sem(f"rows{s}_loaded") for s in range(2)]
        rows_sw = [sem(f"rows{s}_loaded_by_pool") for s in range(2)]
        w1_used = sem("w1_half0_used")
        beside_in, pe_out = sem("prompt_rows_ready"), sem("pe_copied")
        chunk_done = [sem(f"chunk{s}_products") for s in range(2)]
        chunk_out = [sem(f"chunk{s}_silu") for s in range(2)]
        prompt_out, second, moved, own_done = sem("prompt_silu"), sem("second_products"), sem("rep_ready"), sem("chain")
        block = ctx.enter_context(nc.Block())
        PR = GP * PBLK + 1
        slot = lambda x: rows[:, (1 - x) * CH * 256:(2 - x) * CH * 256].rearrange("p (g n) -> p g n", g=CH)
        beside = rows[:, 2 * CH * 256:]

        def group(g):
            return (g % NCH) ^ 1

        def load_chunk(eng, g, at, count, loaded=None):
            eng.wait_ge(chunk_done[g % 2], g // 2)
            load_pages(eng, c, slot(g % 2)[:, at:at + count], d["cache_cmp"][g // NCH], group(g) * CH + at, count,
                       (loaded or rows_in)[g % 2])

        @block.sync
        def _(sp):
            def load_w1(kv, h):
                sp.dma_start(w1[:, h].rearrange("p t n -> p (t n)"), d["cmp_w1"][kv, h]).then_inc(w1_in[h], 16)

            load_w1(0, 0)
            sp.dma_start(pe_in[:, :, :], d["cmp_pe"]).then_inc(small, 16)
            sp.dma_start(w2[:, :, :], d["cmp_w2"]).then_inc(small, 16)
            load_w1(0, 1)
            for g in range(2, 2 * NCH):
                if g == NCH + 1:
                    sp.wait_ge(w1_used, 1)
                    load_w1(1, 0)
                    sp.wait_ge(chunk_done[1], NCH // 2)
                    load_w1(1, 1)
                load_chunk(sp, g, 0, 12)

        @block.gpsimd
        def _(pool):
            for g in range(2, 2 * NCH):
                load_chunk(pool, g, 24, 8, rows_sw)

        @block.tensor
        def _(pe):
            pe.wait_ge(small, 32)
            for kv in range(2):
                pe.wait_ge(w1_in[0], 16 * (kv + 1))
                for ch in range(NCH):
                    s = ch % 2
                    n = kv * (NCH // 2) + ch // 2
                    cols = P + PR if ch == 0 else P
                    if ch == 0:
                        pe.wait_ge(beside_in, kv + 1)
                    if n == 0:
                        pe.wait_ge(first_in, 16 * 2 * CH)
                    else:
                        pe.wait_ge(rows_in[s], 16 * 24 * n)
                        pe.wait_ge(rows_sw[s], 16 * 8 * n)
                        pe.wait_ge(chunk_out[s], n)
                    if kv and ch == 0:
                        pe.wait_ge(prompt_out, 1)
                    first = (1 - s) * CH * 256
                    for t in range(BLOCK):
                        if ch == 0 and t == BLOCK // 2:
                            pe.wait_ge(w1_in[1], 16 * (kv + 1))
                        mm = pe.matmul(ps_c[s][:, 0:cols], w1[:, t // 32, t % 32, :],
                                       rows[:, first + t:first + (cols - 1) * BLOCK + t + 1:BLOCK],
                                       start=t == 0, stop=t == BLOCK - 1)
                        if ch == NCH - 1 and t == 31 and kv == 0:
                            mm.then_inc(w1_used, 1)
                    mm.then_inc(chunk_done[s], 1)
            pe.wait_ge(chunk_out[0], NCH)
            pe.wait_ge(chunk_out[1], NCH)
            pe.wait_ge(prompt_out, 2)
            pe.matmul(ps_k[:, :], w2[:, 0, :], hid[:, 0, 0:512], start=True, stop=True).then_inc(second, 1)
            pe.matmul(ps_q[:, 0:16], w2[:, 0, :], hid[:, 0, 512:528], start=True, stop=True).then_inc(second, 1)
            for j in range(4):
                mm = pe.matmul(ps_v[:, j * P:(j + 1) * P], hid[:, 1, j:512:4], w2[:, 1, :], start=True, stop=True)
            mm.then_inc(second, 1)
            pe.wait_ge(moved, 1)
            pe.matmul(ps_c[0][:, 0:P], hid_rep[:, :, :, :].rearrange("p a b n -> p (a b n)"), w2[:, 1, :],
                      start=True, stop=True).then_inc(second, 1)

        @block.scalar
        def _(act):
            for kv in range(2):
                act.wait_ge(chunk_done[0], kv * (NCH // 2) + 1)
                act.activation(pe_w[:, kv:kv + 1], ps_c[0][:, P + PR - 1:P + PR], ACT.Copy).then_inc(pe_out, 1)
                act.wait_ge(pe_out, kv + 1)
                act.activation(hid[:, kv, 512:528], ps_c[0][:, P:P + PR - 1], ACT.Silu, bias=pe_w[:, kv:kv + 1])\
                   .then_inc(prompt_out, 1)
                for ch in range(NCH):
                    s = ch % 2
                    act.wait_ge(chunk_done[s], kv * (NCH // 2) + ch // 2 + 1)
                    act.activation(hid[:, kv, group(ch) * P:(group(ch) + 1) * P], ps_c[s][:, 0:P], ACT.Silu,
                                   bias=pe_w[:, kv:kv + 1]).then_inc(chunk_out[s], 1)
                    if kv * NCH + ch + 2 < 2 * NCH:
                        load_chunk(act, kv * NCH + ch + 2, 12, 12)

        @block.vector
        def _(dve):
            own = Seq(dve, own_done)
            dve.wait_ge(small, 32)
            for kv in range(2):
                if kv:
                    dve.wait_ge(chunk_done[0], 1)
                at = GP * SEQ
                own(dve.tensor_copy(beside[:, 0:at].rearrange("p (g t) -> p g t", g=GP),
                                    HT[:, CK_U + 2 * kv:CK_U + 2 * kv + 2, 0:SEQ]))
                own.link(dve.tensor_copy(beside[:, at:at + BLOCK], pe_in[:, kv, :]))
                dve.sem_inc(beside_in, 1)
            own.link(dve.memset(kcBD[:, :, :, :], 0.0))
            dve.wait_ge(prompt_out, 2)
            dve.tensor_copy(hid_rep[:, :, :, :], hid[:, 1, 512:528].rearrange("p (g n) -> p g n", g=GP)
                            .unsqueeze(2).broadcast_to([P, GP, 8, PBLK])).then_inc(moved, 1)
            dve.wait_ge(second, 1)
            own(dve.tensor_copy(kcT[:, :], ps_k[:, :]))
            dve.wait_ge(second, 2)
            for g2 in range(2):
                rows_g = slice(g2 * HD, (g2 + 1) * HD)
                own(dve.tensor_copy(kcBD[rows_g, :, g2, :], ps_q[rows_g, 0:16].rearrange("p (g n) -> p g n", g=GP)))
            dve.wait_ge(second, 3)
            own(dve.tensor_copy(vcS[:, :], ps_v[:, :]))
            dve.wait_ge(second, 4)
            own.link(dve.tensor_copy(v_rep[:, :], ps_c[0][:, 0:P]))


def attention_setup(c, HT, d, tabs, biasC, Vtok, gT, Vnew, skew_out):
    nc = c.nc
    with ExitStack() as ctx:
        sem = lambda n: nc.alloc_semaphore(f"set_{n}")
        sb = lambda n, s: ctx.enter_context(nc.sbuf_tensor(f"set_{n}", s, F32))
        oh = sb("onehot", [N_BUCKETS + 1, 2, 1024])
        R = sb("bias_row", [16, 1024])
        sg = sb("gates", [48, T])
        ps = [ctx.enter_context(nc.psum_tensor(f"set_ps{j}", [P, 512], F32)) for j in range(6)]
        loaded, scaled, gated, row_out = [sem(n) for n in ("loaded", "q_scaled", "gates", "bias_row_out")]
        made, moved, gate_out = sem("psum_ready"), sem("psum_moved"), sem("gates_out")
        bias_part = sem("block_bias_parts")
        block = ctx.enter_context(nc.Block())

        @block.sync
        def _(sp):
            sp.dma_start(oh[:, :, :], d["onehot_rows"]).then_inc(loaded, 16)
            sp.dma_start(tabs[:, :], d["tabs"]).then_inc(loaded, 16)
            sp.wait_ge(gated, 1)
            sp.dma_start(d["gate_scratch"], sg[:, SEQ:T]).then_inc(gate_out, 16)
            sp.wait_ge(moved, 2)
            sp.dma_start(d["bias_scratch"], R[:, :]).then_inc(row_out, 16)
            sp.wait_ge(row_out, 16)
            sp.dma_start(d["bias_skew"], bass.AP(d["bias_scratch"].tensor, 0, [[0, P], [1024, HEADS], [1, SKEW]]))\
              .then_inc(skew_out, 16)
            sp.wait_ge(gate_out, 16)

        @block.tensor
        def _(pe):
            pe.wait_ge(loaded, 32)
            for j in range(2):
                pe.matmul(ps[j][0:16, :], tabs[:, 0:16], oh[:, 0, j * 512:(j + 1) * 512], start=True, stop=True)\
                  .then_inc(made, 1)
            for x in range(PBLK + 2 * (TILES - 1)):
                at = BLOCK * (2 * (TILES - 1) - x) - (BLOCK - 1) + 511
                mm = pe.matmul(ps[2][:, x * 16:(x + 1) * 16], oh[:, 1, at:at + P], tabs[:, 0:16], start=True, stop=True)
            mm.then_inc(made, 1)
            pe.wait_ge(gated, 1)
            for i in range(TILES):
                mm = pe.transpose(ps[3][:, i * 48:(i + 1) * 48], sg[:, i * P:(i + 1) * P], c.ident[0:48, 0:48])
            mm.then_inc(made, 1)
            for j, u in enumerate((SV_U, SV_U + 1, WV_U, WV_U + 1)):
                mm = pe.transpose(ps[4][0:NB, j * P:(j + 1) * P], HT[:, u, SEQ:T], c.ident[:, :])
            mm.then_inc(made, 1)
            for i in range(TILES):
                b = ps[5] if i % 2 == 0 else ps[0]
                if i == 1:
                    pe.wait_ge(moved, 2)
                if i >= 2:
                    pe.wait_ge(moved, 4 + i)
                for j, u in enumerate((SV_U, SV_U + 1, WV_U, WV_U + 1)):
                    mm = pe.transpose(b[:, j * P:(j + 1) * P], HT[:, u, i * P:(i + 1) * P], c.ident[:, :])
                mm.then_inc(made, 1)

        @block.scalar
        def _(act):
            act.activation(sg[:, :], HT[0:48, GATE_U, :], ACT.Sigmoid).then_inc(gated, 1)

        @block.vector
        def _(dve):
            dve.tensor_scalar(HT[:, 0:8, :], HT[:, 0:8, :], HD ** -0.5, None, ALU.mult).then_inc(scaled, 1)
            for j in range(2):
                dve.wait_ge(made, j + 1)
                dve.tensor_copy(R[:, j * 512:(j + 1) * 512], ps[j][0:16, :]).then_inc(moved, 1)
            dve.wait_ge(made, 3)
            for i in range(TILES):
                x = 2 * (TILES - 1) - 2 * i
                ins = dve.tensor_copy(biasC[:, i], ps[2][:, x * 16:(x + PBLK) * 16].rearrange("p (n h) -> p h n", n=PBLK))
                ins.then_inc(moved if i == TILES - 1 else bias_part, 1)
            dve.wait_ge(made, 4)
            dve.tensor_copy(gT[:, :, :], ps[3][:, 0:192].rearrange("p (i n) -> p i n", i=TILES)).then_inc(moved, 1)
            dve.wait_ge(made, 5)
            dve.tensor_copy(Vnew[:, :], ps[4][0:NB, :]).then_inc(moved, 1)
            for i in range(TILES):
                dve.wait_ge(made, 6 + i)
                dve.tensor_copy(Vtok[:, i, :], (ps[5] if i % 2 == 0 else ps[0])[:, :]).then_inc(moved, 1)


def prompt_compressed(c, HT, d, kcBD, v_rep, T_bias, biasC, gT, Otok, skew_out):
    nc = c.nc
    with ExitStack() as ctx:
        sem = lambda n: nc.alloc_semaphore(f"pc_{n}")
        sb = lambda n, s: ctx.enter_context(nc.sbuf_tensor(f"pc_{n}", s, F32))
        S = sb("scores", [P, TILES * HEADS, PBLK])
        mx = sb("max", [P, TILES * HEADS])
        sm = sb("sum", [P, TILES * HEADS])
        PT = sb("probsT", [P, SEQ])
        BDv = sb("values_block_diagonal", [P, 8, 2, HD])
        mask = sb("head_mask", [P, 16])
        mask_in, t_in, bd_done = sem("mask_in"), sem("bias_tiles_in"), sem("values_laid_out")
        ps_s = ctx.enter_context(nc.psum_tensor("pc_ps", [P, 512], F32))
        ps_t = ctx.enter_context(nc.psum_tensor("pc_pt", [P, 512], F32))
        ps_o = [ctx.enter_context(nc.psum_tensor(f"pc_po{j}", [P, 2, 512], F32)) for j in range(2)]
        scores, shifted, expd, probs, turned, turned_out, outs, outs_moved, own_done = [sem(n) for n in
            ("scores", "shifted", "exp", "probs", "turned", "turned_out", "outs", "outs_moved", "chain")]
        block = ctx.enter_context(nc.Block())
        wide = lambda a: a.unsqueeze(2).broadcast_to([P, TILES * HEADS, PBLK])

        @block.sync
        def _(sp):
            sp.dma_start(mask[:, :], d["head_mask"]).then_inc(mask_in, 16)
            sp.wait_ge(skew_out, 16)
            sp.dma_start(T_bias[:, :, :], bass.AP(d["bias_skew"].tensor, P - 1, [[HEADS * SKEW - 1, P], [SKEW, HEADS], [1, SEQ]]))\
              .then_inc(t_in, 16)
            sp.wait_ge(t_in, 16)

        @block.tensor
        def _(pe):
            for i in range(TILES):
                for u in range(8):
                    at = (i * 8 + u) * 16
                    mm = pe.matmul(ps_s[:, at:at + 16], HT[:, u, i * P:(i + 1) * P],
                                   kcBD[:, u // REP].rearrange("p g n -> p (g n)"), start=True, stop=True)
            mm.then_inc(scores, 1)
            pe.wait_ge(probs, 1)
            for i in range(TILES):
                mm = pe.transpose(ps_t[:, i * P:(i + 1) * P],
                                  S[:, i * HEADS:(i + 1) * HEADS, :].rearrange("p h n -> p (h n)"), c.ident[:, :])
            mm.then_inc(turned, 1)
            pe.wait_ge(turned_out, 1)
            pe.wait_ge(bd_done, 2)
            for i in range(TILES):
                if i >= 2:
                    pe.wait_ge(outs_moved, i - 1)
                for j in range(2):
                    mm = pe.matmul(ps_o[i % 2][:, j, :], PT[:, i * P:(i + 1) * P],
                                   BDv[:, 4 * j:4 * j + 4].rearrange("p c g n -> p (c g n)"), start=True, stop=True)
                mm.then_inc(outs, 1)

        @block.scalar
        def _(act):
            act.wait_ge(shifted, 1)
            act.activation(S[:, :, :], S[:, :, :], ACT.Exp).then_inc(expd, 1)

        @block.vector
        def _(dve):
            own = Seq(dve, own_done)
            dve.wait_ge(mask_in, 16)
            for g2 in range(2):
                dve.tensor_tensor(BDv[:, :, g2, :],
                                  v_rep[:, g2 * HD:(g2 + 1) * HD].unsqueeze(1).broadcast_to([P, 8, HD]),
                                  mask[:, :].rearrange("p (c g) -> p c g", g=2)[:, :, g2].unsqueeze(2)
                                  .broadcast_to([P, 8, HD]), ALU.mult).then_inc(bd_done, 1)
            dve.wait_ge(scores, 1)
            own.link(dve.tensor_tensor(S[:, :, :], ps_s[:, :].rearrange("p (m n) -> p m n", n=PBLK),
                                       biasC[:, :, :, :].rearrange("p i h n -> p (i h) n"), ALU.add))
            own.link(dve.tensor_reduce(mx[:, :], S[:, :, :], AX, ALU.max))
            own.link(dve.tensor_scalar(mx[:, :], mx[:, :], FLOOR, None, ALU.max))
            dve.tensor_tensor(S[:, :, :], S[:, :, :], wide(mx[:, :]), ALU.subtract).then_inc(shifted, 1)
            dve.wait_ge(expd, 1)
            own.link(dve.tensor_reduce(sm[:, :], S[:, :, :], AX, ALU.add))
            own.link(dve.tensor_scalar(sm[:, :], sm[:, :], 1e-30, None, ALU.max))
            own.link(dve.reciprocal(sm[:, :], sm[:, :]))
            own.link(dve.tensor_tensor(sm[:, :].rearrange("p (i h) -> p i h", i=TILES),
                                       sm[:, :].rearrange("p (i h) -> p i h", i=TILES), gT[:, :, 0:16], ALU.mult))
            dve.tensor_tensor(S[:, :, :], S[:, :, :], wide(sm[:, :]), ALU.mult).then_inc(probs, 1)
            dve.wait_ge(turned, 1)
            dve.tensor_copy(PT[:, :], ps_t[:, :]).then_inc(turned_out, 1)
            for i in range(TILES):
                dve.wait_ge(outs, i + 1)
                dve.tensor_copy(Otok[:, i, :], ps_o[i % 2][:, :, :].rearrange("p a b -> p (a b)")).then_inc(outs_moved, 1)


def prompt_attention(c, HT, d, T_bias, Vtok, gT, Otok):
    nc = c.nc
    items = [(s, g2, br, i) for s in range(2) for g2 in range(2) for br in range(2) for i in range(TILES)]
    N = len(items)
    with ExitStack() as ctx:
        sem = lambda n: nc.alloc_semaphore(f"pa_{n}")
        sb = lambda n, s: ctx.enter_context(nc.sbuf_tensor(f"pa_{n}", s, F32))
        Qs = [sb(f"q{s}", [P, 2, SEQ]) for s in range(2)]
        Tb = [sb(f"bias{s}", [P, 2, SEQ]) for s in range(2)]
        Sb = [sb(f"scores{j}", [P, SEQ]) for j in range(3)]
        E = [sb(f"exp{j}", [P, SEQ]) for j in range(3)]
        ET = [sb(f"expT{j}", [P, SEQ]) for j in range(2)]
        nm = sb("neg_max", [P, 2 * 16])
        rs = sb("row_sum", [P, 2 * 16])
        sc = sb("scale", [P, 2, 16])
        tmp = sb("tmp", [P, 16, HD])
        ps_s = [ctx.enter_context(nc.psum_tensor(f"pa_s{j}", [P, 512], F32)) for j in range(2)]
        ps_t = [ctx.enter_context(nc.psum_tensor(f"pa_t{j}", [P, 512], F32)) for j in range(2)]
        ps_o = [ctx.enter_context(nc.psum_tensor(f"pa_o{j}", [P, 2, 512], F32)) for j in range(2)]
        staged, cleared = [sem(f"chunk{s}_staged") for s in range(2)], sem("cleared")
        scored, biased, expd, turned, turned_out, mixed, merged, own_done = [sem(n) for n in
            ("scores", "biased", "exp", "turned", "turned_out", "mixed", "merged", "chain")]
        kv_saved = sem("kv_saved")
        block = ctx.enter_context(nc.Block())
        waited = sem("waited")
        n_merge = 6

        @block.sync
        def _(sp):
            sp.dma_start(d["kv_out"], HT[:, CK_U:GATE_U, :]).then_inc(kv_saved, 16)
            sp.wait_ge(kv_saved, 16)

        @block.gpsimd
        def _(pool):
            pool.wait_ge(cleared, 2)
            with pool.Fori(0, GP) as gp:
                with pool.Fori(0, 2) as rr:
                    for s in range(2):
                        pool.wait_ge(merged, (gp * 4 + rr * 2) + (s + 1))
                        u = gp * REP + rr * 2 + s
                        own = Seq(pool, staged[s], (gp * 2 + rr) * 4)
                        for g2 in range(2):
                            rows = slice(g2 * HD, (g2 + 1) * HD)
                            own.link(pool.tensor_copy(Qs[s][rows, g2, :], HT[rows, bass.ds(u, 1), 0:SEQ]
                                                      .rearrange("p o t -> p (o t)")))
                            own.link(pool.tensor_copy(Tb[s][:, g2, :], T_bias[:, bass.ds(u * 2 + g2, 1), :]
                                                      .rearrange("p o t -> p (o t)")))

        @block.tensor
        def _(pe):
            with pe.Fori(0, GP) as gp:
                with pe.Fori(0, 2) as rr:
                    it = gp * 2 + rr
                    for n in range(N + 3):
                        if n < N:
                            s, g2, br, i = items[n]
                            if n % 16 == 0:
                                pe.wait_ge(staged[s], it * 4 + 4)
                            if n >= 2:
                                pe.wait_ge(biased, it * N + (n - 1))
                            pe.matmul(ps_s[n % 2][:, 0:(i + 1) * P], Qs[s][:, g2, i * P:(i + 1) * P],
                                      HT[:, bass.ds(gp + (SK_U + 4 * br), 1), 0:(i + 1) * P]
                                      .rearrange("p o t -> p (o t)"), start=True, stop=True).then_inc(scored, 1)
                        if 2 <= n < N + 2:
                            m = n - 2
                            s, g2, br, i = items[m]
                            pe.wait_ge(expd, it * N + (m + 1))
                            if m >= 2:
                                pe.wait_ge(turned_out, it * N + (m - 1))
                            for j in range(i + 1):
                                mm = pe.transpose(ps_t[m % 2][:, j * P:(j + 1) * P], E[m % 3][:, j * P:(j + 1) * P],
                                                  c.ident[:, :])
                            mm.then_inc(turned, 1)
                        if n >= 3:
                            m = n - 3
                            s, g2, br, i = items[m]
                            pe.wait_ge(turned_out, it * N + (m + 1))
                            if m % 16 == 0:
                                pe.wait_ge(merged, it * 2 + (s + 1))
                            at = (br * 2 + g2) * TILES + i
                            out = ps_o[s][:, at // 8, (at % 8) * HD:(at % 8 + 1) * HD]
                            for j in range(i + 1):
                                v = Vtok[:, j, :].rearrange("p (b n) -> p b n", b=2)[:, br, :]
                                mm = pe.matmul(out, ET[m % 2][:, j * P:(j + 1) * P],
                                               v[:, bass.ds(gp * P + g2 * HD, HD)], start=j == 0, stop=j == i)
                            mm.then_inc(mixed, 1)

        @block.scalar
        def _(act):
            with act.Fori(0, GP) as gp:
                with act.Fori(0, 2) as rr:
                    it = gp * 2 + rr
                    for n, (s, g2, br, i) in enumerate(items):
                        act.wait_ge(biased, it * N + (n + 1))
                        if n >= 3:
                            act.wait_ge(turned, it * N + (n - 2))
                        w = (i + 1) * P
                        k = s * 16 + (br * 2 + g2) * TILES + i
                        act.activation(E[n % 3][:, 0:w], Sb[n % 3][:, 0:w], ACT.Exp, bias=nm[:, k:k + 1], scale=-1.0,
                                       accum_out=rs[:, k:k + 1]).then_inc(expd, 1)

        @block.vector
        def _(dve):
            for s in range(2):
                dve.memset(Qs[s][:, :, :], 0.0).then_inc(cleared, 1)
            dve.sem_inc(merged, 1)
            dve.sem_inc(merged, 1)
            with dve.Fori(0, GP) as gp:
                with dve.Fori(0, 2) as rr:
                    it = gp * 2 + rr
                    own = Seq(dve, own_done, it * (2 * n_merge))

                    def merge(s):
                        dve.wait_ge(mixed, it * N + 16 * (s + 1))
                        k = slice(s * 16, (s + 1) * 16)
                        own.link(dve.reciprocal(sc[:, s, :], rs[:, k]))
                        for br in range(2):
                            g = gT[:, :, 16 * (br + 1):16 * (br + 2)].rearrange("p i (c g) -> p c g i", g=2)
                            o = sc[:, s, 8 * br:8 * br + 8].rearrange("p (g i) -> p g i", g=2)
                            own(dve.tensor_tensor(o, o, g[:, bass.ds(gp * REP + rr * 2 + s, 1)]
                                                  .rearrange("p o g i -> p (o g) i"), ALU.mult))
                        own.wait()
                        own.link(dve.tensor_tensor(tmp[:, :, :], ps_o[s][:, :, :].rearrange("p a (b n) -> p (a b) n", n=HD),
                                                   sc[:, s, :].unsqueeze(2).broadcast_to([P, 16, HD]), ALU.mult))
                        own.link(dve.tensor_tensor(tmp[:, 0:8, :], tmp[:, 0:8, :], tmp[:, 8:16, :], ALU.add))
                        o = Otok[:, :, :].rearrange("p i (c n) -> p c i n", n=P)[:, bass.ds(gp * REP + rr * 2 + s, 1)]\
                            .rearrange("p o i n -> p (o i) n")
                        for g2 in range(2):
                            og = o[:, :, g2 * HD:(g2 + 1) * HD]
                            ins = dve.tensor_tensor(og, og, tmp[:, 4 * g2:4 * g2 + 4, :], ALU.add)
                            if g2 == 0:
                                own.link(ins)
                            else:
                                ins.then_inc(merged, 1)

                    for n in range(N + 2):
                        if n < N:
                            s, g2, br, i = items[n]
                            w = (i + 1) * P
                            k = s * 16 + (br * 2 + g2) * TILES + i
                            dve.wait_ge(scored, it * N + (n + 1))
                            if n >= 3:
                                dve.wait_ge(expd, it * N + (n - 2))
                            dve.sem_inc(waited, 1)
                            dve.tensor_tensor_reduce(Sb[n % 3][:, 0:w], ps_s[n % 2][:, 0:w],
                                                     Tb[s][:, g2, SEQ - w:SEQ], -1.0, 3e38, ALU.add, ALU.min,
                                                     nm[:, k:k + 1]).then_inc(biased, 1)
                        if n >= 2:
                            m = n - 2
                            s, g2, br, i = items[m]
                            dve.wait_ge(turned, it * N + (m + 1))
                            if m >= 2:
                                dve.wait_ge(mixed, it * N + (m - 1))
                            dve.tensor_copy(ET[m % 2][:, 0:(i + 1) * P], ps_t[m % 2][:, 0:(i + 1) * P])\
                               .then_inc(turned_out, 1)
                        if n == 20:
                            merge(0)
                    merge(1)
                    assert own.n == 2 * (n_merge)


def turn_outputs(c, Otok):
    nc = c.nc
    with ExitStack() as ctx:
        ps = [ctx.enter_context(nc.psum_tensor(f"to_ps{j}", [P, 512], F32)) for j in range(2)]
        turned = nc.alloc_semaphore("to_turned")
        moved = nc.alloc_semaphore("to_moved")
        block = ctx.enter_context(nc.Block())

        @block.tensor
        def _(pe):
            for u in range(KC):
                if u >= 2:
                    pe.wait_ge(moved, u - 1)
                for i in range(TILES):
                    mm = pe.transpose(ps[u % 2][:, i * P:(i + 1) * P], Otok[:, i, u * P:(u + 1) * P], c.ident[:, :])
                mm.then_inc(turned, 1)

        @block.vector
        def _(dve):
            for u in range(KC):
                dve.wait_ge(turned, u + 1)
                dve.tensor_copy(c.XW[:, u, 0:SEQ], ps[u % 2][:, :]).then_inc(moved, 1)


def sample_scores(c, HT, d, tabs, kcT, psS, psW, psM, consts):
    nc = c.nc
    PG, SLOTS = 8, 4
    with ExitStack() as ctx:
        sem = lambda n: nc.alloc_semaphore(f"ss_{n}")
        sb = lambda n, s: ctx.enter_context(nc.sbuf_tensor(f"ss_{n}", s, F32))
        oh = sb("onehot", [N_BUCKETS + 1, PAST + WIN + NBLK + 1])
        wk = sb("win_k", [P, NB, GP, WIN])
        kb = sb("k_pages", [P, SLOTS, PG, GP * P])
        qz = sb("q_padded", [P, NB * 272])
        loaded, wk_in, patched, out_done, cleared, q_in = [sem(n) for n in
            ("loaded", "win_in", "win_patched", "win_out", "cleared", "q_in")]
        k_in_sw = [sem(f"pages{s}_in_by_pool") for s in range(SLOTS)]
        k_in = [sem(f"pages{s}_in") for s in range(SLOTS)]
        k_used = [sem(f"pages{s}_used") for s in range(SLOTS)]
        block = ctx.enter_context(nc.Block())
        q_of = lambda b, g: qz[:, (b * GP + g) * P:(b * GP + g + 1) * P]

        @block.sync
        def _(sp):
            sp.dma_start(oh[:, :], d["onehot_sample"]).then_inc(loaded, 16)
            sp.dma_start(consts[0][:, :], d["batch_mask"]).then_inc(loaded, 16)
            sp.dma_start(consts[1][:, :], d["group_sum"]).then_inc(loaded, 16)
            sp.dma_start(wk[:, :, :, :], d["win_k"]).then_inc(wk_in, 16)
            for n in range(NB * PAGES // PG):
                s = n % SLOTS
                if n >= SLOTS:
                    sp.wait_ge(k_used[s], n // SLOTS)
                load_pages(sp, c, kb[:, s, 0:3], d["slc_k"], n * PG, 3, k_in[s])
            sp.wait_ge(patched, 1)
            sp.dma_start(d["win_k_out"], wk[:, :, :, :]).then_inc(out_done, 16)
            sp.wait_ge(out_done, 16)

        @block.scalar
        def _(act):
            for n in range(NB * PAGES // PG):
                s = n % SLOTS
                if n >= SLOTS:
                    act.wait_ge(k_used[s], n // SLOTS)
                load_pages(act, c, kb[:, s, 3:6], d["slc_k"], n * PG + 3, 3, k_in[s])

        @block.gpsimd
        def _(pool):
            pool.memset(qz[:, :], 0.0).then_inc(cleared, 1)
            for n in range(NB * PAGES // PG):
                s = n % SLOTS
                if n >= SLOTS:
                    pool.wait_ge(k_used[s], n // SLOTS)
                load_pages(pool, c, kb[:, s, 6:8], d["slc_k"], n * PG + 6, 2, k_in_sw[s])

        @block.vector
        def _(dve):
            dve.wait_ge(wk_in, 16)
            dve.tensor_copy(wk[:, :, :, WIN - 1], HT[:, WK_U:WK_U + 2, SEQ:T].rearrange("p g b -> p b g"))\
               .then_inc(patched, 1)
            dve.wait_ge(cleared, 1)
            v = qz[:, :].rearrange("p (b x) -> p b x", x=272)
            for g2 in range(2):
                rows = slice(g2 * HD, (g2 + 1) * HD)
                for g in range(GP):
                    at = g * 136 + g2
                    dve.tensor_copy(v[rows, :, at:at + 7:2], HT[rows, g * REP:(g + 1) * REP, SEQ:T]
                                    .rearrange("p r b -> p b r")).then_inc(q_in, 1)

        @block.tensor
        def _(pe):
            pe.wait_ge(loaded, 48)
            tab = tabs[:, 16:16 + P]
            for j in range(4):
                pe.matmul(psS[:, j, :], tab, oh[:, j * 512:(j + 1) * 512], start=True, stop=False, skip_group_check=True)
            pe.matmul(psW[:, :], tab, oh[:, PAST:PAST + WIN], start=True, stop=False, skip_group_check=True)
            pe.matmul(psM[:, 0:NBLK + 1], tab, oh[:, PAST + WIN:], start=True, stop=False, skip_group_check=True)
            pe.wait_ge(q_in, 4)
            pe.wait_ge(patched, 1)
            for b in range(NB):
                for g in range(GP):
                    last = b == NB - 1 and g == GP - 1
                    pe.matmul(psW[:, :], q_of(b, g), wk[:, b, g, :], start=False, stop=last, skip_group_check=True)
                    pe.matmul(psM[:, 0:NBLK], q_of(b, g),
                              kcT[:, b * PAGES * 4:(b + 1) * PAGES * 4].rearrange("p (n x) -> p n x", x=4)[:, :, 2 * g:2 * g + 2],
                              start=False, stop=last, skip_group_check=True)
                    pe.matmul(psM[:, NBLK:NBLK + 1], q_of(b, g), HT[:, SK_U + g, SEQ + b:SEQ + b + 1],
                              start=False, stop=last, skip_group_check=True)
            for n in range(NB * PAGES // PG):
                s, b = n % SLOTS, n * PG // PAGES
                pe.wait_ge(k_in[s], 16 * 6 * (n // SLOTS + 1))
                pe.wait_ge(k_in_sw[s], 16 * 2 * (n // SLOTS + 1))
                for j in range(PG // 4):
                    bank = (n * PG % PAGES) // 4 + j
                    for g in range(GP):
                        mm = pe.matmul(psS[:, bank, :], q_of(b, g), kb[:, s, 4 * j:4 * j + 4, g * P:(g + 1) * P],
                                       start=False, stop=(b == NB - 1 and g == GP - 1), skip_group_check=True)
                mm.then_inc(k_used[s], 1)


V_PG, V_SLOTS = 8, 4


def sample_softmax(c, d, Ps, psS, psW, psM, consts, Vnew, early):
    nc = c.nc
    Pslc, Pwin, Pcmp = Ps
    bmask, gsum = consts
    wv, vb, Vn, wv_in, vn_in, patched, v_in, v_in_sw = early
    with ExitStack() as ctx:
        sem = lambda n: nc.alloc_semaphore(f"sx_{n}")
        sb = lambda n, s: ctx.enter_context(nc.sbuf_tensor(f"sx_{n}", s, F32))
        ps_i = ctx.enter_context(nc.psum_tensor("sx_ps", [P, 512], F32))
        g = sb("gates", [P, 3])
        nm = sb("neg_max", [P, 4])
        sm = sb("sums", [P, 4])
        pc = sb("cmp", [P, NBLK])
        pcg = sb("cmp_gated", [P, NBLK])
        score = sb("score", [P, NBLK + 1])
        top = sb("top", [P, 8])
        drop = sb("drop", [P, NBLK + 1])
        g_in, own_done, shifted, expd, cmp_ready, summed = [sem(n) for n in
            ("gates_in", "chain", "max_ready", "exp", "cmp_ready", "group_sums")]
        block = ctx.enter_context(nc.Block())

        @block.sync
        def _(sp):
            with nc.allow_non_contiguous_dma(reason="384 numbers"):
                for b in range(NB):
                    sp.dma_start(g[b * HEADS:(b + 1) * HEADS, :],
                                 d["gate_scratch"].rearrange("(r h) b -> b h r", r=3)[b]).then_inc(g_in, 16)
            sp.dma_start(wv[:, :, :, :], d["win_v"]).then_inc(wv_in, 16)
            load_pages(sp, c, vb[:, 0, 0:6], d["slc_v"], 0, 6, v_in[0])

        @block.gpsimd
        def _(pool):
            load_pages(pool, c, vb[:, 0, 6:8], d["slc_v"], 6, 2, v_in_sw[0])
            for b in range(NB):
                pool.dma_start(Vn[0:1, b, :], Vnew[b:b + 1, 0:2 * P]).then_inc(vn_in, 16)
            pool.wait_ge(wv_in, 16)
            for b in range(NB):
                pool.dma_start(wv[P - 1:P, b, 3, :], Vnew[b:b + 1, 2 * P:4 * P]).then_inc(patched, 16)


        @block.tensor
        def _(pe):
            pe.wait_ge(cmp_ready, 1)
            pe.matmul(ps_i[:, 0:NBLK], gsum[:, :], pc[:, :], start=True, stop=True).then_inc(summed, 1)

        @block.scalar
        def _(act):
            act.wait_ge(shifted, 1)
            act.activation(pc[:, :], psM[:, 0:NBLK], ACT.Exp, bias=nm[:, 0:1], accum_out=sm[:, 0:1]).then_inc(expd, 1)
            act.wait_ge(shifted, 2)
            act.activation(Pwin[:, :], psW[:, :], ACT.Exp, bias=nm[:, 1:2], accum_out=sm[:, 1:2]).then_inc(expd, 1)
            act.wait_ge(shifted, 3)
            act.activation(Pslc[:, :], Pslc[:, :], ACT.Exp, bias=nm[:, 2:3], accum_out=sm[:, 2:3]).then_inc(expd, 1)

        @block.vector
        def _(dve):
            own = Seq(dve, own_done)
            own.link(dve.tensor_reduce(nm[:, 0:1], psM[:, 0:NBLK], AX, ALU.max))
            dve.tensor_scalar(nm[:, 0:1], nm[:, 0:1], -1.0, None, ALU.mult).then_inc(shifted, 1)
            own.link(dve.tensor_reduce(nm[:, 1:2], psW[:, :], AX, ALU.max))
            dve.tensor_scalar(nm[:, 1:2], nm[:, 1:2], -1.0, None, ALU.mult).then_inc(shifted, 1)
            dve.wait_ge(expd, 1)
            own.link(dve.reciprocal(sm[:, 3:4], sm[:, 0:1]))
            dve.tensor_scalar(pc[:, :], pc[:, :], sm[:, 3:4], None, ALU.mult).then_inc(cmp_ready, 1)
            dve.wait_ge(g_in, 16 * NB)
            dve.wait_ge(cmp_ready, 1)
            own.link(dve.tensor_scalar(pcg[:, :], pc[:, :], g[:, 0:1], None, ALU.mult))
            for par in range(2):
                own(dve.tensor_tensor(Pcmp[:, par].rearrange("p (b n) -> p b n", b=NB),
                                      pcg[:, par:NBLK:2].unsqueeze(1).broadcast_to([P, NB, PAGES]),
                                      bmask[:, :].unsqueeze(2).broadcast_to([P, NB, PAGES]), ALU.mult))
            dve.wait_ge(summed, 1)
            own.link(dve.tensor_copy(score[:, 0:NBLK], ps_i[:, 0:NBLK]))
            own(dve.memset(score[:, 0:1], 1e4))
            own.link(dve.memset(score[:, NBLK - 1:NBLK + 1], 1e4))
            for r in range(2):
                own.link(dve.max(top[:, :], score[:, :]))
                own.link(dve.match_replace(score[:, :], top[:, :], score[:, :], NEG))
            own.link(dve.tensor_scalar(drop[:, :], score[:, :], FLOOR, NEG, ALU.is_gt, ALU.mult))
            own(dve.tensor_tensor(Pslc[:, 0:PAST].rearrange("p (n t) -> p n t", t=BLOCK),
                                  psS[:, :, :].rearrange("p a (n t) -> p (a n) t", t=BLOCK),
                                  drop[:, 0:NBLK].unsqueeze(2).broadcast_to([P, NBLK, BLOCK]), ALU.add))
            own.link(dve.tensor_tensor(Pslc[:, PAST:PAST + 1], psM[:, NBLK:NBLK + 1], drop[:, NBLK:NBLK + 1], ALU.add))
            own.link(dve.tensor_reduce(nm[:, 2:3], Pslc[:, :], AX, ALU.max))
            dve.tensor_scalar(nm[:, 2:3], nm[:, 2:3], -1.0, None, ALU.mult).then_inc(shifted, 1)
            dve.wait_ge(expd, 2)
            own.link(dve.reciprocal(sm[:, 1:2], sm[:, 1:2]))
            own.link(dve.tensor_tensor(sm[:, 1:2], sm[:, 1:2], g[:, 2:3], ALU.mult))
            own(dve.tensor_scalar(Pwin[:, :], Pwin[:, :], sm[:, 1:2], None, ALU.mult))
            dve.wait_ge(expd, 3)
            own.link(dve.reciprocal(sm[:, 2:3], sm[:, 2:3]))
            own.link(dve.tensor_tensor(sm[:, 2:3], sm[:, 2:3], g[:, 1:2], ALU.mult))
            own(dve.tensor_scalar(Pslc[:, :], Pslc[:, :], sm[:, 2:3], None, ALU.mult))


def sample_values(c, d, Ps, vcS, early):
    nc = c.nc
    Pslc, Pwin, Pcmp = Ps
    PG, SLOTS = V_PG, V_SLOTS
    wv, vb, Vn, _, vn_in, patched, v_in, v_in_sw = early
    turns = [Pslc[:, j * P:(j + 1) * P] for j in range(16)] + [Pwin[:, j * P:(j + 1) * P] for j in range(4)] + \
            [Pcmp[:, par, :] for par in range(2)]
    with ExitStack() as ctx:
        sem = lambda n: nc.alloc_semaphore(f"sv_{n}")
        sb = lambda n, s: ctx.enter_context(nc.sbuf_tensor(f"sv_{n}", s, F32))
        PT = sb("probsT", [P, len(turns), P])
        PTn = sb("probsT_new", [1, P])
        ps_t = [ctx.enter_context(nc.psum_tensor(f"sv_t{j}", [P, 512], F32)) for j in range(2)]
        po = ctx.enter_context(nc.psum_tensor("sv_o", [HEADS, NB, 2 * P], F32))
        ps_back = ctx.enter_context(nc.psum_tensor("sv_back", [P, NB, GP, HEADS], F32))
        O = Pslc[0:HEADS, 0:NB * 2 * P].rearrange("p (b n) -> p b n", b=NB)
        summed, back = sem("sums_out"), sem("turned_back")
        out_done, turned, moved, mixed, picked = [sem(n) for n in ("win_out", "turned", "moved", "mixed", "picked")]
        v_used = [sem(f"pages{s}_used") for s in range(SLOTS)]
        block = ctx.enter_context(nc.Block())
        rounds = (len(turns) + 4) // 4

        @block.sync
        def _(sp):
            for n in range(1, NB * PAGES // PG):
                s = n % SLOTS
                if n >= SLOTS:
                    sp.wait_ge(v_used[s], n // SLOTS)
                load_pages(sp, c, vb[:, s, 0:3], d["slc_v"], n * PG, 3, v_in[s])
                if n == 2:
                    sp.wait_ge(patched, 16 * NB)
                    sp.dma_start(d["win_v_out"], wv[:, :, :, :]).then_inc(out_done, 16)
            sp.wait_ge(out_done, 16)

        @block.scalar
        def _(act):
            for n in range(1, NB * PAGES // PG):
                s = n % SLOTS
                if n >= SLOTS:
                    act.wait_ge(v_used[s], n // SLOTS)
                load_pages(act, c, vb[:, s, 3:6], d["slc_v"], n * PG + 3, 3, v_in[s])

        @block.gpsimd
        def _(pool):
            for n in range(1, NB * PAGES // PG):
                s = n % SLOTS
                if n >= SLOTS:
                    pool.wait_ge(v_used[s], n // SLOTS)
                load_pages(pool, c, vb[:, s, 6:8], d["slc_v"], n * PG + 6, 2, v_in_sw[s])

        @block.tensor
        def _(pe):
            for r in range(rounds):
                if r >= 2:
                    pe.wait_ge(moved, r - 1)
                for j in range(r * 4, min(r * 4 + 4, len(turns))):
                    mm = pe.transpose(ps_t[r % 2][:, (j % 4) * P:(j % 4 + 1) * P], turns[j], c.ident[:, :])
                if r == rounds - 1:
                    j = len(turns)
                    mm = pe.transpose(ps_t[r % 2][0:1, (j % 4) * P:(j % 4 + 1) * P], Pslc[:, PAST:PAST + 1], c.ident[:, :])
                mm.then_inc(turned, 1)
            pe.wait_ge(moved, rounds + 1)
            probs = lambda tile, b: PT[:, tile, b * HEADS:(b + 1) * HEADS]
            for b in range(NB):
                for par in range(2):
                    pe.matmul(po[:, b, :], probs(20 + par, b), vcS[:, :].rearrange("p (g x n) -> p x g n", g=GP, x=2)[:, par],
                              start=b % 2 == 0 and par == 0, stop=False, skip_group_check=True)
            for n in range(NB * PAGES // PG):
                s, b = n % SLOTS, n * PG // PAGES
                pe.wait_ge(v_in[s], 16 * 6 * (n // SLOTS + 1))
                pe.wait_ge(v_in_sw[s], 16 * 2 * (n // SLOTS + 1))
                for j in range(PG):
                    mm = pe.matmul(po[:, b, :], probs((n * PG) % PAGES + j, b), vb[:, s, j, :], start=False, stop=False,
                                   skip_group_check=True)
                mm.then_inc(v_used[s], 1)
            pe.wait_ge(vn_in, 16 * NB)
            pe.wait_ge(patched, 16 * NB)
            for b in range(NB):
                for j in range(4):
                    pe.matmul(po[:, b, :], probs(16 + j, b), wv[:, b, j, :], start=False, stop=False, skip_group_check=True)
                mm = pe.matmul(po[:, b, :], PTn[0:1, b * HEADS:(b + 1) * HEADS], Vn[0:1, b, :], start=False,
                               stop=b % 2 == 1, skip_group_check=True)
            mm.then_inc(mixed, 1)
            pe.wait_ge(summed, 1)
            for b in range(NB):
                for g in range(GP):
                    mm = pe.transpose(ps_back[:, b, g, :], O[:, b, g * P:(g + 1) * P], c.ident[0:HEADS, 0:HEADS])
            mm.then_inc(back, 1)

        @block.vector
        def _(dve):
            for r in range(rounds):
                dve.wait_ge(turned, r + 1)
                k = min(4, len(turns) - r * 4)
                dve.tensor_copy(PT[:, r * 4:r * 4 + k, :], ps_t[r % 2][:, 0:k * P].rearrange("p (k n) -> p k n", n=P))\
                   .then_inc(moved, 1)
                if r == rounds - 1:
                    j = len(turns) % 4
                    dve.tensor_copy(PTn[0:1, :], ps_t[r % 2][0:1, j * P:(j + 1) * P]).then_inc(moved, 1)
            dve.wait_ge(mixed, 1)
            dve.tensor_copy(O[:, :, :], po[:, :, :]).then_inc(summed, 1)
            dve.wait_ge(back, 1)
            for g2 in range(2):
                rows = slice(g2 * HD, (g2 + 1) * HD)
                for g in range(GP):
                    at = g * 8 + g2
                    dve.tensor_copy(c.XW[rows, g * REP:(g + 1) * REP, SEQ:T],
                                    ps_back[rows, :, g, at:at + 7:2].rearrange("p b r -> p r b")).then_inc(picked, 1)


def hgrn_gates(c, HT, d):
    nc = c.nc
    with ExitStack() as ctx:
        sem = lambda n: nc.alloc_semaphore(f"hg_{n}")
        sb = lambda n, s: ctx.enter_context(nc.sbuf_tensor(f"hg_{n}", s, F32))
        lg = sb("logits", [P, 2, HH])
        mx = sb("max", [P, HH])
        lb = sb("lb", [P, HH])
        om = sb("one_minus_lb", [P, HH])
        loaded, shifted, expd, sig, own_done, f_done = [sem(n) for n in
            ("loaded", "shifted", "exp", "sigmoids", "chain", "f")]
        block = ctx.enter_context(nc.Block())

        @block.sync
        def _(sp):
            sp.dma_start(lg[:, :, :], d["lb_logits"]).then_inc(loaded, 16)

        @block.scalar
        def _(act):
            act.activation(HT[:, 8:16, :], HT[:, 8:16, :], ACT.Sigmoid).then_inc(sig, 1)
            act.activation(HT[:, 24:32, :], HT[:, 24:32, :], ACT.Sigmoid).then_inc(sig, 1)
            act.activation(HT[:, 0:8, :], HT[:, 0:8, :], ACT.Silu).then_inc(sig, 1)
            act.wait_ge(shifted, 1)
            act.activation(lg[:, :, :], lg[:, :, :], ACT.Exp).then_inc(expd, 1)

        @block.vector
        def _(dve):
            own = Seq(dve, own_done)
            dve.wait_ge(loaded, 16)
            own.link(dve.tensor_tensor(mx[:, :], lg[:, 0, :], lg[:, 1, :], ALU.max))
            dve.tensor_tensor(lg[:, :, :], lg[:, :, :], mx[:, :].unsqueeze(1).broadcast_to([P, 2, HH]),
                              ALU.subtract).then_inc(shifted, 1)
            dve.wait_ge(expd, 1)
            own.link(dve.tensor_tensor(mx[:, :], lg[:, 0, :], lg[:, 1, :], ALU.add))
            own.link(dve.reciprocal(mx[:, :], mx[:, :]))
            own.link(dve.tensor_tensor(lg[:, :, :], lg[:, :, :], mx[:, :].unsqueeze(1).broadcast_to([P, 2, HH]), ALU.mult))
            own.link(dve.tensor_tensor(lb[:, :], lg[:, 0, :], lg[:, 1, :], ALU.add))
            own.link(dve.tensor_tensor(lb[:, :], lb[:, :], lg[:, 0, :], ALU.subtract))
            own.link(dve.tensor_scalar(om[:, :], lb[:, :], -1.0, 1.0, ALU.mult, ALU.add))
            dve.wait_ge(sig, 1)
            for h in range(HH):
                dve.tensor_scalar(HT[:, 8 + h, :], HT[:, 8 + h, :], om[:, h:h + 1], lb[:, h:h + 1], ALU.mult, ALU.add)\
                   .then_inc(f_done, 1)


def hgrn_prompt(c, HT, d):
    nc = c.nc
    fine = [0, 16, 8, 4, 2, 1]
    MASKS = [16, 8, 4, 2, 1, 0]
    NL, NF = len(LEVELS), len(fine)
    COARSE = 4
    PICKS = {5: (0, 1), 6: (2, 3, 4, 5)}
    NE = NL + 2
    NM = 2 * NL + 1
    with ExitStack() as ctx:
        sem = lambda n: nc.alloc_semaphore(f"hp_{n}")
        sb = lambda n, s, t=F32: ctx.enter_context(nc.sbuf_tensor(f"hp_{n}", s, t))
        two = lambda n: [sb(f"{n}_{x}", [P, SEQ]) for x in range(2)]
        q, k, v, eG, ke, qe = [two(n) for n in ("q", "k", "v", "eG", "ke", "qe")]
        M = {m: two(f"m{m}") for m in LEVELS + [1]}
        lf, G, reset = [sb(n, [P, SEQ]) for n in ("log_f", "G", "reset")]
        Dl = [sb(f"diff{j}", [P, SEQ]) for j in range(2)]
        vt, kt = sb("v_tok", [P, SEQ]), sb("ke_tok", [P, SEQ])
        A = sb("A", [P, SEQ])
        masks = sb("masks", [P, NF, P], I32)
        S = [sb(f"S{j}", [P, P]) for j in range(2)]
        Sout = sb("S_out", [P, HH, P])
        ps_a = ctx.enter_context(nc.psum_tensor("hp_a", [P, 512], F32))
        ps_f = [ctx.enter_context(nc.psum_tensor(f"hp_f{j}", [P, 512], F32)) for j in range(2)]
        ps_t = [ctx.enter_context(nc.psum_tensor(f"hp_t{j}", [P, 512], F32)) for j in range(2)]
        ps_o = ctx.enter_context(nc.psum_tensor("hp_o", [P, 512], F32))
        ps_s = ctx.enter_context(nc.psum_tensor("hp_s", [P, 512], F32))
        const_in, cleared, staged, k_in, logs, scanned, diff, expd, mult, extra, turned, turned_out, coarse, \
            coarse_out, fine_done, fine_out, s_new, s_out, o_done, o_out, waited, saved = [sem(n) for n in
            ("const_in", "cleared", "staged", "keys", "logs", "scanned", "diffs", "exps", "products", "pool_products",
             "turned", "turned_out", "coarse", "coarse_out", "fine", "fine_out", "state_products", "states", "outputs",
             "outputs_out", "waited", "saved")]
        waited_pool = sem("pool_waited")
        block = ctx.enter_context(nc.Block())
        tiles = lambda a: a.rearrange("p (i t) -> p i t", i=TILES)
        of = lambda src, h: src[:, bass.ds(h, 1), 0:SEQ].rearrange("p o t -> p (o t)")

        def steps(eng, step):
            step(0, None, None, 0)
            step(1, 0, None, 1)
            with eng.Fori(0, HH // 2 - 2) as i:
                step(i * 2 + 2, i * 2 + 1, i * 2, 0)
                step(i * 2 + 3, i * 2 + 2, i * 2 + 1, 1)
            step(HH - 2, HH - 3, HH - 4, 0)
            step(HH - 1, HH - 2, HH - 3, 1)
            step(None, HH - 1, HH - 2, 0)
            step(None, None, HH - 1, 1)

        def has_next(h):
            return h is not None and not (isinstance(h, int) and h == HH - 1)

        def head_free(eng, h):
            if not (isinstance(h, int) and h == 0):
                eng.wait_ge(o_out, h)

        def inputs_free(eng, h):
            if not isinstance(h, int) or h >= 2:
                eng.wait_ge(fine_done, (h - 2) * NF + 1)
                eng.wait_ge(mult, (h - 1) * NM)
                eng.wait_ge(extra, (h - 1) * 3)

        def factors_free(eng, h):
            if not isinstance(h, int) or h >= 2:
                eng.wait_ge(fine_done, (h - 1) * NF)

        @block.sync
        def _(sp):
            sp.dma_start(masks[:, :, :], d["level_masks"]).then_inc(const_in, 16)
            sp.dma_start(reset[:, :], d["tile_reset"]).then_inc(const_in, 16)
            sp.wait_ge(s_out, 1 + HH * TILES)
            sp.dma_start(d["hgrn_p_out"], Sout[:, :, :]).then_inc(saved, 16)
            sp.wait_ge(saved, 16)

        def halves(a, m):
            b = a.rearrange("p (n two m) -> p n two m", two=2, m=m)
            return b[:, :, 0, :], b[:, :, 1, :]

        @block.gpsimd
        def _(pool):
            pool.memset(A[:, :], 0.0).then_inc(cleared, 1)
            pool.sem_inc(o_out, 1)

            def stage(h, p):
                inputs_free(pool, h)
                own = Seq(pool, staged, h * 2)
                pool.sem_inc(waited_pool, 1)
                own.link(pool.tensor_copy(q[p][:, :], of(HT, h)))
                pool.sem_inc(waited_pool, 1)
                own.link(pool.tensor_copy(v[p][:, :], of(HT, h + 16)))

            def step(h, hb, hc, p):
                if h is None:
                    return
                own = Seq(pool, extra, h * 3)
                factors_free(pool, h)
                m0, m1 = halves(M[1][p][:, :], 1)
                own.link(pool.tensor_tensor(m1, halves(q[p][:, :], 1)[1],
                                            HT[:, bass.ds(h + 8, 1), 1:SEQ:2].rearrange("p o t -> p (o t)").unsqueeze(2),
                                            ALU.mult))
                pool.wait_ge(k_in, h + 1)
                pool.sem_inc(waited_pool, 1)
                own.link(pool.tensor_copy(m0, halves(k[p][:, :], 1)[0]))
                if has_next(h):
                    stage(h + 1, 1 - p)
                pool.wait_ge(expd, h * NE + NE)
                head_free(pool, h)
                own.link(pool.tensor_tensor(qe[p][:, :], eG[p][:, :], q[p][:, :], ALU.mult))

            stage(0, 0)
            steps(pool, step)

        @block.vector
        def _(dve):
            dve.wait_ge(const_in, 32)
            dve.sem_inc(s_out, 1)

            def step(h, hb, hc, p):
                if h is not None and (not isinstance(h, int) or h >= 2):
                    dve.wait_ge(coarse, h - 1)
                for n in range(NL + 1):
                    if h is not None:
                        if n < NL:
                            diffs(h, n + 1)
                        if n == 0:
                            dve.wait_ge(k_in, h + 1)
                            dve.wait_ge(staged, h * 2 + 1)
                        if n == 2:
                            factors_free(dve, h)
                        mults(h, p, n)
                    if hc is not None and n < TILES:
                        state(hc, p, n)
                    if hb is not None:
                        for x in PICKS.get(n, ()):
                            pick(hb, x)
                if has_next(h):
                    start(h + 1)

            def start(h):
                dve.wait_ge(logs, h + 1)
                if not (isinstance(h, int) and h == 0):
                    dve.wait_ge(expd, h * NE)
                    dve.wait_ge(diff, h * NM)
                    dve.wait_ge(mult, h * NM)
                dve.tensor_tensor_scan(G[:, :], reset[:, :], lf[:, :], 0.0, ALU.mult, ALU.add).then_inc(scanned, 1)
                dve.wait_ge(scanned, h + 1)
                diffs(h, 0)

            def diffs(h, n):
                dl = Dl[n % 2]
                if n >= 2:
                    dve.wait_ge(mult, h * NM + 2 * (n - 1))
                if n < NL:
                    m = LEVELS[n]
                    g0, g1 = halves(G[:, :], m)
                    d0, d1 = halves(dl[:, :], m)
                    ref = g0[:, :, m - 1:m].broadcast_to([P, SEQ // (2 * m), m])
                    dve.tensor_tensor(d0, ref, g0, ALU.subtract).then_inc(diff, 1)
                    dve.tensor_tensor(d1, g1, ref, ALU.subtract).then_inc(diff, 1)
                else:
                    end = tiles(G[:, :])[:, :, P - 1:P].broadcast_to([P, TILES, P])
                    dve.tensor_tensor(tiles(dl[:, :]), end, tiles(G[:, :]), ALU.subtract).then_inc(diff, 1)

            def mults(h, p, n):
                dl = Dl[n % 2]
                dve.wait_ge(expd, h * NE + (n + 1))
                if n < NL:
                    m = LEVELS[n]
                    d0, d1 = halves(dl[:, :], m)
                    m0, m1 = halves(M[m][p][:, :], m)
                    dve.tensor_tensor(m0, d0, halves(k[p][:, :], m)[0], ALU.mult).then_inc(mult, 1)
                    dve.tensor_tensor(m1, d1, halves(q[p][:, :], m)[1], ALU.mult).then_inc(mult, 1)
                else:
                    dve.tensor_tensor(ke[p][:, :], dl[:, :], k[p][:, :], ALU.mult).then_inc(mult, 1)

            def pick(h, n):
                if n == 0:
                    dve.wait_ge(cleared, 1)
                    dve.wait_ge(coarse_out, h * 3 + 3)
                else:
                    dve.wait_ge(fine_out, h * NF + n)
                dve.wait_ge(fine_done, h * NF + (n + 1))
                dve.sem_inc(waited, 1)
                dve.copy_predicated(tiles(A[:, :]), masks[:, MASKS.index(fine[n]), :].unsqueeze(1).broadcast_to([P, TILES, P]),
                                    tiles(ps_f[n % 2][:, :])).then_inc(fine_out, 1)

            def state(h, p, i):
                dve.wait_ge(s_new, h * TILES + (i + 1))
                dst = S[(i + 1) % 2][:, :] if i < TILES - 1 else Sout[:, bass.ds(h, 1), :].rearrange("p o n -> p (o n)")
                if i == 0:
                    dve.tensor_copy(dst, ps_s[:, 0:P]).then_inc(s_out, 1)
                else:
                    dve.wait_ge(s_out, h * TILES + (i + 1))
                    dve.scalar_tensor_tensor(dst, S[i % 2][:, :], eG[p][:, (i + 1) * P - 1:(i + 1) * P],
                                             ps_s[:, 0:P], ALU.mult, ALU.add).then_inc(s_out, 1)

            start(0)
            steps(dve, step)

        @block.scalar
        def _(act):
            def step(h, hb, hc, p):
                for n in range(NL + 1):
                    if h is not None:
                        act.wait_ge(diff, h * NM + min(2 * (n + 1), NM))
                        act.activation(Dl[n % 2][:, :], Dl[n % 2][:, :], ACT.Exp).then_inc(expd, 1)
                    if n == COARSE:
                        if hc is not None:
                            outputs(hc)
                        if hb is not None:
                            coarse_levels(hb)
                if h is not None:
                    act.wait_ge(scanned, h + 1)
                    head_free(act, h)
                    if not (isinstance(h, int) and h == 0):
                        act.wait_ge(s_out, (h - 1) * TILES + 1)
                    act.activation(eG[p][:, :], G[:, :], ACT.Exp).then_inc(expd, 1)
                if has_next(h):
                    prepare(h + 1, 1 - p)
                if hb is not None:
                    act.wait_ge(turned, hb * 2 + 2)
                    act.activation(kt[:, :], ps_t[1][:, :], ACT.Copy).then_inc(turned_out, 1)

            def outputs(h):
                act.wait_ge(o_done, h + 1)
                act.sem_inc(waited, 1)
                act.activation(of(c.XW, h), ps_o[:, :], ACT.Copy).then_inc(o_out, 1)

            def prepare(h, p):
                if not (isinstance(h, int) and h == 0):
                    act.wait_ge(scanned, h)
                act.sem_inc(waited, 1)
                act.activation(lf[:, :], of(HT, h + 8), ACT.Ln).then_inc(logs, 1)
                inputs_free(act, h)
                act.sem_inc(waited, 1)
                act.activation(k[p][:, :], of(HT, h + 8), ACT.Copy, bias=1.0, scale=-1.0).then_inc(k_in, 1)

            def coarse_levels(hb):
                act.wait_ge(turned, hb * 2 + 1)
                act.activation(vt[:, :], ps_t[0][:, :], ACT.Copy).then_inc(turned_out, 1)
                act.wait_ge(coarse, hb + 1)
                act.wait_ge(cleared, 1)
                A4, a4 = tiles(A[:, :]), tiles(ps_a[:, :])
                for r0, r1, t0, t1 in ((0, 64, 64, 128), (0, 32, 32, 64), (64, 96, 96, 128)):
                    act.activation(A4[r0:r1, :, t0:t1], a4[r0:r1, :, t0:t1], ACT.Copy).then_inc(coarse_out, 1)

            prepare(0, 0)
            steps(act, step)

        @block.tensor
        def _(pe):
            def step(_, h, hc, pa):
                p = 1 - pa
                if h is not None:
                    pe.wait_ge(staged, h * 2 + 2)
                    pe.wait_ge(mult, h * NM + 4)
                if hc is not None:
                    pe.wait_ge(extra, hc * 3 + 3)
                    pe.wait_ge(turned_out, hc * 2 + 2)
                    pe.wait_ge(fine_out, hc * NF + NF)
                    pe.wait_ge(coarse_out, hc * 3 + 3)
                    pe.wait_ge(o_out, hc + 1)
                for i in range(TILES):
                    if hc is not None:
                        tile(hc, pa, i)
                    if h is not None:
                        coarse_levels(h, p, i)
                if h is not None:
                    fine_levels(h, p)

            def tile(h, p, i):
                t = slice(i * P, (i + 1) * P)
                pe.wait_ge(s_out, h * TILES + (i + 1))
                pe.matmul(ps_s[:, 0:P], kt[:, t], vt[:, t], start=True, stop=True).then_inc(s_new, 1)
                mm = pe.matmul(ps_o[:, t], vt[:, t], A[:, t], start=True, stop=i == 0)
                if i:
                    mm = pe.matmul(ps_o[:, t], S[i % 2][:, :], qe[p][:, t], start=False, stop=True)
                if i == TILES - 1:
                    mm.then_inc(o_done, 1)

            def coarse_levels(h, p, i):
                mm = pe.transpose(ps_t[0][:, i * P:(i + 1) * P], v[p][:, i * P:(i + 1) * P], c.ident[:, :])
                if i == TILES - 1:
                    mm.then_inc(turned, 1)
                for m in (64, 32):
                    for b in range(P // (2 * m)):
                        s0 = b * 2 * m
                        mm = pe.matmul(ps_a[s0:s0 + m, i * P + s0 + m:i * P + s0 + 2 * m],
                                       M[m][p][:, i * P + s0:i * P + s0 + m],
                                       M[m][p][:, i * P + s0 + m:i * P + s0 + 2 * m], start=True, stop=True)
                if i == TILES - 1:
                    mm.then_inc(coarse, 1)

            def fine_levels(h, p):
                for n, m in enumerate(fine):
                    if m > 1:
                        pe.wait_ge(mult, h * NM + 2 * (LEVELS.index(m) + 1))
                    if m == 1:
                        pe.wait_ge(extra, h * 3 + 2)
                    if m == 0:
                        pe.wait_ge(k_in, h + 1)
                    if n >= 2:
                        pe.wait_ge(fine_out, h * NF + (n - 1))
                    a, b = (M[m][p], M[m][p]) if m else (k[p], q[p])
                    for i in range(TILES):
                        mm = pe.matmul(ps_f[n % 2][:, i * P:(i + 1) * P], a[:, i * P:(i + 1) * P],
                                       b[:, i * P:(i + 1) * P], start=True, stop=True)
                    mm.then_inc(fine_done, 1)
                    if n == 1:
                        pe.wait_ge(mult, h * NM + NM)
                        for i in range(TILES):
                            mm = pe.transpose(ps_t[1][:, i * P:(i + 1) * P], ke[p][:, i * P:(i + 1) * P], c.ident[:, :])
                        mm.then_inc(turned, 1)

            steps(pe, step)


def hgrn_sample(c, HT, d):
    nc = c.nc
    with ExitStack() as ctx:
        sem = lambda n: nc.alloc_semaphore(f"hs_{n}")
        sb = lambda n, s: ctx.enter_context(nc.sbuf_tensor(f"hs_{n}", s, F32))
        S0 = sb("state", [P, HH, NB, P])
        rows = sb("rows", [NB, 2, HH, P])
        vm = sb("v_masked", [NB, 2, NB, P])
        K = sb("keys", [P, HH, NB])
        ps_big = ctx.enter_context(nc.psum_tensor("hs_turned", [P, 2 * HH, P], F32))
        ps_k1 = ctx.enter_context(nc.psum_tensor("hs_outer", [P, NB, P], F32))
        ps_o = ctx.enter_context(nc.psum_tensor("hs_o", [P, HH, NB], F32))
        ps_t = ps_big[0:NB].rearrange("p (a h) n -> p a h n", a=2)
        ps_k = [ps_big[:, 0:NB, :], ps_k1[:, :, :]]
        turned, rows_in, masked, scaled, outer, stepped, mixed, picked, keys = [sem(n) for n in
            ("turned", "rows_in", "v_masked", "scaled", "outer", "stepped", "mixed", "picked", "keys")]
        loaded = [sem(f"head{h}_loaded") for h in range(HH)]
        saved = sem("saved")
        block = ctx.enter_context(nc.Block())

        @block.sync
        def _(sp):
            for h in range(HH):
                sp.dma_start(S0[:, h], d["state_hgrn"][:, h]).then_inc(loaded[h], 16)
            for h in range(HH):
                sp.wait_ge(stepped, h + 1)
                sp.dma_start(d["hgrn_s_out"][:, h], S0[:, h]).then_inc(saved, 16)
            sp.wait_ge(saved, 16 * HH)

        @block.tensor
        def _(pe):
            pe.wait_ge(keys, 1)
            for h in range(HH):
                pe.transpose(ps_t[:, 0, h, :], K[:, h, :], c.ident[:, :])
                mm = pe.transpose(ps_t[:, 1, h, :], HT[:, 16 + h, SEQ:T], c.ident[:, :])
            mm.then_inc(turned, 1)
            pe.wait_ge(rows_in, 1)
            for h in range(HH + 1):
                if h < HH:
                    pe.wait_ge(masked, h + 1)
                    if h >= 2:
                        pe.wait_ge(stepped, h - 1)
                    for j in range(2):
                        mm = pe.matmul(ps_k[h % 2][:, 4 * j:4 * j + 4, :], rows[:, 0, h, :],
                                       vm[:, h % 2, 4 * j:4 * j + 4, :], start=True, stop=True)
                    mm.then_inc(outer, 1)
                if h:
                    pe.wait_ge(stepped, h)
                    for b in range(NB):
                        mm = pe.matmul(ps_o[:, h - 1, b:b + 1], S0[:, h - 1, b, :], HT[:, h - 1, SEQ + b:SEQ + b + 1],
                                       start=True, stop=True)
            mm.then_inc(mixed, 1)

        @block.gpsimd
        def _(pool):
            pool.wait_ge(rows_in, 1)
            for h in range(HH):
                if h >= 2:
                    pool.wait_ge(outer, h - 1)
                pool.tensor_tensor(vm[:, h % 2], rows[:, 1, h, :].unsqueeze(1).broadcast_to([NB, NB, P]),
                                   c.ident[0:NB, 0:NB].unsqueeze(2).broadcast_to([NB, NB, P]), ALU.mult).then_inc(masked, 1)
                pool.wait_ge(masked, h + 1)

        @block.vector
        def _(dve):
            dve.tensor_scalar(K[:, :, :], HT[:, 8:16, SEQ:T], -1.0, 1.0, ALU.mult, ALU.add).then_inc(keys, 1)
            dve.wait_ge(turned, 1)
            dve.tensor_copy(rows[:, :, :, :], ps_t).then_inc(rows_in, 1)
            for h in range(HH + 1):
                if h < HH:
                    dve.wait_ge(loaded[h], 16)
                    dve.tensor_tensor(S0[:, h], S0[:, h], HT[:, 8 + h, SEQ:T].unsqueeze(2).broadcast_to([P, NB, P]),
                                      ALU.mult).then_inc(scaled, 1)
                if h:
                    dve.wait_ge(scaled, h)
                    dve.wait_ge(outer, h)
                    dve.tensor_tensor(S0[:, h - 1], S0[:, h - 1], ps_k[(h - 1) % 2], ALU.add).then_inc(stepped, 1)
            dve.wait_ge(mixed, 1)
            dve.tensor_copy(c.XW[:, :, SEQ:T], ps_o[:, :, :]).then_inc(picked, 1)


def hgrn_norm(c, HT, sq, onw):
    nc = c.nc
    with ExitStack() as ctx:
        sem = lambda n: nc.alloc_semaphore(f"hn_{n}")
        sb = lambda n, s: ctx.enter_context(nc.sbuf_tensor(f"hn_{n}", s, F32))
        pick = sb("pick", [P, HH, HH])
        spread = sb("spread", [HH, HH, P])
        r = sb("inverse_rms", [HH, T])
        ps = ctx.enter_context(nc.psum_tensor("hn_ps", [HH, 2, 512], F32))
        ps_b = [ctx.enter_context(nc.psum_tensor(f"hn_spread{j}", [P, 2, 512], F32)) for j in range(2)]
        squared, summed, mean_in, rooted, own_done, spread_in, gated, normed, consts = [sem(n) for n in
            ("squares", "sums", "means", "roots", "chain", "spread_in", "gated", "normed", "consts")]
        block = ctx.enter_context(nc.Block())

        @block.tensor
        def _(pe):
            pe.wait_ge(consts, 3)
            for h in range(HH):
                pe.wait_ge(squared, h + 1)
                for x in range(2):
                    mm = pe.matmul(ps[:, x, 0:TH], pick[:, h, :], sq[:, h, x * TH:(x + 1) * TH], start=h == 0,
                                   stop=h == HH - 1, skip_group_check=True)
            mm.then_inc(summed, 1)
            pe.wait_ge(rooted, 1)
            for h in range(HH):
                if h >= 2:
                    pe.wait_ge(normed, h - 1)
                for x in range(2):
                    mm = pe.matmul(ps_b[h % 2][:, x, 0:TH], spread[:, h, :], r[:, x * TH:(x + 1) * TH], start=True, stop=True)
                mm.then_inc(spread_in, 1)

        @block.scalar
        def _(act):
            for h in range(HH):
                act.activation(sq[:, h, :], c.XW[:, h, :], ACT.Square).then_inc(squared, 1)
            act.wait_ge(mean_in, 1)
            act.activation(r[:, :], r[:, :], ACT.Sqrt).then_inc(rooted, 1)

        @block.vector
        def _(dve):
            own = Seq(dve, own_done)
            dve.memset(pick[:, :, :], 0.0).then_inc(consts, 1)
            dve.tensor_copy(spread[:, :, :], c.ident[0:HH, 0:HH].unsqueeze(2).broadcast_to([HH, HH, P])).then_inc(consts, 1)
            dve.wait_ge(consts, 2)
            dve.memset(pick[:, :, :].rearrange("p a b -> p (a b)")[:, 0:HH * HH:HH + 1], 1.0).then_inc(consts, 1)
            for h in range(HH):
                dve.wait_ge(squared, h + 1)
                dve.scalar_tensor_tensor(c.XW[:, h, :], c.XW[:, h, :], onw[:, 0:1], HT[:, 24 + h, :], ALU.mult, ALU.mult)\
                   .then_inc(gated, 1)
            dve.wait_ge(summed, 1)
            own.link(dve.tensor_scalar(pairs(r[:, :]), ps[:, :, 0:TH], 1.0 / P, EPS, ALU.mult, ALU.add))
            dve.reciprocal(r[:, :], r[:, :]).then_inc(mean_in, 1)
            for h in range(HH):
                dve.wait_ge(gated, h + 1)
                dve.wait_ge(spread_in, h + 1)
                dve.tensor_tensor(pairs(c.XW[:, h, :]), pairs(c.XW[:, h, :]), ps_b[h % 2][:, :, 0:TH], ALU.mult)\
                   .then_inc(normed, 1)


def program(nc, d):
    with ExitStack() as top:
        c = Core(nc, top)
        c.pages = top.enter_context(nc.sbuf_tensor("pages", [1, NB * PAGES], I32))
        onw = top.enter_context(nc.sbuf_tensor("hgrn_norm_w", [P, 1], F32))
        loaded = top.enter_context(nc.semaphore("setup_loaded"))
        with nc.Block() as block:
            @block.sync
            def _(sp):
                for dst, src in ((c.X[:, :, :], "x"), (c.nw[:, :, :, :], "norm_w"), (c.ident[:, :], "ident"),
                                 (c.pages[:, :], "page_table"), (onw[:, :], "hgrn_norm_w")):
                    sp.dma_start(dst, d[src]).then_inc(loaded, 16)
                for s in range(RING):
                    load_tile(sp, c, d["nsa_w_in"], s, s, KC)
                sp.wait_ge(loaded, 80)

            @block.gpsimd
            def _(pool):
                pool.memset(c.ones[:, :], 1.0)
                for s in range(RING):
                    pool.sem_inc(c.psum_free[s], 1)
        c.loads = [1] * RING

        def swiglu(layer, nxt, post):
            with ExitStack() as ctx:
                Hh, Hl = [ctx.enter_context(nc.sbuf_tensor(f"ffn{layer}_h_{n}", [P, FF, T], F32R)) for n in ("hi", "lo")]
                with ExitStack() as inner:
                    sb = lambda n, s: inner.enter_context(nc.sbuf_tensor(f"ffn{layer}_{n}", s, F32))
                    a_t, g_t = sb("a", [P, 2, T]), sb("g", [P, 2, T])
                    sems = ([nc.alloc_semaphore(f"ffn{layer}_silu{m}") for m in range(2)],
                            nc.alloc_semaphore(f"ffn{layer}_made"),
                            [nc.alloc_semaphore(f"ffn{layer}_used{m}") for m in range(2)])
                    linear(c, f"gu{layer}", d[f"w_gu{layer}"], 2 * FF, 1, KC, c.X,
                           evac_swiglu(c, Hh, Hl, a_t, g_t, sems), (d[f"w_down{layer}"], SUBK), c.nw[:, layer, 2],
                           norm=(post, ssq, a_t, g_t))
                mixed(f"down{layer}", d[f"w_down{layer}"], 2, SUBK, (Hh, Hl), nxt, c.XW, ssq)

        def mixed(name, w, subs, kcs, src, nxt, Y, ssq):
            with nc.sbuf_tensor(f"{name}_sq", [P, T], F32) as sq:
                sems = [nc.alloc_semaphore(f"{name}_{n}") for n in ("squared", "added")]
                linear(c, name, w, KC, subs, kcs, src, evac_squares(c, Y, sq, ssq, sems, RING // subs), nxt)

        with ExitStack() as nsa:
            nsa.enter_context(nc.cleanup_on_exit())
            sb = lambda n, s: nsa.enter_context(nc.sbuf_tensor(n, s, F32))
            HT = sb("HT", [P, NSA_UNITS, T])
            kcT = sb("kcT", [P, NB * PAGES * 4])
            kcBD = sb("kcBD", [P, GP, 2, PBLK])
            vcS = sb("vcS", [P, 4 * P])
            v_rep = sb("v_rep", [P, P])
            with ExitStack() as cm:
                rows = cm.enter_context(nc.sbuf_tensor("cmp_rows", [P, 2 * PAGES_A_CHUNK * 256 + (GP * PBLK + 1) * BLOCK], F32))
                first_in = nc.alloc_semaphore("cmp_first_rows_loaded")

                def first_chunks(sp, step):
                    flat = rows[:, 0:2 * PAGES_A_CHUNK * 256].rearrange("p (g n) -> p g n", n=256)
                    for x in range(4):
                        page = sp.value_load(c.pages[0:1, bass.ds(step * 4 + x, 1)], min_val=0, max_val=POOL - 1)
                        sp.dma_start(flat[:, bass.ds(step * 4 + x, 1), :].rearrange("p o n -> p (o n)"),
                                     d["cache_cmp"][0, bass.ds(page, 1)].rearrange("o p n -> p (o n)"))\
                          .then_inc(first_in, 16)

                linear(c, "nsa_in", d["nsa_w_in"], NSA_UNITS, 1, KC, c.X, evac_scaled(c, HT), (d["nsa_w_out"], KC),
                       c.nw[:, 0, 0], beside=first_chunks,
                       norm=(None, None, None, rows[:, 2 * PAGES_A_CHUNK * 256:2 * PAGES_A_CHUNK * 256 + 2 * T]
                             .rearrange("p (a t) -> p a t", a=2)))
                compress(c, HT, d, rows, first_in, kcT, kcBD, vcS, v_rep)
            Vnew = sb("Vnew", [NB, 4 * P])
            tabs = sb("tabs", [N_BUCKETS + 1, 16 + P])
            c.XW = sb("attention_out", [P, KC, T])
            with ExitStack() as pr:
                sp_ = lambda n, s: pr.enter_context(nc.sbuf_tensor(n, s, F32))
                Otok = sp_("Otok", [P, TILES, D_MODEL])
                Vtok = sp_("Vtok", [P, TILES, 4 * P])
                gT = sp_("gT", [P, TILES, 48])
                T_bias = sp_("T_bias", [P, HEADS, SEQ])
                with ExitStack() as bc:
                    biasC = bc.enter_context(nc.sbuf_tensor("biasC", [P, TILES, HEADS, PBLK], F32))
                    skew_out = nc.alloc_semaphore("bias_skew_out")
                    attention_setup(c, HT, d, tabs, biasC, Vtok, gT, Vnew, skew_out)
                    prompt_compressed(c, HT, d, kcBD, v_rep, T_bias, biasC, gT, Otok, skew_out)
                prompt_attention(c, HT, d, T_bias, Vtok, gT, Otok)
                turn_outputs(c, Otok)
            with ExitStack() as sa:
                ss = lambda n, s: sa.enter_context(nc.sbuf_tensor(n, s, F32))
                Ps = (ss("Pslc", [P, PAST + 1]), ss("Pwin", [P, WIN]), ss("Pcmp", [P, 2, P]))
                bmask, gsum = ss("bmask", [P, NB]), ss("gsum", [P, P])
                with ExitStack() as pp:
                    psS = pp.enter_context(nc.psum_tensor("psS", [P, 4, 512], F32))
                    psW = pp.enter_context(nc.psum_tensor("psW", [P, 512], F32))
                    psM = pp.enter_context(nc.psum_tensor("psM", [P, 512], F32))
                    sample_scores(c, HT, d, tabs, kcT, psS, psW, psM, (bmask, gsum))
                    wv, vb, Vn = ss("win_v", [P, NB, 4, 2 * P]), ss("v_pages", [P, V_SLOTS, V_PG, 2 * P]), ss("v_new", [1, NB, 2 * P])
                    early = (wv, vb, Vn, *[nc.alloc_semaphore(f"sv_{n}") for n in ("win_in", "v_new_in", "win_patched")],
                             *[[nc.alloc_semaphore(f"sv_pages{x}_{n}") for x in range(V_SLOTS)] for n in ("in", "in_by_pool")])
                    sample_softmax(c, d, Ps, psS, psW, psM, (bmask, gsum), Vnew, early)
                sample_values(c, d, Ps, vcS, early)
            with nc.sbuf_tensor("nsa_out_ssq", [P, T], F32) as squares:
                mixed("nsa_out", d["nsa_w_out"], 1, KC, c.XW, (d["w_gu0"], KC), c.XW, squares)
                norm_step(c, "nsa_out_norm", squares, (c.XW, c.nw[:, 0, 1]))
        c.XW = top.enter_context(nc.sbuf_tensor("mixer_out", [P, KC, T], F32))
        ssq = top.enter_context(nc.sbuf_tensor("squares_summed", [P, T], F32))
        with nc.cleanup_on_exit():
            swiglu(0, (d["hgrn_w_in"], KC), None)
        with ExitStack() as hg:
            hg.enter_context(nc.cleanup_on_exit())
            sb = lambda n, s: hg.enter_context(nc.sbuf_tensor(n, s, F32))
            HT = sb("HT2", [P, HGRN_UNITS, T])
            with nc.sbuf_tensor("hgrn_in_y", [P, 2, T], F32) as y, nc.sbuf_tensor("hgrn_in_sq", [P, 2, T], F32) as sq:
                linear(c, "hgrn_in", d["hgrn_w_in"], HGRN_UNITS, 1, KC, c.X, evac_scaled(c, HT), (d["hgrn_w_out"], KC),
                       c.nw[:, 1, 0], norm=((c.XW, c.nw[:, 0, 3]), ssq, y, sq))
            hgrn_gates(c, HT, d)
            hgrn_prompt(c, HT, d)
            hgrn_sample(c, HT, d)
            with nc.sbuf_tensor("hgrn_squares", [P, HH, T], F32) as squares:
                hgrn_norm(c, HT, squares, onw)
            mixed("hgrn_out", d["hgrn_w_out"], 1, KC, c.XW, (d["w_gu1"], KC), c.XW, ssq)
        with nc.cleanup_on_exit():
            swiglu(1, None, (c.XW, c.nw[:, 1, 1]))
            norm_step(c, "last_norm", ssq, (c.XW, c.nw[:, 1, 3]), d["y"])



def bucket(n):
    n = np.asarray(n)
    m = N_BUCKETS // 2
    nf = np.maximum(n, 1).astype(np.float32)
    r = np.log(nf / np.float32(m)).astype(np.float32) / np.float32(np.log(MAX_DISTANCE / m))
    large = m + (r * np.float32(N_BUCKETS - m)).astype(np.int32)
    return np.where(n < 0, -1, np.where(n < m, n, np.minimum(large, N_BUCKETS - 1)))


def onehot(n):
    b = bucket(n)
    b = np.where(b < 0, N_BUCKETS, b)
    return (np.arange(N_BUCKETS + 1)[:, None] == b[None, :]).astype(np.float32)


def unit_tiles(w, subs, kcs):
    N = w.shape[1]
    a = w.reshape(subs, kcs, P, N // P, P)
    return np.ascontiguousarray(a.transpose(3, 0, 2, 1, 4).reshape(N // P * subs, P, kcs * P))


def shape_constants():
    s = np.arange(P)
    out = {
        "ident": np.eye(P, dtype=np.float32),
        "onehot_rows": np.ascontiguousarray(np.stack([onehot(511 - np.arange(1024)), onehot(np.arange(1024) - 511)], 1)),
        "onehot_sample": np.concatenate([onehot(PAST - np.arange(PAST)), onehot(WIN - 1 - np.arange(WIN)),
                                         onehot(PAST - (BLOCK * np.arange(NBLK) + BLOCK - 1)), onehot([0])], 1),
        "head_mask": np.kron(np.eye(16, dtype=np.float32), np.ones((PBLK, 1), np.float32)),
        "batch_mask": np.kron(np.eye(NB, dtype=np.float32), np.ones((HEADS, 1), np.float32)),
        "tile_reset": np.ascontiguousarray(np.broadcast_to((np.arange(SEQ) % P != 0).astype(np.float32), (P, SEQ))),
    }
    h = np.arange(P)
    key = (h // HEADS) * 100 + (h % HEADS // 8) * 10 + h % 2
    out["group_sum"] = (key[:, None] == key[None, :]).astype(np.float32)
    masks = []
    for m in (16, 8, 4, 2, 1):
        masks.append((s[:, None] // (2 * m) == s[None, :] // (2 * m)) & (s[:, None] % (2 * m) < m)
                     & (s[None, :] % (2 * m) >= m))
    masks.append(s[:, None] == s[None, :])
    out["level_masks"] = np.ascontiguousarray(np.stack(masks, 1).astype(np.int32))
    return out


def kernel(x_prompt, x_sample, cache_cmp_kv, cache_slc_kv, state_win_kv, state_hgrn, page_table, norm_w, nsa_w_in,
           nsa_w_out, nsa_cmp_pe, nsa_cmp_w1, nsa_cmp_w2, rel_bias, hgrn_w_in, hgrn_w_out, hgrn_norm_w,
           hgrn_lb_logits, ffn_w_gu, ffn_w_down):
    import concourse.bacc as bacc
    from concourse.bass_utils import run_bass_kernel_spmd

    A = lambda a: np.asarray(a)
    C = np.ascontiguousarray
    a = shape_constants()
    x = np.concatenate([A(x_prompt)[0], A(x_sample)[:, 0]], 0)
    a["x"] = C(x.T.reshape(KC, P, T).transpose(1, 0, 2))
    a["norm_w"] = C(A(norm_w).reshape(2, 4, KC, P).transpose(3, 0, 1, 2))
    a["page_table"] = A(page_table).reshape(1, NB * PAGES)
    a["hgrn_norm_w"] = C(A(hgrn_norm_w)[0].reshape(P, 1))
    w = A(nsa_w_in)[0]
    nq, nkv = HEADS * HD, 6 * KVH * HD
    wq = w[:, :nq].reshape(D_MODEL, GP, 2, REP, HD).transpose(0, 1, 3, 2, 4).reshape(D_MODEL, nq)
    wg = w[:, nq + nkv:].reshape(D_MODEL, 3, GP, 2, REP).transpose(0, 1, 2, 4, 3).reshape(D_MODEL, 48)
    w = np.concatenate([wq, w[:, nq:nq + nkv], wg, np.zeros((D_MODEL, 80), np.float32)], 1)
    a["nsa_w_in"] = unit_tiles(w, 1, KC)
    wo = A(nsa_w_out)[0].reshape(GP, 2, REP, HD, D_MODEL).transpose(0, 2, 1, 3, 4).reshape(nq, D_MODEL)
    a["nsa_w_out"] = unit_tiles(wo, 1, KC)
    a["hgrn_w_in"] = unit_tiles(A(hgrn_w_in)[0], 1, KC)
    a["hgrn_w_out"] = unit_tiles(A(hgrn_w_out)[0], 1, KC)
    for l in range(2):
        gu = A(ffn_w_gu)[l].reshape(D_MODEL, 2, FF, P).transpose(0, 2, 1, 3).reshape(D_MODEL, 2 * D_FF)
        a[f"w_gu{l}"] = unit_tiles(gu, 1, KC)
        a[f"w_down{l}"] = unit_tiles(A(ffn_w_down)[l], 2, SUBK)
    cc = A(cache_cmp_kv)[0].reshape(POOL, P, 2, GP, 2, HD)
    a["cache_cmp"] = C(cc.transpose(2, 0, 4, 5, 3, 1).reshape(2, POOL, P, GP * P))
    cs = A(cache_slc_kv)[0].reshape(POOL, P, 2, GP, 2, HD)
    a["slc_k"] = C(cs[:, :, 0].transpose(0, 3, 4, 2, 1).reshape(POOL, P, GP * P))
    a["slc_v"] = C(cs[:, :, 1].reshape(POOL, P, 2 * P))
    sw = np.roll(A(state_win_kv)[0], -1, axis=1)
    sw = sw.reshape(NB, WIN, 2, GP, 2, HD)
    a["win_k"] = C(sw[:, :, 0].transpose(3, 4, 0, 2, 1).reshape(P, NB, GP, WIN))
    a["win_v"] = C(sw[:, :, 1].reshape(NB, 4, P, 2 * P).transpose(2, 0, 1, 3))
    w1 = A(nsa_cmp_w1)[0].reshape(2, 2, 32, HD, HD)
    bd = np.zeros((2, 2, 2, HD, 32, 2, HD), np.float32)
    w2 = np.zeros((2, HD, 2, 2, HD), np.float32)
    for g in range(2):
        bd[:, :, g, :, :, g, :] = w1.transpose(0, 1, 3, 2, 4)
        w2[g, :, :, g, :] = A(nsa_cmp_w2)[0].transpose(1, 0, 2)
    a["cmp_w1"] = bd.reshape(2, 2, P, 32 * P)
    a["cmp_w2"] = w2.reshape(P, 2, P)
    pe = A(nsa_cmp_pe)[0].transpose(2, 0, 1)
    a["cmp_pe"] = C(np.concatenate([pe, pe], 0))
    tab = np.concatenate([A(rel_bias).reshape(N_BUCKETS, GP, 2, REP).transpose(0, 1, 3, 2).reshape(N_BUCKETS, 16),
                          np.full((1, 16), NEG, np.float32)], 0)
    a["tabs"] = C(np.concatenate([tab] * (NB + 1), 1))
    a["lb_logits"] = C(A(hgrn_lb_logits).reshape(2, HH, P).transpose(2, 0, 1))
    a["state_hgrn"] = C(A(state_hgrn)[0].transpose(2, 1, 0, 3))

    nc = bacc.Bacc("TRN2", target_bir_lowering=False, num_devices=1)
    d = {n: nc.dram_tensor(f"in_{n}", v.shape, mybir.dt.from_np(v.dtype), kind="ExternalInput").ap()
         for n, v in a.items()}
    outs = {"y": (P, KC, T), "kv_out": (P, 12, T), "win_k_out": (P, NB, GP, WIN), "win_v_out": (P, NB, 4, 2 * P),
            "hgrn_p_out": (P, HH, P), "hgrn_s_out": (P, HH, NB, P)}
    for n, s in outs.items():
        d[n] = nc.dram_tensor(f"out_{n}", s, F32, kind="ExternalOutput").ap()
    d["gate_scratch"] = nc.dram_tensor("gate_scratch", (48, NB), F32, kind="Internal").ap()
    d["bias_skew"] = nc.dram_tensor("bias_skew", (P, HEADS, SKEW), F32, kind="Internal").ap()
    d["bias_scratch"] = nc.dram_tensor("bias_scratch", (16, 1024), F32, kind="Internal").ap()
    program(nc, d)
    r = run_bass_kernel_spmd(nc, [{f"in_{n}": v for n, v in a.items()}], core_ids=[0]).results[0]
    o = {n: np.asarray(r[f"out_{n}"]) for n in outs}
    y = o["y"].transpose(2, 1, 0).reshape(T, D_MODEL)
    kv = o["kv_out"].reshape(2, HD, 3, 2, GP, T).transpose(2, 5, 3, 4, 0, 1).reshape(3, T, 2, KVH, HD)
    wk = o["win_k_out"].reshape(2, HD, NB, GP, WIN).transpose(2, 4, 3, 0, 1).reshape(NB, WIN, KVH, HD)
    wv = o["win_v_out"].transpose(1, 2, 0, 3).reshape(NB, WIN, KVH, HD)
    return (C(y[None, :SEQ]), C(y[SEQ:, None]), C(kv[0][None, None, :SEQ]), C(kv[1][None, None, :SEQ]),
            C(kv[2][None, None, :SEQ]), C(o["hgrn_p_out"].transpose(1, 0, 2)[None, None]),
            C(kv[0][None, SEQ:, None]), C(kv[1][None, SEQ:, None]), C(np.stack([wk, wv], 2)[None]),
            C(o["hgrn_s_out"].transpose(2, 1, 0, 3)[None]))
```
